# Optimizing a Trainium2 kernel written in Bass

```python
import math
import jax, jax.numpy as jnp
from jax import lax
import numpy as np

D_MODEL = 1024
BATCH = 1
SEQ = 512
DEPTH = 2

CHUNK = 64
LEFT_CHUNKS = 8
BAND_CHUNKS = LEFT_CHUNKS + 1
BAND_LEN = BAND_CHUNKS * CHUNK
HEAD_DIM = 64
MIX_A_WIDTH = D_MODEL // 2
MIX_B_WIDTH = D_MODEL - MIX_A_WIDTH
A_HEADS = MIX_A_WIDTH // HEAD_DIM
MAX_REL = 2 * CHUNK
SSM_GROUP = 16
SSM_GROUPS = MIX_B_WIDTH // SSM_GROUP
SSM_STATE = 64
DT_MIN = 1e-3
DT_MAX = 1e-1
C_WIDTH = D_MODEL
C_HEADS = C_WIDTH // HEAD_DIM
SB_BLOCK = 128
D_FF = -(-8 * D_MODEL // (3 * 256)) * 256
DEEPNORM_ALPHA = (2 * DEPTH) ** 0.25
DEEPNORM_BETA = (8 * DEPTH) ** -0.25
LN_EPS = 1e-5
N_EVEN = (DEPTH + 1) // 2
N_ODD = DEPTH // 2
EVEN_IN = 3 * MIX_A_WIDTH + MIX_B_WIDTH
ODD_IN = 3 * C_WIDTH

kernel_name = "hybrid_chunkattn_s5_stickbreak_deepnorm"

def layer_norm(x, g, b):
    xf = x.astype(jnp.float32)
    mu = jnp.mean(xf, axis=-1, keepdims=True)
    var = jnp.mean(jnp.square(xf - mu), axis=-1, keepdims=True)
    y = (xf - mu) * lax.rsqrt(var + LN_EPS) * g.astype(jnp.float32) + b.astype(jnp.float32)
    return y.astype(x.dtype)

def chunk_band_attention(q, k, v, rel_table):
    b_, s_, _ = q.shape
    n_chunks = s_ // CHUNK

    def heads(t):
        return t.reshape(b_, n_chunks, CHUNK, A_HEADS, HEAD_DIM).transpose(0, 3, 1, 2, 4)

    band = jnp.arange(n_chunks)[:, None] + jnp.arange(BAND_CHUNKS)[None, :]
    valid = jnp.repeat(band >= LEFT_CHUNKS, CHUNK, axis=1)
    q_pos = LEFT_CHUNKS * CHUNK + jnp.arange(CHUNK)
    k_pos = jnp.arange(BAND_LEN)
    rel = jnp.clip(q_pos[:, None] - k_pos[None, :], -MAX_REL, MAX_REL) + MAX_REL
    bias = rel_table[:, rel].astype(jnp.float32)
    scale = HEAD_DIM ** -0.5
    pad = ((0, 0), (LEFT_CHUNKS, 0), (0, 0), (0, 0))

    def one_sequence(args):
        qh, kh, vh = args
        kb = jnp.pad(kh, pad)[:, band].reshape(A_HEADS, n_chunks, BAND_LEN, HEAD_DIM)
        vb = jnp.pad(vh, pad)[:, band].reshape(A_HEADS, n_chunks, BAND_LEN, HEAD_DIM)
        s = jnp.einsum('hcqd,hckd->hcqk', qh, kb).astype(jnp.float32) * scale + bias[:, None]
        s = jnp.where(valid[None, :, None, :], s, -1e30)
        p = jax.nn.softmax(s, axis=-1)
        return jnp.einsum('hcqk,hckd->hcqd', p.astype(vb.dtype), vb)

    o = lax.map(one_sequence, (heads(q), heads(k), heads(v)))
    return o.transpose(0, 2, 3, 1, 4).reshape(b_, s_, MIX_A_WIDTH)

def _complex_affine_combine(e1, e2):
    a1r, a1i, b1r, b1i = e1
    a2r, a2i, b2r, b2i = e2
    ar = a2r * a1r - a2i * a1i
    ai = a2r * a1i + a2i * a1r
    br = a2r * b1r - a2i * b1i + b2r
    bi = a2r * b1i + a2i * b1r + b2i
    return (ar, ai, br, bi)

def s5_mixer(u, lam_re, lam_im, b_re, b_im, c_re, c_im, d_skip, log_dt, glu_w, glu_b):
    b_, s_, _ = u.shape
    f32 = jnp.float32
    ug = u.reshape(b_, s_, SSM_GROUPS, SSM_GROUP).astype(f32)
    dt = jnp.exp(log_dt.astype(f32))[:, None]
    lr = lam_re.astype(f32)
    li = lam_im.astype(f32)
    mag = jnp.exp(lr * dt)
    ar = mag * jnp.cos(li * dt)
    ai = mag * jnp.sin(li * dt)
    den = lr * lr + li * li
    fr = ((ar - 1.0) * lr + ai * li) / den
    fi = (ai * lr - (ar - 1.0) * li) / den
    br_, bi_ = b_re.astype(f32), b_im.astype(f32)
    bbar_r = fr[..., None] * br_ - fi[..., None] * bi_
    bbar_i = fr[..., None] * bi_ + fi[..., None] * br_
    bu_r = jnp.einsum('bsgi,gpi->sbgp', ug, bbar_r)
    bu_i = jnp.einsum('bsgi,gpi->sbgp', ug, bbar_i)
    a_r = jnp.broadcast_to(ar[None, None], (s_, 1, SSM_GROUPS, SSM_STATE))
    a_i = jnp.broadcast_to(ai[None, None], (s_, 1, SSM_GROUPS, SSM_STATE))
    _, _, x_r, x_i = lax.associative_scan(_complex_affine_combine, (a_r, a_i, bu_r, bu_i), axis=0)
    y = (jnp.einsum('sbgp,gip->bsgi', x_r, c_re.astype(f32))
         - jnp.einsum('sbgp,gip->bsgi', x_i, c_im.astype(f32))
         + d_skip.astype(f32) * ug)
    y = jax.nn.gelu(y).reshape(b_, s_, MIX_B_WIDTH)
    y = y * jax.nn.sigmoid(y @ glu_w.astype(f32) + glu_b.astype(f32))
    return y.astype(u.dtype)

def stick_breaking_attention(q, k, v):
    b_, s_, _ = q.shape

    def heads(t):
        return t.reshape(b_, s_, C_HEADS, HEAD_DIM).transpose(0, 2, 1, 3)

    qh, kh, vh = heads(q), heads(k), heads(v)
    scale = HEAD_DIM ** -0.5
    outs = []
    for blk in range(s_ // SB_BLOCK):
        t0 = blk * SB_BLOCK
        end = t0 + SB_BLOCK
        qb = qh[:, :, t0:end]
        kp = kh[:, :, :end]
        vp = vh[:, :, :end]
        z = jnp.einsum('bhqd,bhkd->bhqk', qb, kp).astype(jnp.float32) * scale
        t_idx = t0 + jnp.arange(SB_BLOCK)
        s_idx = jnp.arange(end)
        strict = s_idx[None, :] < t_idx[:, None]
        log_keep = jnp.where(strict, jax.nn.log_sigmoid(-z), 0.0)
        rev = lax.cumsum(log_keep, axis=3, reverse=True)
        after = jnp.concatenate([rev[..., 1:], jnp.zeros_like(rev[..., :1])], axis=-1)
        w = jnp.where(strict, jnp.exp(jax.nn.log_sigmoid(z) + after), 0.0)
        outs.append(jnp.einsum('bhqk,bhkd->bhqd', w.astype(vp.dtype), vp))
    o = jnp.concatenate(outs, axis=2)
    return o.transpose(0, 2, 1, 3).reshape(b_, s_, C_WIDTH)

def swiglu(x, w1, w3, w2):
    return (jax.nn.silu(x @ w1) * (x @ w3)) @ w2

def setup_inputs(seed: int = 0) -> dict:
    key = jax.random.key(seed)
    ks = jax.random.split(key, 24)
    f32 = jnp.float32
    nrm = lambda k, shape, s: jax.random.normal(k, shape, f32) * s
    x = jax.random.normal(ks[0], (BATCH, SEQ, D_MODEL), f32)
    even_w_in = nrm(ks[1], (N_EVEN, D_MODEL, EVEN_IN), D_MODEL ** -0.5)
    even_rel_bias = nrm(ks[2], (N_EVEN, A_HEADS, 2 * MAX_REL + 1), 0.1)
    n_idx = jnp.arange(SSM_STATE, dtype=f32)
    ssm_lambda_re = -0.5 + nrm(ks[3], (N_EVEN, SSM_GROUPS, SSM_STATE), 0.01)
    ssm_lambda_im = jnp.broadcast_to(math.pi * n_idx, (N_EVEN, SSM_GROUPS, SSM_STATE)).astype(f32)
    b_scale = (2 * SSM_GROUP) ** -0.5
    ssm_b_re = nrm(ks[4], (N_EVEN, SSM_GROUPS, SSM_STATE, SSM_GROUP), b_scale)
    ssm_b_im = nrm(ks[5], (N_EVEN, SSM_GROUPS, SSM_STATE, SSM_GROUP), b_scale)
    c_scale = (2 * SSM_STATE) ** -0.5
    ssm_c_re = nrm(ks[6], (N_EVEN, SSM_GROUPS, SSM_GROUP, SSM_STATE), c_scale)
    ssm_c_im = nrm(ks[7], (N_EVEN, SSM_GROUPS, SSM_GROUP, SSM_STATE), c_scale)
    ssm_d = nrm(ks[8], (N_EVEN, SSM_GROUPS, SSM_GROUP), 1.0)
    ssm_log_dt = jax.random.uniform(ks[9], (N_EVEN, SSM_GROUPS), f32, math.log(DT_MIN), math.log(DT_MAX))
    ssm_glu_w = nrm(ks[10], (N_EVEN, MIX_B_WIDTH, MIX_B_WIDTH), MIX_B_WIDTH ** -0.5)
    ssm_glu_b = nrm(ks[11], (N_EVEN, MIX_B_WIDTH), 0.01)
    even_w_out = nrm(ks[12], (N_EVEN, D_MODEL, D_MODEL), DEEPNORM_BETA * D_MODEL ** -0.5)
    odd_w_in = nrm(ks[13], (N_ODD, D_MODEL, ODD_IN), D_MODEL ** -0.5)
    odd_w_out = nrm(ks[14], (N_ODD, C_WIDTH, D_MODEL), DEEPNORM_BETA * C_WIDTH ** -0.5)
    ffn_w1 = nrm(ks[15], (DEPTH, D_MODEL, D_FF), D_MODEL ** -0.5)
    ffn_w3 = nrm(ks[16], (DEPTH, D_MODEL, D_FF), D_MODEL ** -0.5)
    ffn_w2 = nrm(ks[17], (DEPTH, D_FF, D_MODEL), DEEPNORM_BETA * D_FF ** -0.5)
    ln_mix_g = 1.0 + nrm(ks[18], (DEPTH, D_MODEL), 0.01)
    ln_mix_b = nrm(ks[19], (DEPTH, D_MODEL), 0.01)
    ln_ffn_g = 1.0 + nrm(ks[20], (DEPTH, D_MODEL), 0.01)
    ln_ffn_b = nrm(ks[21], (DEPTH, D_MODEL), 0.01)
    return {"x": x, "even_w_in": even_w_in, "even_rel_bias": even_rel_bias,
            "ssm_lambda_re": ssm_lambda_re, "ssm_lambda_im": ssm_lambda_im,
            "ssm_b_re": ssm_b_re, "ssm_b_im": ssm_b_im, "ssm_c_re": ssm_c_re, "ssm_c_im": ssm_c_im,
            "ssm_d": ssm_d, "ssm_log_dt": ssm_log_dt, "ssm_glu_w": ssm_glu_w, "ssm_glu_b": ssm_glu_b,
            "even_w_out": even_w_out, "odd_w_in": odd_w_in, "odd_w_out": odd_w_out,
            "ffn_w1": ffn_w1, "ffn_w3": ffn_w3, "ffn_w2": ffn_w2,
            "ln_mix_g": ln_mix_g, "ln_mix_b": ln_mix_b, "ln_ffn_g": ln_ffn_g, "ln_ffn_b": ln_ffn_b}

def reference(x, even_w_in, even_rel_bias, ssm_lambda_re, ssm_lambda_im, ssm_b_re, ssm_b_im,
              ssm_c_re, ssm_c_im, ssm_d, ssm_log_dt, ssm_glu_w, ssm_glu_b, even_w_out,
              odd_w_in, odd_w_out, ffn_w1, ffn_w3, ffn_w2, ln_mix_g, ln_mix_b, ln_ffn_g, ln_ffn_b):
    h = x
    for layer in range(DEPTH):
        if layer % 2 == 0:
            e = layer // 2
            proj = h @ even_w_in[e]
            qa, ka, va, ub = jnp.split(proj, [MIX_A_WIDTH, 2 * MIX_A_WIDTH, 3 * MIX_A_WIDTH], axis=-1)
            oa = chunk_band_attention(qa, ka, va, even_rel_bias[e])
            ob = s5_mixer(ub, ssm_lambda_re[e], ssm_lambda_im[e], ssm_b_re[e], ssm_b_im[e],
                          ssm_c_re[e], ssm_c_im[e], ssm_d[e], ssm_log_dt[e], ssm_glu_w[e], ssm_glu_b[e])
            mix = jnp.concatenate([oa, ob], axis=-1) @ even_w_out[e]
        else:
            o = layer // 2
            qc, kc, vc = jnp.split(h @ odd_w_in[o], 3, axis=-1)
            mix = stick_breaking_attention(qc, kc, vc) @ odd_w_out[o]
        h = layer_norm(DEEPNORM_ALPHA * h + mix, ln_mix_g[layer], ln_mix_b[layer])
        ffn = swiglu(h, ffn_w1[layer], ffn_w3[layer], ffn_w2[layer])
        h = layer_norm(DEEPNORM_ALPHA * h + ffn, ln_ffn_g[layer], ln_ffn_b[layer])
    return h


_drawn_inputs = setup_inputs


def setup_inputs(seed=0):
    import zlib

    import numpy as np

    out = dict(_drawn_inputs(seed))
    spreads = {}
    factors = {'even_rel_bias': 8.0,
     'ssm_lambda_re': 64.0,
     'ssm_lambda_im': 64.0,
     'ssm_b_re': 64.0,
     'ssm_b_im': 64.0,
     'ssm_c_re': 64.0,
     'ssm_c_im': 64.0,
     'ssm_log_dt': 64.0,
     'ssm_glu_b': 64.0,
     'ln_mix_g': 3.944,
     'ln_mix_b': 3.942,
     'ln_ffn_g': 11.864,
     'ln_ffn_b': 11.313}
    for name, (base, spread) in spreads.items():
        noise = np.random.default_rng([zlib.crc32(name.encode()), seed]).standard_normal(out[name].shape)
        drawn = base * np.exp(spread * noise) if base else spread * noise
        out[name] = __import__('jax').numpy.asarray(drawn.astype(out[name].dtype))
    for name, factor in factors.items():
        out[name] = (out[name] * factor).astype(out[name].dtype)
    return out
```

```python
import math
from contextlib import ExitStack

import numpy as np
import concourse.bass as bass
from concourse import mybir

P = 128
D = 1024
S = 512
KT = D // P
NT = S // P
DFF = 2816
FT = DFF // P
WA = 512
AT = WA // P
HD = 64
A_HEADS = WA // HD
C_HEADS = D // HD
CHUNK = 64
MAX_REL = 2 * CHUNK
NREL = 2 * MAX_REL + 1
G, GI, PS = 32, 16, 64
PAIRS = G // 2
GQ = G // AT
PQ = PAIRS // AT
L = P // GI
NC = S // L
ALPHA = 4.0 ** 0.25
EPS = 1e-5
QSCALE = HD ** -0.5
MASKED = -1e30

WB = 1024
RAW = 3
WS = 5
TAIL = 4

ALU = mybir.AluOpType
ACT = mybir.ActivationFunctionType
F32 = mybir.dt.float32
F32R = mybir.dt.float32r
AX = mybir.AxisListType

TWO_PI_1 = 6.28125
TWO_PI_2 = math.floor((2 * math.pi - TWO_PI_1) * 2 ** 20) / 2 ** 20
TWO_PI_3 = float(np.float32(2 * math.pi - TWO_PI_1 - TWO_PI_2))
ROUNDER = 1.5 * 2.0 ** 23
PI_BELOW = 3.1415925

TRI = {0: 0, 1: 512, 3: 896, 2: 1024}
TRI_W = 1280


def build(nc, x, even_w_in, rel, lam_re, lam_im, b_re, b_im, c_re, c_im, d_skip, log_dt, glu_w, glu_b,
          even_w_out, odd_w_in, odd_w_out, w1, w3, w2, ln_mix_g, ln_mix_b, ln_ffn_g, ln_ffn_b, out):
    blocks = []

    def feature_tile(w, c0):
        blocks.append(w[:, c0:c0 + P].rearrange("(k p) n -> p k n", p=P))

    def row_tiles(w, r0, c0, cols):
        n = WB // cols
        blocks.append(w[r0:r0 + n * P, c0:c0 + cols].rearrange("(k p) n -> p k n", p=P))

    ewi, ewo = even_w_in[0], even_w_out[0]
    owi, owo = odd_w_in[0], odd_w_out[0]
    for m in range(AT):
        feature_tile(ewi, 3 * WA + m * P)
    for b in range(4):
        row_tiles(ewi, b * 2 * P, 2 * WA, WA)
    for m in range(AT):
        feature_tile(ewi, m * P)
        feature_tile(ewi, WA + m * P)
    GLU = len(blocks)
    for b in range(2):
        blocks.append(glu_w[0][:, b * 256:(b + 1) * 256].rearrange("(k p) n -> p k n", p=P))
    EOUT = len(blocks)
    for k in range(KT):
        row_tiles(ewo, k * P, 0, D)
    FFN = [len(blocks), 0]

    def ffn_blocks(layer):
        FFN[layer] = len(blocks)
        for m in range(FT):
            feature_tile(w1[layer], m * P)
            feature_tile(w3[layer], m * P)
        for k in range(FT):
            row_tiles(w2[layer], k * P, 0, D)

    ffn_blocks(0)
    OV = len(blocks)
    for k in range(KT):
        row_tiles(owi, k * P, 2 * D, D)
    OQK = len(blocks)
    for m in range(KT):
        feature_tile(owi, m * P)
        feature_tile(owi, D + m * P)
    OOUT = len(blocks)
    for k in range(KT):
        row_tiles(owo, k * P, 0, D)
    ffn_blocks(1)
    NBLK = len(blocks)

    ctx = ExitStack()
    with ctx:
        base = 16512
        fence = ctx.enter_context(nc.sbuf_tensor("fence", [P, (229344 - base) // 4], F32))
        at = [base]

        def put(name, shape, dt=F32, off=None):
            o = at[0] if off is None else off
            t = nc.alloc_sbuf_tensor_at(name, shape, dt, offset=o)
            size = (4 * int(np.prod(shape[1:])) + 31) // 32 * 32
            if off is None:
                at[0] += size
            return t, o + size

        def fixed(name, shape, dt=F32):
            return put(name, shape, dt)[0]

        raw = fixed("raw", [P, RAW, WB])
        whi = fixed("whi", [P, WS, WB], F32R)
        wlo = fixed("wlo", [P, WS, WB], F32R)
        xhi = fixed("xhi", [P, KT, S], F32R)
        xlo = fixed("xlo", [P, KT, S], F32R)
        arena = at[0]
        h = fixed("h", [P, NT, D])
        g_region = at[0]
        ghi = fixed("ghi", [P, FT, S], F32R)
        glo = fixed("glo", [P, FT, S], F32R)
        lnp = fixed("lnp", [P, 2, D])
        arena_end = at[0]
        ident = fixed("ident", [P, P])
        tri = fixed("tri", [P, P], F32R)
        ones = fixed("ones", [P, P], F32R)
        sg = fixed("sg", [P, 2, S])
        gt = fixed("gt", [P, 2, S])
        stats = fixed("stats", [P, NT, 2, 6])
        mv = fixed("mv", [P, NT, 2])
        lns = fixed("lns", [P, NT, 4])
        glub = fixed("glub", [P, AT])
        sm = fixed("sm", [P, 2, 4])
        assert at[0] <= 229344

        e = [arena]

        def even(name, shape, dt=F32):
            t, e[0] = put(name, shape, dt, e[0])
            assert e[0] <= arena_end, (name, e[0] - arena_end)
            return t

        pt = even("pt", [P, NT, S])
        sc = even("sc", [P, 2, S])
        bias = even("bias", [P, 2, S])
        assert e[0] == g_region
        qT = even("qT", [P, AT, S])
        kT = even("kT", [P, AT, S])
        v = even("v", [P, NT, WA])
        yT = even("yT", [P, AT, L, NC])
        phr = even("phr", [P, PAIRS, NC])
        phi = even("phi", [P, PAIRS, NC])
        u8 = even("u8", [P, AT, GQ, NC])
        uP = even("uP", [P, L, NC])
        y8 = even("y8", [P, GQ, NC])
        winr = even("winr", [P, PQ, P])
        wini = even("wini", [P, PQ, P])
        cxr = even("cxr", [P, PQ, L + 1, GI])
        cxi = even("cxi", [P, PQ, L + 1, GI])
        toep = even("toep", [P, GQ, P])
        wnr = even("wnr", [P, PQ, L, GI])
        wni = even("wni", [P, PQ, L, GI])
        gk = even("gk", [P, GQ, L, GI])
        zin_r = even("zin_r", [P, PQ, NC])
        zin_i = even("zin_i", [P, PQ, NC])
        zr = even("zr", [P, PQ, NC])
        zi = even("zi", [P, PQ, NC])
        xsr = even("xsr", [P, PQ, NC + 1])
        xsi = even("xsi", [P, PQ, NC + 1])
        decay = even("decay", [P, PQ, NC])
        bbr = even("bbr", [P, PAIRS, GI])
        bbi = even("bbi", [P, PAIRS, GI])
        bnr = even("bnr", [P, PAIRS, GI])
        bni = even("bni", [P, PAIRS, GI])
        cr = even("cr", [P, PAIRS, GI])
        nci = even("nci", [P, PAIRS, GI])
        pw = even("pw", [P, 3, PAIRS, L + 1])
        par = even("par", [P, 7, PAIRS])
        ph = even("ph", [P, 2, 2, PAIRS])
        dd = even("dd", [GI, G, GI])
        t4 = [sg[:, 0, :], sg[:, 1, :], gt[:, 0, :], gt[:, 1, :]]
        pl, o = put("pl", [PAIRS, 24, P], F32, g_region)
        reltab, o = put("reltab", [A_HEADS, NREL], F32, o)
        relext, o = put("relext", [A_HEADS, 5 * P], F32, o)
        dt2, o = put("dt2", [PAIRS, 2], F32, o)
        assert o <= g_region + 2 * 4 * AT * S
        cdr, o = put("cdr", [P, AT, 2, PS], F32, g_region + 2 * 4 * AT * S)
        cdi, o = put("cdi", [P, AT, 2, PS], F32, o)
        yhi, o = put("yhi", [P, AT, S], F32R, g_region)
        ylo, o = put("ylo", [P, AT, S], F32R, o)

        oq, o = put("oq", [P, KT, S], F32, g_region)
        ok, o = put("ok", [P, KT, S], F32, o)
        ov, o = put("ov", [P, NT, D], F32, o)
        lg, o = put("lg", [P, TRI_W], F32, o)
        sp, o = put("sp", [P, TRI_W], F32, o)
        sphi, o = put("sphi", [P, TRI_W], F32R, o)
        splo, o = put("splo", [P, TRI_W], F32R, o)
        wt, o = put("wt", [P, 3, TRI_W], F32, o)
        assert o <= g_region + 2 * 4 * FT * S, o - g_region

        ps = ctx.enter_context(nc.psum_tensor("ps", [P, 8, S], F32))
        psf = ps[:].rearrange("p b n -> p (b n)")

        u_dram = nc.dram_tensor("u_scratch", (AT, P, S), F32, kind="Internal").ap()
        y_dram = nc.dram_tensor("y_scratch", (AT, P, S), F32, kind="Internal").ap()
        rel_dram = nc.dram_tensor("rel_scratch", (A_HEADS, 5 * P), F32, kind="Internal").ap()

        def sem(name):
            return ctx.enter_context(nc.semaphore(name))

        w_landed = [sem(f"w_landed{i}") for i in range(RAW)]
        w_hi, w_lo, w_used = sem("w_hi"), sem("w_lo"), sem("w_used")
        x_landed = [sem(f"x_landed{i}") for i in range(NT)]
        lam_landed, b_landed, c_landed, rel_landed, glub_landed, d_landed = (
            sem(n) for n in ("lam_landed", "b_landed", "c_landed", "rel_landed", "glub_landed", "d_landed"))
        const_ready, const_zero = sem("const_ready"), sem("const_zero")
        turned, x_hi, x_ready = sem("turned"), sem("x_hi"), sem("x_ready")
        proj_out, v_out = sem("proj_out"), sem("v_out")
        dt_ready, m_ready, mag_ready, arg_ready, trig_ready = (
            sem(n) for n in ("dt_ready", "m_ready", "mag_ready", "arg_ready", "trig_ready"))
        pl_ready, pl_turned, par_read, c_turned, par_out = (
            sem(n) for n in ("pl_ready", "pl_turned", "par_read", "c_turned", "par_out"))
        u_stored, y_stored = sem("u_stored"), sem("y_stored")
        u_landed = [sem(f"u_landed{i}") for i in range(AT)]
        y_landed, toep_landed = sem("y_landed"), sem("toep_landed")
        wn_ready, cx_ready, gk_ready, xs_ready = (
            sem(n) for n in ("wn_ready", "cx_ready", "gk_ready", "xs_ready"))
        ssm_done, ssm_out = sem("ssm_done"), sem("ssm_out")
        relext_ready, rel_stored = sem("relext_ready"), sem("rel_stored")
        bias_landed = [sem(f"bias_landed{i}") for i in range(2)]
        s_done, s_biased, s_negmax, s_exp, p_ready, pt_done, pt_out, pv_done, ao_hi, ao_out = (
            sem(n) for n in ("s_done", "s_biased", "s_negmax", "s_exp", "p_ready", "pt_done", "pt_out",
                             "pv_done", "ao_hi", "ao_out"))
        y_gelu, y_hi, y_ready, glu_done, glu_sig, ob_ready, ob_hi, mix_b = (
            sem(n) for n in ("y_gelu", "y_hi", "y_ready", "glu_done", "glu_sig", "ob_ready", "ob_hi", "mix_b"))
        acc_done, var_ready, std_ready, scale_ready, normed, h_ready, lnp_landed, h_landed = (
            sem(n) for n in ("acc_done", "var_ready", "std_ready", "scale_ready", "normed", "h_ready",
                             "lnp_landed", "h_landed"))
        silu_ready, g_ready, g_hi, g_lo = (sem(n) for n in ("silu_ready", "g_ready", "g_hi", "g_lo"))
        ov_out, oqk_out = sem("ov_out"), sem("oqk_out")
        z_done, l_ready, z_read, sp_raw, sp_masked, sp_hi, sp_lo, r_done, lw_ready, w_exp, w_ready, opv_done, o_out = (
            sem(n) for n in ("z_done", "l_ready", "z_read", "sp_raw", "sp_masked", "sp_hi", "sp_lo", "r_done", "lw_ready",
                             "w_exp", "w_ready", "opv_done", "o_out"))
        omix_hi, omix = sem("omix_hi"), sem("omix")
        dve_self, act_self = sem("dve_self"), sem("act_self")
        out_stored = sem("out_stored")

        N_QK = 2 * AT
        STEPS = 7
        SSM_STEPS = [(q, s) for q in range(AT) for s in range(STEPS)]
        AFTER_QK = 2

        def ssm_behind_qk(n):
            return SSM_STEPS[n * AFTER_QK:(n + 1) * AFTER_QK]

        def ssm_behind_head(hd):
            a = N_QK * AFTER_QK
            return SSM_STEPS[a + (3 * hd + 1) // 2:a + (3 * hd + 4) // 2]

        block = ctx.enter_context(nc.Block())

        @block.sync
        def _(sp_):
            eng = nc.sync
            issued = [0]

            def weights_upto(n):
                while issued[0] < min(n, NBLK):
                    b = issued[0]
                    if b >= RAW:
                        sp_.wait_ge(w_lo, b - RAW + 1)
                    src = blocks[b]
                    dst = raw[:, b % RAW, :].rearrange("p (k n) -> p k n", k=src.shape[1])
                    eng.dma_start(dst, src).then_inc(w_landed[b % RAW], 16)
                    issued[0] += 1

            xt = x[0].rearrange("(t p) d -> t p d", p=P)
            eng.dma_start(h[:, 0, :], xt[0]).then_inc(x_landed[0], 16)
            weights_upto(1)
            for t in range(1, NT):
                eng.dma_start(h[:, t, :], xt[t]).then_inc(x_landed[t], 16)
            eng.dma_start(pl[:, 7, :], lam_re[0].rearrange("(a b) p -> a (b p)", b=2)).then_inc(lam_landed, 16)
            eng.dma_start(pl[:, 8, :], lam_im[0].rearrange("(a b) p -> a (b p)", b=2)).then_inc(lam_landed, 16)
            eng.dma_start(dt2[:], log_dt[0].rearrange("(a b) -> a b", b=2)).then_inc(lam_landed, 16)
            weights_upto(2)
            eng.dma_start(bnr[:], b_re[0].rearrange("(a b) p i -> (b p) a i", b=2)).then_inc(b_landed, 16)
            eng.dma_start(bni[:], b_im[0].rearrange("(a b) p i -> (b p) a i", b=2)).then_inc(b_landed, 16)
            for dst, src in ((cdr, c_re), (cdi, c_im)):
                for dup in range(2):
                    eng.dma_start(dst[:, :, dup, :], src[0].rearrange("(t g) j p -> (g j) t p", g=GQ)).then_inc(
                        c_landed, 16)
            eng.dma_start(reltab[:], rel[0]).then_inc(rel_landed, 16)
            eng.dma_start(dd[:].rearrange("i g j -> i (g j)"),
                          d_skip[0].rearrange("g j -> (g j)").partition_broadcast(GI)).then_inc(d_landed, 16)
            eng.dma_start(glub[:], glu_b[0].rearrange("(t p) -> p t", p=P), allow_slow_non_contiguous=True).then_inc(glub_landed, 16)
            weights_upto(5)
            sp_.wait_ge(relext_ready, 2)
            eng.dma_start(rel_dram, relext[:]).then_inc(rel_stored, 16)

            for q in range(AT):
                weights_upto(q + 5)
                sp_.wait_ge(proj_out, q + 1)
                eng.dma_start(u_dram[q], uP[:].rearrange("p s c -> p (s c)")).then_inc(u_stored, 16)
                sp_.wait_ge(u_stored, 16 * (q + 1))
                src = u_dram[q].rearrange("(g i) (s c) -> s i g c", g=GQ, s=L)
                for s in range(L):
                    r = L - 1 - s
                    eng.dma_start(u8[GI * r:GI * (r + 1), q], src[s]).then_inc(u_landed[q], 16)

            def load_bias(hd):
                if hd >= 2:
                    sp_.wait_ge(s_biased, NT * (hd - 1))
                src = bass.AP(rel_dram.tensor, hd * 5 * P, [[1, P], [1, S]])
                eng.dma_start(bias[:, hd % 2, :], src).then_inc(bias_landed[hd % 2], 16)

            def ssm_moves(steps):
                for q, s in steps:
                    if s == 3:
                        sp_.wait_ge(gk_ready, q + 1)
                        if q:
                            sp_.wait_ge(ssm_done, STEPS * q)
                        else:
                            sp_.wait_ge(const_ready, 6)
                        for r in range(L):
                            eng.dma_start(toep[GI * r:GI * (r + 1), :, GI * (L - 1 - r):],
                                          gk[0:GI, :, 0:r + 1, :].rearrange("i g t j -> i g (t j)")).then_inc(
                                              toep_landed, 16)
                    if s == 6:
                        sp_.wait_ge(ssm_out, STEPS * (q + 1))
                        eng.dma_start(y_dram[q], y8[:].rearrange("p g c -> p (g c)")).then_inc(y_stored, 16)
                        sp_.wait_ge(y_stored, 16 * (q + 1))
                        src = y_dram[q].rearrange("(t j) (g c) -> g j t c", t=L, g=GQ)
                        for g in range(GQ):
                            eng.dma_start(yT[GI * g:GI * (g + 1), q], src[g]).then_inc(y_landed, 16)

            sp_.wait_ge(rel_stored, 16)
            sp_.wait_ge(x_ready, NT)
            load_bias(0)
            load_bias(1)
            for n in range(N_QK):
                weights_upto(8 + n + 6)
                ssm_moves(ssm_behind_qk(n))
            weights_upto(GLU + WS + RAW)
            for hd in range(A_HEADS):
                if hd + 2 < A_HEADS:
                    load_bias(hd + 2)
                ssm_moves(ssm_behind_head(hd))

            def load_norm(n):
                for i, p in enumerate([(ln_mix_g, ln_mix_b), (ln_ffn_g, ln_ffn_b)][n % 2]):
                    eng.dma_start(lnp[:, i, :], p[n // 2].partition_broadcast(P)).then_inc(lnp_landed, 16)

            sp_.wait_ge(pv_done, A_HEADS)
            sp_.wait_ge(s_biased, A_HEADS * NT)
            for t in range(NT):
                eng.dma_start(h[:, t, :], xt[t]).then_inc(h_landed, 16)
            sp_.wait_ge(ssm_done, STEPS * AT)
            sp_.wait_ge(xs_ready, AT)
            load_norm(0)
            weights_upto(FFN[0] + 3)
            for n, upto in ((1, OV + 3), (2, FFN[1] + 3), (3, NBLK)):
                sp_.wait_ge(h_ready, NT * n)
                load_norm(n)
                weights_upto(upto)
            ot = out[0].rearrange("(t p) d -> t p d", p=P)
            for t in range(NT):
                sp_.wait_ge(h_ready, 3 * NT + t + 1)
                eng.dma_start(ot[t], h[:, t, :]).then_inc(out_stored, 16)
            sp_.wait_ge(out_stored, 16 * NT)

        @block.gpsimd
        def _(pool):
            eng = nc.gpsimd
            eng.memset(ident[:], 0.0).then_inc(const_zero, 1)
            eng.memset(ones[:].bitcast(F32), 1.0).then_inc(const_ready, 1)
            eng.memset(toep[:], 0.0).then_inc(const_ready, 1)
            eng.memset(xsr[:, :, 0:1], 0.0).then_inc(const_ready, 1)
            eng.memset(xsi[:, :, 0:1], 0.0).then_inc(const_ready, 1)
            pool.wait_ge(const_zero, 1)
            eng.affine_select(out=ident[:], in_=ident[:], compare_op=ALU.not_equal, fill=1.0, base=0,
                              pattern=[[-1, P]], channel_multiplier=1).then_inc(const_ready, 1)
            pool.wait_ge(const_ready, 5)
            eng.affine_select(out=tri[:], in_=ones[:].bitcast(F32), compare_op=ALU.is_gt, fill=0.0, base=0,
                              pattern=[[-1, P]], channel_multiplier=1).then_inc(const_ready, 1)
            split = [0]

            def lower_upto(n):
                while split[0] < min(n, NBLK):
                    b = split[0]
                    pool.wait_ge(w_hi, b + 1)
                    eng.tensor_tensor(wlo[:, b % WS, :], raw[:, b % RAW, :], whi[:, b % WS, :].bitcast(F32),
                                      ALU.subtract).then_inc(w_lo, 1)
                    split[0] += 1

            def mask(t, signal):
                for j in range(NT):
                    o = TRI[j]
                    eng.affine_select(out=t[:, o:o + P], in_=t[:, o:o + P], compare_op=ALU.is_gt, fill=0.0,
                                      base=0, pattern=[[1, P]], channel_multiplier=-1).then_inc(signal, 1)

            lower_upto(OQK + WS)
            for hd in range(C_HEADS + 1):
                lower_upto(OQK + min(hd, C_HEADS - 1) + WS)
                if hd < C_HEADS:
                    pool.wait_ge(sp_raw, hd + 1)
                    mask(sp, sp_masked)
                if hd:
                    pool.wait_ge(w_exp, hd)
                    mask(wt[:, (hd - 1) % 3], w_ready)
            lower_upto(NBLK)

        @block.scalar
        def _(act):
            eng = nc.scalar
            rounded = [0]
            own = [0]

            def upper_upto(n):
                while rounded[0] <= min(n, NBLK - 1):
                    b = rounded[0]
                    act.wait_ge(w_landed[b % RAW], 16 * (b // RAW + 1))
                    if b >= WS:
                        act.wait_ge(w_used, b - WS + 1)
                    eng.copy(whi[:, b % WS, :], raw[:, b % RAW, :]).then_inc(w_hi, 1)
                    rounded[0] += 1

            def link(ins):
                own[0] += 1
                ins.then_inc(act_self, 1)
                act.wait_ge(act_self, own[0])

            def upper_x(n, t):
                act.wait_ge(turned, NT * n + t + 1)
                eng.copy(xhi[:, :, t * P:(t + 1) * P],
                         psf[:, 2 * t * S:2 * (t + 1) * S].rearrange("p (k n) -> p k n", k=KT)).then_inc(x_hi, 1)

            act.wait_ge(lam_landed, 48)
            eng.activation(dt2[:], dt2[:], ACT.Exp).then_inc(dt_ready, 1)
            for t in range(NT):
                upper_x(0, t)
            upper_upto(1)
            act.wait_ge(m_ready, 1)
            eng.activation(pl[:, 10, :], pl[:, 9, :], ACT.Exp).then_inc(mag_ready, 1)
            upper_upto(3)
            act.wait_ge(arg_ready, 1)
            eng.activation(pl[:, 6, :], pl[:, 12, :], ACT.Sin).then_inc(trig_ready, 1)
            eng.activation(pl[:, 5, :], pl[:, 13, :], ACT.Sin).then_inc(trig_ready, 1)

            def project_out(n, dst, scale=None):
                act.wait_ge(w_used, (n if n < AT else n + 4) + 1)
                src = ps[:, 4 + n % 2, :]
                if dst is None:
                    q = n
                    if q:
                        act.wait_ge(u_stored, 16 * q)
                    ins = eng.copy(uP[:].rearrange("p s c -> p c s"), src.rearrange("p (c s) -> p c s", s=L))
                elif scale:
                    ins = eng.mul(dst, src.rearrange("p (t n) -> p t n", n=P), scale)
                else:
                    ins = eng.copy(dst, src)
                ins.then_inc(proj_out, 1)

            for q in range(AT):
                upper_upto(q + 4)
                project_out(q, None)
            upper_upto(8)
            act.wait_ge(c_turned, 1)
            for b in range(4):
                upper_upto(8 + b)
            act.wait_ge(w_used, 2 * AT)
            for t in range(NT):
                eng.copy(v[:, t, :], ps[:, t, :]).then_inc(v_out, 1)

            def ssm_outs(steps):
                for q, s in steps:
                    if s in (0, 1):
                        act.wait_ge(ssm_done, STEPS * q + s + 1)
                        eng.copy((winr, wini)[s][:].rearrange("p a n -> p (a n)"), ps[:, 7, :]).then_inc(ssm_out, 1)
                    if s in (5, 6):
                        act.wait_ge(ssm_done, STEPS * q + s + 1)
                        if q:
                            act.wait_ge(y_stored, 16 * q)
                        eng.copy(y8[:].rearrange("p (a b) c -> p a b c", b=2)[:, :, s - 5, :],
                                 ps[:, 7, 0:PQ * NC].rearrange("p (a c) -> p a c", c=NC)).then_inc(ssm_out, 1)

            act.wait_ge(pl_turned, 1)
            act.wait_ge(rel_stored, 16)
            act.wait_ge(par_out, 1)
            for n in range(N_QK):
                upper_upto(8 + n + 4)
                if n % 2 == 0:
                    project_out(AT + n, qT[:, n // 2, :].rearrange("p (t n) -> p t n", n=P)[:, :, ::-1], QSCALE)
                else:
                    project_out(AT + n, kT[:, n // 2, :])
                ssm_outs(ssm_behind_qk(n))
            upper_upto(GLU + WS - 1)

            it = [(hd, i) for hd in range(A_HEADS) for i in range(NT)]

            def softmax_exp(n):
                w = (it[n][1] + 1) * P
                act.wait_ge(s_negmax, n + 1)
                eng.activation(sc[:, n % 2, 0:w], sc[:, n % 2, 0:w], ACT.Exp, bias=sm[:, n % 2, 1:2],
                               accum_out=sm[:, n % 2, 2:3]).then_inc(s_exp, 1)

            def turned_out(n):
                hd, i = it[n]
                act.wait_ge(pt_done, n + 1)
                if hd and i == 0:
                    act.wait_ge(pv_done, hd)
                eng.copy(pt[:, 0:i + 1, i * P:(i + 1) * P],
                         ps[:, 2 + n % 2, 0:(i + 1) * P].rearrange("p (j n) -> p j n", n=P)[:, :, ::-1]).then_inc(
                             pt_out, 1)

            def pair_upper(j):
                act.wait_ge(pv_done, 2 * j + 2)
                eng.copy(xhi[:, j, :], ps[:, 6, :]).then_inc(ao_hi, 1)

            for n in range(len(it) + 1):
                if n < len(it):
                    softmax_exp(n)
                if n:
                    turned_out(n - 1)
                    hd, i = it[n - 1]
                    if i == NT - 1:
                        ssm_outs(ssm_behind_head(hd))
                        if hd % 2:
                            pair_upper(hd // 2)

            act.wait_ge(y_landed, 16 * GQ * AT)
            for q in range(AT):
                eng.activation(yT[:, q], yT[:, q], ACT.Gelu_apprx_tanh).then_inc(y_gelu, 1)
            for q in range(AT):
                act.wait_ge(y_gelu, q + 1)
                if q == 0:
                    act.wait_ge(pv_done, A_HEADS)
                eng.copy(yhi[:, q, :], yT[:, q].rearrange("p t c -> p (t c)")).then_inc(y_hi, 1)
            act.wait_ge(glub_landed, 16)
            for m in range(AT):
                if m % 2:
                    act.wait_ge(w_used, GLU + m // 2 + 1)
                else:
                    act.wait_ge(glu_done, m // 2 + 1)
                if m >= 2:
                    act.wait_ge(ob_ready, m - 1)
                eng.activation(sg[:, m % 2, :], ps[:, 4 + m % 2, :], ACT.Sigmoid,
                               bias=glub[:, m:m + 1]).then_inc(glu_sig, 1)
                act.wait_ge(ob_ready, m + 1)
                eng.copy(xhi[:, AT + m, :].rearrange("p (c t) -> p c t", t=L),
                         gt[:, m % 2, :].rearrange("p (t c) -> p c t", t=L)).then_inc(ob_hi, 1)

            def norm(n, first):
                for t in range(NT + 1):
                    if t < NT:
                        act.wait_ge(var_ready, NT * n + t + 1)
                        eng.activation(lns[:, t, 1:2], lns[:, t, 0:1], ACT.Sqrt).then_inc(std_ready, 1)
                        act.wait_ge(scale_ready, NT * n + t + 1)
                        eng.activation(h[:, t, :], h[:, t, :], ACT.Identity, bias=lns[:, t, 3:4],
                                       scale=lns[:, t, 2:3]).then_inc(normed, 1)
                    if t and n < 3:
                        upper_x(n + 1, t - 1)

            def product(first, nk):
                for k in range(nk):
                    upper_upto(first + k)

            def ffn(layer):
                f = FFN[layer]
                for m in range(FT):
                    upper_upto(f + 2 * m + 4)
                    c = layer * FT + m
                    act.wait_ge(w_used, f + 2 * m + 1)
                    if m >= 2:
                        act.wait_ge(g_ready, c - 1)
                    eng.activation(sg[:, m % 2, :], ps[:, 2 * (m % 2), :], ACT.Silu).then_inc(silu_ready, 1)
                    upper_upto(f + 2 * m + 5)
                    act.wait_ge(g_ready, c + 1)
                    eng.copy(ghi[:, m, :], gt[:, m % 2, :]).then_inc(g_hi, 1)
                product(f + 2 * FT, FT)

            product(EOUT, KT)
            upper_upto(FFN[0])
            norm(0, FFN[0])
            ffn(0)
            upper_upto(OV)
            norm(1, OV)
            product(OV, KT)
            upper_upto(OQK + 3)
            act.wait_ge(w_used, OV + KT)
            for t in range(NT):
                eng.copy(ov[:, t, :], psf[:, 2 * t * S:2 * (t + 1) * S]).then_inc(ov_out, 1)

            def stick_logs(hd):
                act.wait_ge(z_done, hd + 1)
                if hd:
                    act.wait_ge(z_read, hd)
                link(eng.activation(lg[:], psf[:, 0:TRI_W], ACT.Abs))
                link(eng.activation(lg[:], lg[:], ACT.Exp, scale=-1.0))
                eng.activation(lg[:], lg[:], ACT.Ln, bias=1.0).then_inc(l_ready, 1)

            def stick_upper(hd):
                act.wait_ge(sp_masked, NT * (hd + 1))
                if hd:
                    act.wait_ge(r_done, hd)
                eng.copy(sphi[:], sp[:]).then_inc(sp_hi, 1)

            def stick_exp(hd):
                act.wait_ge(lw_ready, hd + 1)
                eng.activation(wt[:, hd % 3], wt[:, hd % 3], ACT.Exp).then_inc(w_exp, 1)

            def oqk_outs(n):
                upper_upto(OQK + n + 4)
                act.wait_ge(w_used, OQK + n + 1)
                if n % 2 == 0:
                    eng.mul(oq[:, n // 2, :], ps[:, 6, :], QSCALE).then_inc(oqk_out, 1)
                else:
                    eng.copy(ok[:, n // 2, :], ps[:, 6, :]).then_inc(oqk_out, 1)

            def pair_out(j):
                act.wait_ge(opv_done, 2 * j + 2)
                eng.copy(oq[:, j, :], ps[:, 7, :]).then_inc(o_out, 1)

            def mix_upper(j):
                act.wait_ge(o_out, j + 1)
                eng.copy(xhi[:, j, :], oq[:, j, :]).then_inc(omix_hi, 1)

            for n in range(2):
                oqk_outs(n)
            stick_logs(0)
            for hd in range(C_HEADS):
                if hd + 2 < C_HEADS:
                    oqk_outs(hd + 2)
                stick_upper(hd)
                if hd + 1 < C_HEADS:
                    stick_logs(hd + 1)
                if hd and hd % 2 == 0:
                    pair_out(hd // 2 - 1)
                stick_exp(hd)
            for j in range(KT - 1):
                mix_upper(j)
            pair_out(KT - 1)
            mix_upper(KT - 1)
            upper_upto(OOUT + 2)
            product(OOUT, KT)
            upper_upto(FFN[1])
            norm(2, FFN[1])
            ffn(1)
            norm(3, NBLK)

        @block.vector
        def _(dve):
            eng = nc.vector
            own = [0]

            def count(ins):
                own[0] += 1
                ins.then_inc(dve_self, 1)

            def settle():
                dve.wait_ge(dve_self, own[0])

            def link(ins):
                count(ins)
                settle()

            def tt(o_, a, b, op):
                return eng.tensor_tensor(o_, a, b, op)

            def lower_x(n, t):
                dve.wait_ge(x_hi, NT * n + t + 1)
                cols = slice(t * P, (t + 1) * P)
                tt(xlo[:, :, cols], psf[:, 2 * t * S:2 * (t + 1) * S].rearrange("p (k n) -> p k n", k=KT),
                   xhi[:, :, cols].bitcast(F32), ALU.subtract).then_inc(x_ready, 1)

            def products4(a_r, a_i, b_r, b_i, n, shape):
                v4 = [t[:, 0:n] if len(shape) == 1 else
                      t[:, 0:n].rearrange("p (a b) -> p a b", b=shape[-1]) if len(shape) == 2 else
                      t[:, 0:n].rearrange("p (a b c) -> p a b c", b=shape[-2], c=shape[-1]) for t in t4]
                for o_, (a, b) in zip(v4, ((a_r, b_r), (a_i, b_i), (a_r, b_i), (a_i, b_r))):
                    count(tt(o_, a, b, ALU.mult))
                settle()
                return v4

            def cmul(o_r, o_i, a_r, a_i, b_r, b_i, n, shape):
                v4 = products4(a_r, a_i, b_r, b_i, n, shape)
                count(tt(o_r, v4[0], v4[1], ALU.subtract))
                count(tt(o_i, v4[2], v4[3], ALU.add))
                settle()

            for t in range(NT):
                lower_x(0, t)

            AR, AI, FR, FI, M8, CS, SN, LR, LI, M, MAG, TH, RS, RC, A, B, C_, D_ = range(18)
            dve.wait_ge(lam_landed, 48)
            dve.wait_ge(dt_ready, 1)
            dtb = dt2[:].unsqueeze(2).broadcast_to((PAIRS, 2, PS))

            def q_(i):
                return pl[:, i, :]

            def q2(i):
                return pl[:, i, :].rearrange("a (b p) -> a b p", b=2)

            tt(q2(M), q2(LR), dtb, ALU.mult).then_inc(m_ready, 1)
            link(tt(q2(TH), q2(LI), dtb, ALU.mult))
            link(eng.tensor_scalar(q_(A), q_(TH), 1 / (2 * math.pi), ROUNDER, ALU.mult, ALU.add))
            link(eng.tensor_scalar(q_(A), q_(A), ROUNDER, None, ALU.subtract))
            for part in (TWO_PI_1, TWO_PI_2, TWO_PI_3):
                link(eng.scalar_tensor_tensor(out=q_(TH), in0=q_(A), scalar=-part, in1=q_(TH),
                                              op0=ALU.mult, op1=ALU.add))
            link(eng.tensor_scalar(q_(RS), q_(TH), PI_BELOW, -PI_BELOW, ALU.min, ALU.max))
            link(eng.tensor_scalar(q_(RC), q_(RS), -1.0, None, ALU.mult))
            link(tt(q_(RC), q_(RC), q_(RS), ALU.min))
            eng.tensor_scalar(q_(RC), q_(RC), math.pi / 2, None, ALU.add).then_inc(arg_ready, 1)
            dve.wait_ge(mag_ready, 1)
            dve.wait_ge(trig_ready, 2)
            count(tt(q_(AR), q_(MAG), q_(CS), ALU.mult))
            count(tt(q_(AI), q_(MAG), q_(SN), ALU.mult))
            count(tt(q_(A), q_(LR), q_(LR), ALU.mult))
            count(tt(q_(B), q_(LI), q_(LI), ALU.mult))
            count(tt(q_(M8), q_(MAG), q_(MAG), ALU.mult))
            settle()
            count(tt(q_(A), q_(A), q_(B), ALU.add))
            count(eng.tensor_scalar(q_(C_), q_(AR), 1.0, None, ALU.subtract))
            count(tt(q_(D_), q_(M8), q_(M8), ALU.mult))
            settle()
            count(eng.reciprocal(q_(A), q_(A)))
            count(tt(q_(M8), q_(D_), q_(D_), ALU.mult))
            count(tt(q_(FR), q_(C_), q_(LR), ALU.mult))
            count(tt(q_(B), q_(AI), q_(LI), ALU.mult))
            count(tt(q_(FI), q_(AI), q_(LR), ALU.mult))
            count(tt(q_(TH), q_(C_), q_(LI), ALU.mult))
            settle()
            count(tt(q_(FR), q_(FR), q_(B), ALU.add))
            count(tt(q_(FI), q_(FI), q_(TH), ALU.subtract))
            settle()
            count(tt(q_(FR), q_(FR), q_(A), ALU.mult))
            count(tt(q_(FI), q_(FI), q_(A), ALU.mult))
            settle()
            eng.engine_nop().then_inc(pl_ready, 1)

            dve.wait_ge(rel_landed, 16)
            eng.tensor_copy(relext[:, 0:S - P], reltab[:, NREL - 1:NREL].broadcast_to((A_HEADS, S - P))).then_inc(
                relext_ready, 1)
            eng.tensor_copy(relext[:, S - P:5 * P], reltab[:, 2 * MAX_REL - 1::-1]
                            ).then_inc(relext_ready, 1)

            dve.wait_ge(d_landed, 16)
            dve.wait_ge(const_ready, 5)
            link(tt(dd[:], dd[:], ident[0:GI, 0:GI].unsqueeze(1).broadcast_to((GI, G, GI)), ALU.mult))

            dve.wait_ge(pl_turned, 1)
            eng.tensor_copy(par[:].rearrange("p a b -> p (a b)"), ps[:, 7, 0:7 * PAIRS]).then_inc(par_read, 1)
            dve.wait_ge(par_read, 1)
            dve.wait_ge(c_turned, 1)
            cre = ps[:, 6, :].rearrange("p (a b j) -> p a b j", b=2, j=GI)
            cim = ps[:, 7, :].rearrange("p (a b j) -> p a b j", b=2, j=GI)
            for b in range(2):
                rows = slice(b * PS, (b + 1) * PS)
                count(eng.tensor_copy(cr[rows], cre[rows, :, b, :]))
                count(eng.tensor_scalar(nci[rows], cim[rows, :, b, :], -1.0, None, ALU.mult))
            settle()
            eng.engine_nop().then_inc(par_out, 1)

            def wide(i, n):
                return par[:, i, :].unsqueeze(2).broadcast_to((P, PAIRS, n))

            dve.wait_ge(b_landed, 32)
            cmul(bbr[:], bbi[:], bnr[:], bni[:], wide(FR, GI), wide(FI, GI), PAIRS * GI, (PAIRS, GI))
            pr, pi, npi = pw[:, 0], pw[:, 1], pw[:, 2]
            count(eng.memset(pw[:, 0, :, 0:1], 1.0))
            count(eng.memset(pw[:, 1, :, 0:1], 0.0))
            count(eng.tensor_copy(pw[:, 0:2, :, 1], par[:, 0:2, :]))
            settle()
            n = 1
            while n < L:
                by_r = pw[:, 0, :, n:n + 1].broadcast_to((P, PAIRS, n))
                by_i = pw[:, 1, :, n:n + 1].broadcast_to((P, PAIRS, n))
                cmul(pw[:, 0, :, n + 1:2 * n + 1], pw[:, 1, :, n + 1:2 * n + 1], pw[:, 0, :, 1:n + 1],
                     pw[:, 1, :, 1:n + 1], by_r, by_i, PAIRS * n, (PAIRS, n))
                n *= 2
            link(eng.tensor_scalar(pw[:, 2], pw[:, 1], -1.0, None, ALU.mult))
            a = (par[:, CS, :], par[:, SN, :])
            for k in range(int(math.log2(L))):
                b = (ph[:, k % 2, 0, :], ph[:, k % 2, 1, :])
                cmul(*b, *a, *a, PAIRS, (PAIRS,))
                a = b
            count(eng.memset(phr[:, :, 0:1], 1.0))
            count(eng.memset(phi[:, :, 0:1], 0.0))
            count(eng.tensor_copy(phr[:, :, 1], a[0]))
            count(eng.tensor_copy(phi[:, :, 1], a[1]))
            settle()
            n, k = 2, int(math.log2(L))
            while n < NC:
                b = (ph[:, k % 2, 0, :], ph[:, k % 2, 1, :])
                cmul(*b, *a, *a, PAIRS, (PAIRS,))
                a = b
                cmul(phr[:, :, n:2 * n], phi[:, :, n:2 * n], phr[:, :, 0:n], phi[:, :, 0:n],
                     a[0].unsqueeze(2).broadcast_to((P, PAIRS, n)), a[1].unsqueeze(2).broadcast_to((P, PAIRS, n)),
                     PAIRS * n, (PAIRS, n))
                n, k = 2 * n, k + 1
            link(eng.memset(decay[:], 0.0))

            def build_in(q):
                if q:
                    dve.wait_ge(ssm_done, STEPS * (q - 1) + 2)
                pq = slice(q * PQ, (q + 1) * PQ)
                br = bbr[:, pq].unsqueeze(2).broadcast_to((P, PQ, L, GI))
                bi = bbi[:, pq].unsqueeze(2).broadcast_to((P, PQ, L, GI))
                ar = pw[:, 0, pq, 0:L].unsqueeze(3).broadcast_to((P, PQ, L, GI))
                ai = pw[:, 1, pq, 0:L].unsqueeze(3).broadcast_to((P, PQ, L, GI))
                v4 = products4(br, bi, ar, ai, PQ * L * GI, (PQ, L, GI))
                tt(wnr[:], v4[0], v4[1], ALU.subtract).then_inc(wn_ready, 1)
                tt(wni[:], v4[2], v4[3], ALU.add).then_inc(wn_ready, 1)
                dve.wait_ge(wn_ready, 2 * q + 2)

            def build_out(q):
                if q:
                    dve.wait_ge(ssm_done, STEPS * q)
                pq = slice(q * PQ, (q + 1) * PQ)
                for half in range(2):
                    lo = half * (L // 2)
                    n = L // 2 + half
                    sh = (P, PQ, n, GI)
                    c_r = cr[:, pq].unsqueeze(2).broadcast_to(sh)
                    c_i = nci[:, pq].unsqueeze(2).broadcast_to(sh)
                    a_r, a_i, a_n = (pw[:, k_, pq, lo:lo + n].unsqueeze(3).broadcast_to(sh) for k_ in range(3))
                    v4 = [t[:, 0:PQ * n * GI].rearrange("p (a b c) -> p a b c", b=n, c=GI) for t in t4]
                    count(tt(v4[0], c_r, a_r, ALU.mult))
                    count(tt(v4[1], c_i, a_i, ALU.mult))
                    count(tt(v4[2], c_r, a_n, ALU.mult))
                    count(tt(v4[3], c_i, a_r, ALU.mult))
                    settle()
                    tt(cxr[:, :, lo:lo + n], v4[0], v4[1], ALU.add).then_inc(cx_ready, 1)
                    tt(cxi[:, :, lo:lo + n], v4[2], v4[3], ALU.add).then_inc(cx_ready, 1)
                    dve.wait_ge(cx_ready, 4 * q + 2 * half + 2)

            def rotate(q):
                pq = slice(q * PQ, (q + 1) * PQ)
                count(eng.tensor_copy(decay[:, :, 1:], par[:, M8, pq].unsqueeze(2).broadcast_to((P, PQ, NC - 1))))
                fr_, fi_ = phr[:, pq], phi[:, pq]
                sr = ps[:, 7, 0:PQ * NC].rearrange("p (a c) -> p a c", c=NC)
                si = ps[:, 7, PQ * NC:2 * PQ * NC].rearrange("p (a c) -> p a c", c=NC)
                dve.wait_ge(ssm_done, STEPS * q + 5)
                v4 = products4(sr, si, fr_, fi_, PQ * NC, (PQ, NC))
                eng.engine_nop().then_inc(ssm_out, 1)
                count(tt(zin_r[:], v4[0], v4[1], ALU.add))
                count(tt(zin_i[:], v4[3], v4[2], ALU.subtract))
                settle()

                def flat(t):
                    return t[:].rearrange("p a c -> p (a c)")

                count(eng.tensor_tensor_scan(flat(zr), flat(decay), flat(zin_r), 0.0, ALU.mult, ALU.add))
                count(eng.tensor_tensor_scan(flat(zi), flat(decay), flat(zin_i), 0.0, ALU.mult, ALU.add))
                settle()
                cmul(xsr[:, :, 1:], xsi[:, :, 1:], zr[:], zi[:], fr_, fi_, PQ * NC, (PQ, NC))
                eng.engine_nop().then_inc(xs_ready, 1)

            def ssm_vector(steps):
                for q, s in steps:
                    if s in (2, 3):
                        dve.wait_ge(ssm_done, STEPS * q + s + 1)
                        if q and s == 2:
                            dve.wait_ge(toep_landed, 16 * L * q)
                        eng.tensor_copy(gk[0:GI].rearrange("i (a b) t j -> i a b (t j)", b=2)[:, :, s - 2, :],
                                        ps[0:GI, 7, :].rearrange("i (a n) -> i a n", n=P)).then_inc(ssm_out, 1)
                        dve.wait_ge(ssm_out, STEPS * q + s + 1)
                    if s == 3:
                        tt(gk[0:GI, :, 0, :], gk[0:GI, :, 0, :], dd[:, q * GQ:(q + 1) * GQ, :],
                           ALU.add).then_inc(gk_ready, 1)
                        if q + 1 < AT:
                            build_in(q + 1)
                    if s == 4:
                        rotate(q)
                    if s == 6 and q + 1 < AT:
                        build_out(q + 1)

            build_in(0)
            build_out(0)
            dve.wait_ge(const_ready, 5)
            for n in range(N_QK):
                ssm_vector(ssm_behind_qk(n))

            it = [(hd, i) for hd in range(A_HEADS) for i in range(NT)]

            def biased(n):
                hd, i = it[n]
                w = (i + 1) * P
                if i == 0:
                    dve.wait_ge(bias_landed[hd % 2], 16 * (hd // 2 + 1))
                    link(eng.memset(bias[P - CHUNK:P, hd % 2, S - CHUNK:S], MASKED))
                dve.wait_ge(s_done, n + 1)
                if n >= 2:
                    dve.wait_ge(pt_done, n - 1)
                eng.tensor_tensor_reduce(sc[:, n % 2, 0:w], ps[:, n % 2, 0:w], bias[:, hd % 2, S - w:S], 1.0, -3e38,
                                         ALU.add, ALU.max, sm[:, n % 2, 0:1]).then_inc(s_biased, 1)
                dve.wait_ge(s_biased, n + 1)
                eng.tensor_scalar(sm[:, n % 2, 1:2], sm[:, n % 2, 0:1], -1.0, None, ALU.mult).then_inc(s_negmax, 1)

            def normalised(n):
                w = (it[n][1] + 1) * P
                dve.wait_ge(s_exp, n + 1)
                link(eng.reciprocal(sm[:, n % 2, 3:4], sm[:, n % 2, 2:3]))
                eng.tensor_scalar(sc[:, n % 2, 0:w], sc[:, n % 2, 0:w], sm[:, n % 2, 3:4], None,
                                  ALU.mult).then_inc(p_ready, 1)

            def pair_lower(j):
                dve.wait_ge(ao_hi, j + 1)
                tt(xlo[:, j, :], ps[:, 6, :], xhi[:, j, :].bitcast(F32), ALU.subtract).then_inc(ao_out, 1)

            for n in range(len(it) + 1):
                if n < len(it):
                    biased(n)
                if n:
                    normalised(n - 1)
                    hd, i = it[n - 1]
                    if i == NT - 1:
                        ssm_vector(ssm_behind_head(hd))
                    if i == 1 and hd and hd % 2 == 0:
                        pair_lower(hd // 2 - 1)
            pair_lower(A_HEADS // 2 - 1)

            for q in range(AT):
                dve.wait_ge(y_hi, q + 1)
                tt(ylo[:, q, :], yT[:, q].rearrange("p t c -> p (t c)"), yhi[:, q, :].bitcast(F32),
                   ALU.subtract).then_inc(y_ready, 1)
            for m in range(AT):
                dve.wait_ge(glu_sig, m + 1)
                tt(gt[:, m % 2, :], yT[:, m].rearrange("p t c -> p (t c)"), sg[:, m % 2, :],
                   ALU.mult).then_inc(ob_ready, 1)
                dve.wait_ge(ob_hi, m + 1)
                tt(xlo[:, AT + m, :].rearrange("p (c t) -> p c t", t=L),
                   gt[:, m % 2, :].rearrange("p (t c) -> p c t", t=L),
                   xhi[:, AT + m, :].rearrange("p (c t) -> p c t", t=L).bitcast(F32), ALU.subtract).then_inc(mix_b, 1)

            def norm(n):
                dve.wait_ge(lnp_landed, 32 * (n + 1))

                def statistics(t):
                    if t < NT - 1:
                        dve.wait_ge(acc_done, (NT - 1) * n + t + 1)
                    else:
                        dve.wait_ge(w_used, (EOUT + KT, FFN[0] + 3 * FT, OOUT + KT, FFN[1] + 3 * FT)[n])
                    link(eng.scalar_tensor_tensor(out=h[:, t, :], in0=h[:, t, :], scalar=ALPHA,
                                                  in1=psf[:, 2 * t * S:2 * (t + 1) * S], op0=ALU.mult, op1=ALU.add))
                    for c in range(2):
                        count(eng.bn_stats(stats[:, t, c, :], h[:, t, c * S:(c + 1) * S]))
                    settle()
                    link(eng.bn_aggr(mv[:, t, :], stats[:, t].rearrange("p a b -> p (a b)")))
                    eng.tensor_scalar(lns[:, t, 0:1], mv[:, t, 1:2], EPS, None, ALU.add).then_inc(var_ready, 1)

                def scales(t):
                    dve.wait_ge(std_ready, NT * n + t + 1)
                    link(eng.reciprocal(lns[:, t, 2:3], lns[:, t, 1:2]))
                    eng.tensor_scalar(lns[:, t, 3:4], mv[:, t, 0:1], -1.0, lns[:, t, 2:3],
                                      ALU.mult, ALU.mult).then_inc(scale_ready, 1)

                def gain(t):
                    dve.wait_ge(normed, NT * n + t + 1)
                    link(tt(h[:, t, :], h[:, t, :], lnp[:, 0, :], ALU.mult))
                    tt(h[:, t, :], h[:, t, :], lnp[:, 1, :], ALU.add).then_inc(h_ready, 1)

                for t in range(NT + 1):
                    if t < NT:
                        statistics(t)
                        scales(t)
                    if t:
                        gain(t - 1)
                    if n < 3 and t >= 2:
                        lower_x(n + 1, t - 2)
                if n < 3:
                    lower_x(n + 1, NT - 1)

            def ffn(layer):
                for m in range(FT):
                    c = layer * FT + m
                    dve.wait_ge(silu_ready, c + 1)
                    dve.wait_ge(w_used, FFN[layer] + 2 * m + 2)
                    if m >= 2:
                        dve.wait_ge(g_lo, c - 1)
                    tt(gt[:, m % 2, :], ps[:, 2 * (m % 2) + 1, :], sg[:, m % 2, :], ALU.mult).then_inc(g_ready, 1)
                    dve.wait_ge(g_hi, c + 1)
                    tt(glo[:, m, :], gt[:, m % 2, :], ghi[:, m, :].bitcast(F32), ALU.subtract).then_inc(g_lo, 1)

            dve.wait_ge(h_landed, 16 * NT)
            norm(0)
            ffn(0)
            norm(1)

            def stick_plus(hd):
                dve.wait_ge(l_ready, hd + 1)
                if hd:
                    dve.wait_ge(sp_lo, hd)
                eng.scalar_tensor_tensor(out=sp[:], in0=psf[:, 0:TRI_W], scalar=0.0, in1=lg[:], op0=ALU.max,
                                         op1=ALU.add).then_inc(sp_raw, 1)
                if hd >= 3:
                    dve.wait_ge(opv_done, hd - 2)
                eng.scalar_tensor_tensor(out=wt[:, hd % 3], in0=psf[:, 0:TRI_W], scalar=0.0, in1=lg[:],
                                         op0=ALU.min, op1=ALU.subtract).then_inc(z_read, 1)

            def stick_lower(hd):
                dve.wait_ge(sp_hi, hd + 1)
                tt(splo[:], sp[:], sphi[:].bitcast(F32), ALU.subtract).then_inc(sp_lo, 1)

            def stick_weight(hd):
                dve.wait_ge(r_done, hd + 1)
                dve.wait_ge(z_read, hd + 1)
                tt(wt[:, hd % 3], wt[:, hd % 3], psf[:, 3 * S:3 * S + TRI_W], ALU.subtract).then_inc(lw_ready, 1)

            stick_plus(0)
            for hd in range(C_HEADS):
                stick_lower(hd)
                if hd + 1 < C_HEADS:
                    stick_plus(hd + 1)
                stick_weight(hd)
            for j in range(KT):
                dve.wait_ge(omix_hi, j + 1)
                tt(xlo[:, j, :], oq[:, j, :], xhi[:, j, :].bitcast(F32), ALU.subtract).then_inc(omix, 1)
            norm(2)
            ffn(1)
            norm(3)

        @block.tensor
        def _(pe):
            eng = nc.tensor

            def three(o_, w_hi_, w_lo_, x_hi_, x_lo_, start, stop):
                eng.matmul(o_, w_hi_, x_hi_, start=start, stop=False)
                eng.matmul(o_, w_hi_, x_lo_, start=False, stop=False)
                return eng.matmul(o_, w_lo_, x_hi_, start=False, stop=stop)

            def feature_major(b, o_, hi, lo, nk=KT, col=0, cols=P):
                pe.wait_ge(w_lo, b + 1)
                wh = whi[:, b % WS, :].rearrange("p (k n) -> p k n", k=nk)
                wl = wlo[:, b % WS, :].rearrange("p (k n) -> p k n", k=nk)
                c = slice(col, col + P)
                for k in range(nk):
                    mm = three(o_, wh[:, k, c], wl[:, k, c], hi[:, k, :], lo[:, k, :], k == 0, k == nk - 1)
                return mm

            def token_rows(b, k, r, width, hi, lo, t, bank, n_half, start, stop):
                c = slice(t * P, (t + 1) * P)
                for half in range(n_half):
                    w = slice(r * width + half * S, r * width + half * S + S)
                    o_ = ps[:, bank + half, :]
                    eng.matmul(o_, hi[:, k, c], whi[:, b % WS, w], start=start, stop=False)
                    eng.matmul(o_, hi[:, k, c], wlo[:, b % WS, w], start=False, stop=False)
                    mm = eng.matmul(o_, lo[:, k, c], whi[:, b % WS, w], start=False, stop=stop)
                return mm

            def token_major(first, nk, hi, lo, ready=None, order=(0, 1, 2, 3), before=None):
                for k in range(nk - TAIL):
                    pe.wait_ge(w_lo, first + k + 1)
                    if ready:
                        ready(k)
                    for t in order:
                        if k == 0 and before:
                            before(t)
                        mm = token_rows(first + k, k, 0, D, hi, lo, t, 2 * t, 2, k == 0, False)
                    mm.then_inc(w_used, 1)
                for t in range(NT):
                    for k in range(nk - TAIL, nk):
                        if t == 0:
                            pe.wait_ge(w_lo, first + k + 1)
                            if ready:
                                ready(k)
                        mm = token_rows(first + k, k, 0, D, hi, lo, t, 2 * t, 2, False, k == nk - 1)
                        if t == NT - 1 and k < nk - 1:
                            mm.then_inc(w_used, 1)
                    if t < NT - 1:
                        mm.then_inc(acc_done, 1)
                mm.then_inc(w_used, 1)
                return mm

            def turn(n, t):
                for k in range(KT):
                    mm = eng.transpose(psf[:, 2 * t * S + k * P:2 * t * S + (k + 1) * P],
                                       h[:, t, k * P:(k + 1) * P], ident[:])
                mm.then_inc(turned, 1)

            pe.wait_ge(const_ready, 5)
            for t in range(NT):
                pe.wait_ge(x_landed[t], 16)
                turn(0, t)
            pe.wait_ge(x_ready, NT)

            def project(n, b):
                if n >= 2:
                    pe.wait_ge(proj_out, n - 1)
                mm = feature_major(b, ps[:, 4 + n % 2, :], xhi, xlo)
                mm.then_inc(w_used, 1)

            project(0, 0)
            pe.wait_ge(pl_ready, 1)
            for i in range(7):
                mm = eng.transpose(ps[:, 7, i * PAIRS:(i + 1) * PAIRS], pl[:, i, :], ident[0:PAIRS, 0:PAIRS])
            mm.then_inc(pl_turned, 1)
            project(1, 1)
            pe.wait_ge(c_landed, 64)
            for t in range(AT):
                eng.transpose(ps[:, 6, t * P:(t + 1) * P], cdr[:, t].rearrange("p a b -> p (a b)"), ident[:])
            project(2, 2)
            project(3, 3)
            pe.wait_ge(par_read, 1)
            for t in range(AT):
                mm = eng.transpose(ps[:, 7, t * P:(t + 1) * P], cdi[:, t].rearrange("p a b -> p (a b)"), ident[:])
            mm.then_inc(c_turned, 1)
            for b in range(4):
                pe.wait_ge(w_lo, AT + b + 1)
                for r in range(2):
                    k = 2 * b + r
                    for t in range(NT):
                        mm = token_rows(AT + b, k, r, WA, xhi, xlo, t, t, 1, k == 0, k == KT - 1)
                mm.then_inc(w_used, 1)

            def ssm_products(steps):
                for q, s in steps:
                    if q or s:
                        pe.wait_ge(ssm_out, STEPS * q + s)
                    p7 = ps[:, 7, :]
                    if s in (0, 1):
                        pe.wait_ge(wn_ready, 2 * q + 2)
                        if q == 0:
                            pe.wait_ge(par_out, 1)
                        src = (wnr, wni)[s]
                        for a in range(PQ):
                            mm = eng.transpose(p7[:, a * P:(a + 1) * P], src[:, a].rearrange("p l i -> p (l i)"),
                                               ident[:])
                    if s in (2, 3):
                        pe.wait_ge(cx_ready, 4 * q + 4)
                        rows = slice((s - 2) * PS, (s - 1) * PS)
                        for a in range(PQ):
                            o_ = p7[0:GI, a * P:(a + 1) * P]
                            eng.matmul(o_, bbr[rows, q * PQ + a, :],
                                       cxr[rows, a, 0:L, :].rearrange("p l j -> p (l j)"), start=True, stop=False)
                            mm = eng.matmul(o_, bbi[rows, q * PQ + a, :],
                                            cxi[rows, a, 0:L, :].rearrange("p l j -> p (l j)"),
                                            start=False, stop=True)
                    if s == 4:
                        pe.wait_ge(u_landed[q], 16 * L)
                        for g in range(GQ):
                            a, b = g // 2, g % 2
                            rows = slice(b * PS, (b + 1) * PS)
                            for part, w in enumerate((winr, wini)):
                                o_ = p7[rows, part * PQ * NC + a * NC:part * PQ * NC + (a + 1) * NC]
                                mm = eng.matmul(o_, w[:, a, rows], u8[:, q, g, :], start=True, stop=True)
                    if s in (5, 6):
                        pe.wait_ge(xs_ready, q + 1)
                        pe.wait_ge(toep_landed, 16 * L * (q + 1))
                        rows = slice((s - 5) * PS, (s - 4) * PS)
                        for a in range(PQ):
                            g = 2 * a + s - 5
                            o_ = p7[:, a * NC:(a + 1) * NC]
                            eng.matmul(o_, toep[:, g, :], u8[:, q, g, :], start=True, stop=False)
                            eng.matmul(o_, cxr[rows, a, 1:, :].rearrange("p l j -> p (l j)"), xsr[rows, a, 0:NC],
                                       start=False, stop=False)
                            mm = eng.matmul(o_, cxi[rows, a, 1:, :].rearrange("p l j -> p (l j)"),
                                            xsi[rows, a, 0:NC], start=False, stop=True)
                    mm.then_inc(ssm_done, 1)

            for n in range(N_QK):
                project(AT + n, 2 * AT + n)
                ssm_products(ssm_behind_qk(n))

            it = [(hd, i) for hd in range(A_HEADS) for i in range(NT)]
            pe.wait_ge(proj_out, 3 * AT)
            pe.wait_ge(v_out, NT)

            def scores(n):
                hd, i = it[n]
                rows = slice((hd % 2) * HD, (hd % 2 + 1) * HD)
                if n >= 2:
                    pe.wait_ge(s_biased, n - 1)
                eng.matmul(ps[:, n % 2, 0:(i + 1) * P], qT[rows, hd // 2, i * P:(i + 1) * P],
                           kT[rows, hd // 2, 0:(i + 1) * P], start=True, stop=True).then_inc(s_done, 1)

            def turn_probs(n):
                hd, i = it[n]
                pe.wait_ge(p_ready, n + 1)
                if n >= 2:
                    pe.wait_ge(pt_out, n - 1)
                for j in range(i + 1):
                    mm = eng.transpose(ps[:, 2 + n % 2, j * P:(j + 1) * P], sc[:, n % 2, j * P:(j + 1) * P], ident[:])
                mm.then_inc(pt_done, 1)

            def head_out(hd):
                rows = slice((hd % 2) * HD, (hd % 2 + 1) * HD)
                pe.wait_ge(pt_out, NT * (hd + 1))
                if hd >= 2 and hd % 2 == 0:
                    pe.wait_ge(ao_out, hd // 2)
                for j in range(NT):
                    mm = eng.matmul(ps[rows, 6, j * P:S], v[:, j, hd * HD:(hd + 1) * HD], pt[:, j, j * P:S],
                                    start=(j == 0), stop=(j == NT - 1))
                mm.then_inc(pv_done, 1)

            scores(0)
            for n in range(len(it)):
                if n + 1 < len(it):
                    scores(n + 1)
                turn_probs(n)
                hd, i = it[n]
                if i == NT - 1:
                    head_out(hd)
                    ssm_products(ssm_behind_head(hd))

            pe.wait_ge(y_ready, AT)
            for m in range(AT):
                b = GLU + m // 2
                if m >= 2:
                    pe.wait_ge(glu_sig, m - 1)
                mm = feature_major(b, ps[:, 4 + m % 2, :], yhi, ylo, nk=AT, col=(m % 2) * P)
                mm.then_inc(w_used if m % 2 else glu_done, 1)
            pe.wait_ge(ao_out, A_HEADS // 2)
            pe.wait_ge(mix_b, AT)
            token_major(EOUT, KT, xhi, xlo)

            def turns(n):
                for t in range(NT):
                    pe.wait_ge(h_ready, NT * (n - 1) + t + 1)
                    turn(n, t)
                pe.wait_ge(x_ready, NT * (n + 1))

            def ffn(layer):
                f = FFN[layer]
                for m in range(FT):
                    c = layer * FT + m
                    for part in range(2):
                        b = f + 2 * m + part
                        if m >= 2 and part == 0:
                            pe.wait_ge(g_ready, c - 1)
                        mm = feature_major(b, ps[:, 2 * (m % 2) + part, :], xhi, xlo)
                        mm.then_inc(w_used, 1)

                def ready(k):
                    pe.wait_ge(g_lo, layer * FT + k + 1)

                def before(t):
                    if t == 0:
                        pe.wait_ge(g_ready, (layer + 1) * FT)

                token_major(f + 2 * FT, FT, ghi, glo, ready, order=(2, 3, 0, 1), before=before)

            turns(1)
            ffn(0)
            turns(2)

            for k in range(KT):
                pe.wait_ge(w_lo, OV + k + 1)
                for t in range(NT):
                    mm = token_rows(OV + k, k, 0, D, xhi, xlo, t, 2 * t, 2, k == 0, k == KT - 1)
                mm.then_inc(w_used, 1)
            pe.wait_ge(ov_out, NT)

            def oqk(n):
                if n:
                    pe.wait_ge(oqk_out, n)
                b = OQK + n
                mm = feature_major(b, ps[:, 6, :], xhi, xlo)
                mm.then_inc(w_used, 1)

            def stick_scores(hd):
                rows = slice((hd % 2) * HD, (hd % 2 + 1) * HD)
                j_ = hd // 2
                pe.wait_ge(oqk_out, 2 * j_ + 2)
                if hd:
                    pe.wait_ge(z_read, hd)
                for j in range(NT):
                    mm = eng.matmul(psf[:, TRI[j]:TRI[j] + (NT - j) * P], ok[rows, j_, j * P:(j + 1) * P],
                                    oq[rows, j_, j * P:S], start=True, stop=True)
                mm.then_inc(z_done, 1)

            def stick_sums(hd):
                pe.wait_ge(sp_lo, hd + 1)
                if hd:
                    pe.wait_ge(lw_ready, hd)
                for j in range(NT):
                    for j2 in range(j, NT):
                        o_ = psf[:, 3 * S + TRI[j] + (j2 - j) * P:3 * S + TRI[j] + (NT - j) * P]
                        cols = slice(TRI[j2], TRI[j2] + (NT - j2) * P)
                        w = tri if j2 == j else ones
                        eng.matmul(o_, w[:], sphi[:, cols], start=(j2 == j), stop=False)
                        mm = eng.matmul(o_, w[:], splo[:, cols], start=False, stop=(j2 == NT - 1))
                mm.then_inc(r_done, 1)

            def stick_out(hd):
                rows = slice((hd % 2) * HD, (hd % 2 + 1) * HD)
                pe.wait_ge(w_ready, NT * (hd + 1))
                if hd >= 2 and hd % 2 == 0:
                    pe.wait_ge(o_out, hd // 2)
                for j in range(NT):
                    mm = eng.matmul(ps[rows, 7, j * P:S], ov[:, j, hd * HD:(hd + 1) * HD],
                                    wt[:, hd % 3, TRI[j]:TRI[j] + (NT - j) * P], start=(j == 0), stop=(j == NT - 1))
                mm.then_inc(opv_done, 1)

            oqk(0)
            oqk(1)
            pe.wait_ge(const_ready, 6)
            stick_scores(0)
            for hd in range(C_HEADS):
                if hd + 2 < C_HEADS:
                    oqk(hd + 2)
                if hd + 1 < C_HEADS:
                    stick_scores(hd + 1)
                stick_sums(hd)
                if hd:
                    stick_out(hd - 1)
            stick_out(C_HEADS - 1)
            pe.wait_ge(omix, KT)
            token_major(OOUT, KT, xhi, xlo)
            turns(3)
            ffn(1)


_INS = ["x", "even_w_in", "even_rel_bias", "ssm_lambda_re", "ssm_lambda_im", "ssm_b_re", "ssm_b_im", "ssm_c_re",
        "ssm_c_im", "ssm_d", "ssm_log_dt", "ssm_glu_w", "ssm_glu_b", "even_w_out", "odd_w_in", "odd_w_out",
        "ffn_w1", "ffn_w3", "ffn_w2", "ln_mix_g", "ln_mix_b", "ln_ffn_g", "ln_ffn_b"]


def kernel(**inputs):
    import concourse.bacc as _bacc
    from concourse.bass_utils import run_bass_kernel_spmd as _run

    nc = _bacc.Bacc("TRN2", target_bir_lowering=False, num_devices=1)
    arrays, args = {}, []
    for name in _INS:
        a = np.ascontiguousarray(inputs[name])
        arrays[f"in_{name}"] = a
        args.append(nc.dram_tensor(f"in_{name}", a.shape, mybir.dt.from_np(a.dtype), kind="ExternalInput").ap())
    out = nc.dram_tensor("out", (1, S, D), F32, kind="ExternalOutput").ap()
    build(nc, *args, out)
    r = _run(nc, [arrays], core_ids=[0])
    return r.results[0]["out"]
```

```python
import math
from contextlib import ExitStack

import numpy as np
import concourse.bass as bass
from concourse import mybir

P = 128
D = 1024
S = 512
KT = D // P
NT = S // P
DFF = 2816
FT = DFF // P
WA = 512
AT = WA // P
HD = 64
A_HEADS = WA // HD
C_HEADS = D // HD
CHUNK = 64
MAX_REL = 2 * CHUNK
NREL = 2 * MAX_REL + 1
G, GI, PS = 32, 16, 64
PAIRS = G // 2
GQ = G // AT
PQ = PAIRS // AT
L = P // GI
NC = S // L
ALPHA = 4.0 ** 0.25
EPS = 1e-5
QSCALE = HD ** -0.5
MASKED = -1e30

WB = 1024
RAW = 3
WS = 5
TAIL = 4

ALU = mybir.AluOpType
ACT = mybir.ActivationFunctionType
F32 = mybir.dt.float32
F32R = mybir.dt.float32r
AX = mybir.AxisListType

TWO_PI_1 = 6.28125
TWO_PI_2 = math.floor((2 * math.pi - TWO_PI_1) * 2 ** 20) / 2 ** 20
TWO_PI_3 = float(np.float32(2 * math.pi - TWO_PI_1 - TWO_PI_2))
ROUNDER = 1.5 * 2.0 ** 23
PI_BELOW = 3.1415925

TRI = {0: 0, 1: 512, 3: 896, 2: 1024}
TRI_W = 1280


def build(nc, x, even_w_in, rel, lam_re, lam_im, b_re, b_im, c_re, c_im, d_skip, log_dt, glu_w, glu_b,
          even_w_out, odd_w_in, odd_w_out, w1, w3, w2, ln_mix_g, ln_mix_b, ln_ffn_g, ln_ffn_b, out):
    blocks = []

    def feature_tile(w, c0):
        blocks.append(w[:, c0:c0 + P].rearrange("(k p) n -> p k n", p=P))

    def row_tiles(w, r0, c0, cols):
        n = WB // cols
        blocks.append(w[r0:r0 + n * P, c0:c0 + cols].rearrange("(k p) n -> p k n", p=P))

    ewi, ewo = even_w_in[0], even_w_out[0]
    owi, owo = odd_w_in[0], odd_w_out[0]
    for m in range(AT):
        feature_tile(ewi, 3 * WA + m * P)
    for b in range(4):
        row_tiles(ewi, b * 2 * P, 2 * WA, WA)
    for m in range(AT):
        feature_tile(ewi, m * P)
        feature_tile(ewi, WA + m * P)
    GLU = len(blocks)
    for b in range(2):
        blocks.append(glu_w[0][:, b * 256:(b + 1) * 256].rearrange("(k p) n -> p k n", p=P))
    EOUT = len(blocks)
    for k in range(KT):
        row_tiles(ewo, k * P, 0, D)
    FFN = [len(blocks), 0]

    def ffn_blocks(layer):
        FFN[layer] = len(blocks)
        for m in range(FT):
            feature_tile(w1[layer], m * P)
            feature_tile(w3[layer], m * P)
        for k in range(FT):
            row_tiles(w2[layer], k * P, 0, D)

    ffn_blocks(0)
    OV = len(blocks)
    for k in range(KT):
        row_tiles(owi, k * P, 2 * D, D)
    OQK = len(blocks)
    for m in range(KT):
        feature_tile(owi, m * P)
        feature_tile(owi, D + m * P)
    OOUT = len(blocks)
    for k in range(KT):
        row_tiles(owo, k * P, 0, D)
    ffn_blocks(1)
    NBLK = len(blocks)

    ctx = ExitStack()
    with ctx:
        base = 16512
        fence = ctx.enter_context(nc.sbuf_tensor("fence", [P, (229344 - base) // 4], F32))
        at = [base]

        def put(name, shape, dt=F32, off=None):
            o = at[0] if off is None else off
            t = nc.alloc_sbuf_tensor_at(name, shape, dt, offset=o)
            size = (4 * int(np.prod(shape[1:])) + 31) // 32 * 32
            if off is None:
                at[0] += size
            return t, o + size

        def fixed(name, shape, dt=F32):
            return put(name, shape, dt)[0]

        raw = fixed("raw", [P, RAW, WB])
        whi = fixed("whi", [P, WS, WB], F32R)
        wlo = fixed("wlo", [P, WS, WB], F32R)
        xhi = fixed("xhi", [P, KT, S], F32R)
        xlo = fixed("xlo", [P, KT, S], F32R)
        arena = at[0]
        h = fixed("h", [P, NT, D])
        g_region = at[0]
        ghi = fixed("ghi", [P, FT, S], F32R)
        glo = fixed("glo", [P, FT, S], F32R)
        lnp = fixed("lnp", [P, 2, D])
        arena_end = at[0]
        ident = fixed("ident", [P, P])
        tri = fixed("tri", [P, P], F32R)
        ones = fixed("ones", [P, P], F32R)
        sg = fixed("sg", [P, 2, S])
        gt = fixed("gt", [P, 2, S])
        stats = fixed("stats", [P, NT, 2, 6])
        mv = fixed("mv", [P, NT, 2])
        lns = fixed("lns", [P, NT, 4])
        glub = fixed("glub", [P, AT])
        sm = fixed("sm", [P, 3, 4])
        assert at[0] <= 229344

        e = [arena]

        def even(name, shape, dt=F32):
            t, e[0] = put(name, shape, dt, e[0])
            assert e[0] <= arena_end, (name, e[0] - arena_end)
            return t

        pt = even("pt", [P, NT, S])
        bias = even("bias", [P, 2, S])
        gk = even("gk", [P, GQ, L, GI])
        assert e[0] == g_region
        qT = even("qT", [P, AT, S])
        kT = even("kT", [P, AT, S])
        v = even("v", [P, NT, WA])
        sc = even("sc", [P, 3, S])
        yT = even("yT", [P, AT, L, NC])
        phr = even("phr", [P, PAIRS, NC])
        phi = even("phi", [P, PAIRS, NC])
        u8 = even("u8", [P, AT, GQ, NC])
        uP = even("uP", [P, L, NC])
        y8 = even("y8", [P, GQ, NC])
        winr = even("winr", [P, PQ, P])
        wini = even("wini", [P, PQ, P])
        cxr = even("cxr", [P, PQ, L + 1, GI])
        cxi = even("cxi", [P, PQ, L + 1, GI])
        toep = even("toep", [P, GQ, P])
        wnr = even("wnr", [P, PQ, L, GI])
        wni = even("wni", [P, PQ, L, GI])
        zin_r = even("zin_r", [P, PQ, NC])
        zin_i = even("zin_i", [P, PQ, NC])
        zr = even("zr", [P, PQ, NC])
        zi = even("zi", [P, PQ, NC])
        xsr = even("xsr", [P, PQ, NC + 1])
        xsi = even("xsi", [P, PQ, NC + 1])
        decay = even("decay", [P, PQ, NC])
        bbr = even("bbr", [P, PAIRS, GI])
        bbi = even("bbi", [P, PAIRS, GI])
        bnr = even("bnr", [P, PAIRS, GI])
        bni = even("bni", [P, PAIRS, GI])
        cr = even("cr", [P, PAIRS, GI])
        nci = even("nci", [P, PAIRS, GI])
        pw = even("pw", [P, 3, PAIRS, L + 1])
        par = even("par", [P, 7, PAIRS])
        ph = even("ph", [P, 2, 2, PAIRS])
        dd = even("dd", [GI, G, GI])
        kept = even("kept", [P, 2, S])
        t4 = [sg[:, i // 2, (i % 2) * 256:(i % 2 + 1) * 256] for i in range(4)]
        pl, o = put("pl", [PAIRS, 24, P], F32, g_region)
        reltab, o = put("reltab", [A_HEADS, NREL], F32, o)
        relext, o = put("relext", [A_HEADS, 5 * P], F32, o)
        dt2, o = put("dt2", [PAIRS, 2], F32, o)
        assert o <= g_region + 2 * 4 * AT * S
        cdr, o = put("cdr", [P, AT, 2, PS], F32, g_region + 2 * 4 * AT * S)
        cdi, o = put("cdi", [P, AT, 2, PS], F32, o)
        yhi, o = put("yhi", [P, AT, S], F32R, g_region)
        ylo, o = put("ylo", [P, AT, S], F32R, o)

        oatt, o = put("oatt", [P, KT, S], F32, g_region)
        oqk_hi, o = put("oqk_hi", [P, 2, 2, S], F32R, o)
        oqk_lo, o = put("oqk_lo", [P, 2, 2, S], F32R, o)
        ov, o = put("ov", [P, NT, D], F32, o)
        lg, o = put("lg", [P, TRI_W], F32, o)
        sp, o = put("sp", [P, TRI_W], F32, o)
        sphi, o = put("sphi", [P, TRI_W], F32R, o)
        splo, o = put("splo", [P, TRI_W], F32R, o)
        wt, o = put("wt", [P, 3, TRI_W], F32, o)
        assert o <= g_region + 2 * 4 * FT * S, o - g_region

        ps = ctx.enter_context(nc.psum_tensor("ps", [P, 8, S], F32))
        psf = ps[:].rearrange("p b n -> p (b n)")

        u_dram = nc.dram_tensor("u_scratch", (AT, P, S), F32, kind="Internal").ap()
        y_dram = nc.dram_tensor("y_scratch", (AT, P, S), F32, kind="Internal").ap()
        rel_dram = nc.dram_tensor("rel_scratch", (A_HEADS, 5 * P), F32, kind="Internal").ap()

        def sem(name):
            return ctx.enter_context(nc.semaphore(name))

        w_landed = [sem(f"w_landed{i}") for i in range(RAW)]
        w_hi, w_lo, w_used = sem("w_hi"), sem("w_lo"), sem("w_used")
        x_landed = [sem(f"x_landed{i}") for i in range(NT)]
        lam_landed, b_landed, c_landed, rel_landed, glub_landed, d_landed = (
            sem(n) for n in ("lam_landed", "b_landed", "c_landed", "rel_landed", "glub_landed", "d_landed"))
        const_ready, const_zero = sem("const_ready"), sem("const_zero")
        turned, x_hi, x_ready = sem("turned"), sem("x_hi"), sem("x_ready")
        proj_out, v_out = sem("proj_out"), sem("v_out")
        dt_ready, m_ready, mag_ready, arg_ready, trig_ready = (
            sem(n) for n in ("dt_ready", "m_ready", "mag_ready", "arg_ready", "trig_ready"))
        pl_ready, pl_turned, par_read, c_turned, par_out = (
            sem(n) for n in ("pl_ready", "pl_turned", "par_read", "c_turned", "par_out"))
        u_stored, y_stored = sem("u_stored"), sem("y_stored")
        u_landed = [sem(f"u_landed{i}") for i in range(AT)]
        y_landed = [sem(f"y_landed{i}") for i in range(AT)]
        toep_landed = sem("toep_landed")
        wn_ready, cx_ready, gk_ready, xs_ready = (
            sem(n) for n in ("wn_ready", "cx_ready", "gk_ready", "xs_ready"))
        ssm_done = sem("ssm_done")
        ssm_out = [sem(f"ssm_out{i}") for i in range(2)]
        tables_ready, pool_self = sem("tables_ready"), sem("pool_self")
        relext_ready, rel_stored = sem("relext_ready"), sem("rel_stored")
        bias_landed = [sem(f"bias_landed{i}") for i in range(2)]
        s_done, s_biased, s_negmax, s_exp, p_ready, pt_done, pt_out, pv_done, ao_hi, ao_out = (
            sem(n) for n in ("s_done", "s_biased", "s_negmax", "s_exp", "p_ready", "pt_done", "pt_out",
                             "pv_done", "ao_hi", "ao_out"))
        ao_kept = sem("ao_kept")
        y_gelu, y_hi, y_ready, glu_done, glu_sig, ob_ready, ob_hi, mix_b = (
            sem(n) for n in ("y_gelu", "y_hi", "y_ready", "glu_done", "glu_sig", "ob_ready", "ob_hi", "mix_b"))
        acc_done, var_ready, std_ready, rstd_ready, scaled, h_ready, h_last, lnp_landed, h_landed = (
            sem(n) for n in ("acc_done", "var_ready", "std_ready", "rstd_ready", "scaled", "h_ready", "h_last",
                             "lnp_landed", "h_landed"))
        silu_ready, g_ready, g_hi, g_lo = (sem(n) for n in ("silu_ready", "g_ready", "g_hi", "g_lo"))
        ov_out, qk_hi, qk_out = sem("ov_out"), sem("qk_hi"), sem("qk_out")
        z_done, l_ready, z_read, sp_raw, sp_masked, sp_hi, sp_lo, r_done, lw_ready, w_exp, w_ready, opv_done, o_out = (
            sem(n) for n in ("z_done", "l_ready", "z_read", "sp_raw", "sp_masked", "sp_hi", "sp_lo", "r_done", "lw_ready",
                             "w_exp", "w_ready", "opv_done", "o_out"))
        omix_hi, omix = sem("omix_hi"), sem("omix")
        dve_self, act_self = sem("dve_self"), sem("act_self")
        out_stored = sem("out_stored")

        ITEMS = [(hd, i) for hd in range(A_HEADS) for i in range(NT)]
        TICKS = len(ITEMS) + NT - 1
        STEPS = 7
        SSM_BANK = (7, 5)

        def ssm_steps(n):
            after = [(n // STEPS - 1, 5), (n // STEPS - 1, 6)] if n % STEPS == 0 else []
            now = [(n // STEPS, n % STEPS)] if n % STEPS < 5 else []
            return [(q, st) for q, st in after + now if 0 <= q < AT]

        def ssm_read(q, st):
            k = STEPS * q + st
            return ssm_out[k % 2], k // 2 + 1

        X_USED = 24

        def qk_of(n):
            return n // 4 + 2 if n % 4 == 3 and n // 4 + 2 < 2 * AT else None

        LEAD = 3
        block = ctx.enter_context(nc.Block())

        @block.sync
        def _(sp_):
            eng = nc.sync
            issued = [0]

            def weights_upto(n):
                while issued[0] < min(n, NBLK):
                    b = issued[0]
                    if b >= RAW:
                        sp_.wait_ge(w_lo, b - RAW + 1)
                    src = blocks[b]
                    dst = raw[:, b % RAW, :].rearrange("p (k n) -> p k n", k=src.shape[1])
                    eng.dma_start(dst, src).then_inc(w_landed[b % RAW], 16)
                    issued[0] += 1

            xt = x[0].rearrange("(t p) d -> t p d", p=P)
            eng.dma_start(pl[:, 7, :], lam_re[0].rearrange("(a b) p -> a (b p)", b=2)).then_inc(lam_landed, 16)
            eng.dma_start(pl[:, 8, :], lam_im[0].rearrange("(a b) p -> a (b p)", b=2)).then_inc(lam_landed, 16)
            eng.dma_start(dt2[:], log_dt[0].rearrange("(a b) -> a b", b=2)).then_inc(lam_landed, 16)
            eng.dma_start(h[:, 0, :], xt[0]).then_inc(x_landed[0], 16)
            weights_upto(1)
            for t in range(1, NT):
                eng.dma_start(h[:, t, :], xt[t]).then_inc(x_landed[t], 16)
            weights_upto(2)
            eng.dma_start(bnr[:], b_re[0].rearrange("(a b) p i -> (b p) a i", b=2)).then_inc(b_landed, 16)
            eng.dma_start(bni[:], b_im[0].rearrange("(a b) p i -> (b p) a i", b=2)).then_inc(b_landed, 16)
            for dst, src in ((cdr, c_re), (cdi, c_im)):
                for dup in range(2):
                    eng.dma_start(dst[:, :, dup, :], src[0].rearrange("(t g) j p -> (g j) t p", g=GQ)).then_inc(
                        c_landed, 16)
            eng.dma_start(reltab[:], rel[0]).then_inc(rel_landed, 16)
            eng.dma_start(dd[:].rearrange("i g j -> i (g j)"),
                          d_skip[0].rearrange("g j -> (g j)").partition_broadcast(GI)).then_inc(d_landed, 16)
            eng.dma_start(glub[:], glu_b[0].rearrange("(t p) -> p t", p=P), allow_slow_non_contiguous=True).then_inc(glub_landed, 16)
            weights_upto(5)

            for q in range(AT):
                weights_upto(q + 7)
                sp_.wait_ge(proj_out, q + 1)
                eng.dma_start(u_dram[q], uP[:].rearrange("p s c -> p (s c)")).then_inc(u_stored, 16)
                sp_.wait_ge(u_stored, 16 * (q + 1))
                src = u_dram[q].rearrange("(g i) (s c) -> s i g c", g=GQ, s=L)
                for s in range(L):
                    r = L - 1 - s
                    eng.dma_start(u8[GI * r:GI * (r + 1), q], src[s]).then_inc(u_landed[q], 16)

            def load_bias(hd):
                if hd >= 2:
                    sp_.wait_ge(s_biased, NT * (hd - 1))
                src = bass.AP(rel_dram.tensor, hd * 5 * P, [[1, P], [1, S]])
                eng.dma_start(bias[:, hd % 2, :], src).then_inc(bias_landed[hd % 2], 16)

            def ssm_moves(steps):
                for q, s in steps:
                    if s == 4:
                        sp_.wait_ge(gk_ready, q + 1)
                        if q:
                            sp_.wait_ge(ssm_done, STEPS * q)
                        else:
                            sp_.wait_ge(const_ready, 6)
                        for r in range(L):
                            eng.dma_start(toep[GI * r:GI * (r + 1), :, GI * (L - 1 - r):],
                                          gk[0:GI, :, 0:r + 1, :].rearrange("i g t j -> i g (t j)")).then_inc(
                                              toep_landed, 16)
                    if s == 6:
                        sp_.wait_ge(*ssm_read(q, 5))
                        sp_.wait_ge(*ssm_read(q, 6))
                        eng.dma_start(y_dram[q], y8[:].rearrange("p g c -> p (g c)")).then_inc(y_stored, 16)
                        sp_.wait_ge(y_stored, 16 * (q + 1))
                        src = y_dram[q].rearrange("(t j) (g c) -> g j t c", t=L, g=GQ)
                        for g in range(GQ):
                            eng.dma_start(yT[GI * g:GI * (g + 1), q], src[g]).then_inc(y_landed[q], 16)

            weights_upto(2 * AT + 4)
            sp_.wait_ge(relext_ready, 2)
            eng.dma_start(rel_dram, relext[:]).then_inc(rel_stored, 16)
            sp_.wait_ge(rel_stored, 16)
            sp_.wait_ge(x_ready, NT)
            load_bias(0)
            load_bias(1)
            weights_upto(2 * AT + 8)
            for n in range(TICKS):
                if qk_of(n) is not None:
                    weights_upto(2 * AT + qk_of(n) + 7)
                if n % NT == 1 and 0 < n // NT < A_HEADS - 1:
                    load_bias(n // NT + 1)
                ssm_moves(ssm_steps(n))

            def load_norm(n):
                for i, p in enumerate([(ln_mix_g, ln_mix_b), (ln_ffn_g, ln_ffn_b)][n % 2]):
                    eng.dma_start(lnp[:, i, :], p[n // 2].partition_broadcast(P)).then_inc(lnp_landed, 16)

            weights_upto(GLU + WS + RAW)
            sp_.wait_ge(pv_done, A_HEADS)
            sp_.wait_ge(s_biased, A_HEADS * NT)
            sp_.wait_ge(ssm_done, STEPS * AT)
            sp_.wait_ge(xs_ready, 2 * AT)
            sp_.wait_ge(toep_landed, 16 * L * AT)
            for t in range(NT):
                eng.dma_start(h[:, t, :], xt[t]).then_inc(h_landed, 16)
            load_norm(0)
            weights_upto(FFN[0] + WS)
            for n, upto in ((1, OV + WS), (2, FFN[1] + WS), (3, NBLK)):
                sp_.wait_ge(h_ready, (NT - 1) * n)
                sp_.wait_ge(h_last, n)
                load_norm(n)
                weights_upto(upto)
            ot = out[0].rearrange("(t p) d -> t p d", p=P)
            for t in range(NT):
                if t < NT - 1:
                    sp_.wait_ge(h_ready, 3 * (NT - 1) + t + 1)
                else:
                    sp_.wait_ge(h_last, 4)
                eng.dma_start(ot[t], h[:, t, :]).then_inc(out_stored, 16)
            sp_.wait_ge(out_stored, 16 * NT)

        @block.gpsimd
        def _(pool):
            eng = nc.gpsimd
            eng.memset(ident[:], 0.0).then_inc(const_zero, 1)
            eng.memset(ones[:].bitcast(F32), 1.0).then_inc(const_ready, 1)
            eng.memset(toep[:], 0.0).then_inc(const_ready, 1)
            eng.memset(xsr[:, :, 0:1], 0.0).then_inc(const_ready, 1)
            eng.memset(xsi[:, :, 0:1], 0.0).then_inc(const_ready, 1)
            pool.wait_ge(const_zero, 1)
            eng.affine_select(out=ident[:], in_=ident[:], compare_op=ALU.not_equal, fill=1.0, base=0,
                              pattern=[[-1, P]], channel_multiplier=1).then_inc(const_ready, 1)
            pool.wait_ge(const_ready, 5)
            eng.affine_select(out=tri[:], in_=ones[:].bitcast(F32), compare_op=ALU.is_gt, fill=0.0, base=0,
                              pattern=[[-1, P]], channel_multiplier=1).then_inc(const_ready, 1)
            split = [0]

            def lower_upto(n):
                while split[0] < min(n, NBLK):
                    b = split[0]
                    pool.wait_ge(w_hi, b + 1)
                    eng.tensor_tensor(wlo[:, b % WS, :], raw[:, b % RAW, :], whi[:, b % WS, :].bitcast(F32),
                                      ALU.subtract).then_inc(w_lo, 1)
                    split[0] += 1

            def mask(t, signal):
                for j in range(NT):
                    o = TRI[j]
                    eng.affine_select(out=t[:, o:o + P], in_=t[:, o:o + P], compare_op=ALU.is_gt, fill=0.0,
                                      base=0, pattern=[[1, P]], channel_multiplier=-1).then_inc(signal, 1)

            own = [0]

            def link(ins):
                own[0] += 1
                ins.then_inc(pool_self, 1)
                pool.wait_ge(pool_self, own[0])

            def sum_of_products(o_, a, b, c, d, op, signal, value):
                n = int(np.prod(o_.shape[1:]))
                t0, t1 = (gt[:, k, 0:n].rearrange("p (a b c) -> p a b c", b=o_.shape[2], c=GI) for k in range(2))
                eng.tensor_tensor(t0, a, b, ALU.mult).then_inc(pool_self, 1)
                own[0] += 1
                link(eng.tensor_tensor(t1, c, d, ALU.mult))
                eng.tensor_tensor(o_, t0, t1, op).then_inc(signal, 1)
                pool.wait_ge(signal, value)

            def build_in(q):
                if q:
                    pool.wait_ge(ssm_done, STEPS * (q - 1) + 2)
                pq = slice(q * PQ, (q + 1) * PQ)
                sh = (P, PQ, L, GI)
                b_r = bbr[:, pq].unsqueeze(2).broadcast_to(sh)
                b_i = bbi[:, pq].unsqueeze(2).broadcast_to(sh)
                a_r, a_i = (pw[:, k, pq, 0:L].unsqueeze(3).broadcast_to(sh) for k in range(2))
                sum_of_products(wnr[:], b_r, a_r, b_i, a_i, ALU.subtract, wn_ready, 2 * q + 1)
                sum_of_products(wni[:], b_r, a_i, b_i, a_r, ALU.add, wn_ready, 2 * q + 2)

            def build_out(q):
                if q:
                    pool.wait_ge(ssm_done, STEPS * q)
                pq = slice(q * PQ, (q + 1) * PQ)
                for half in range(2):
                    lo = half * (L // 2)
                    n = L // 2 + half
                    sh = (P, PQ, n, GI)
                    c_r = cr[:, pq].unsqueeze(2).broadcast_to(sh)
                    c_i = nci[:, pq].unsqueeze(2).broadcast_to(sh)
                    a_r, a_i, a_n = (pw[:, k, pq, lo:lo + n].unsqueeze(3).broadcast_to(sh) for k in range(3))
                    sum_of_products(cxr[:, :, lo:lo + n], c_r, a_r, c_i, a_i, ALU.add, cx_ready,
                                    4 * q + 2 * half + 1)
                    sum_of_products(cxi[:, :, lo:lo + n], c_r, a_n, c_i, a_r, ALU.add, cx_ready,
                                    4 * q + 2 * half + 2)

            lower_upto(2 * AT + 2)
            pool.wait_ge(tables_ready, 1)
            build_in(0)
            lower_upto(2 * AT + 3)
            build_out(0)
            lower_upto(2 * AT + 6)
            for n in range(TICKS):
                if n % STEPS == 2 and n // STEPS + 1 < AT:
                    build_in(n // STEPS + 1)
                if n and n % STEPS == 0 and n // STEPS < AT:
                    build_out(n // STEPS)
                if qk_of(n) is not None:
                    lower_upto(2 * AT + qk_of(n) + 5)

            def norm(n, f):
                lower_upto(f + 1)
                for t in range(NT - 1):
                    if t == NT - 2:
                        lower_upto(f + 2)
                    pool.wait_ge(scaled, (NT - 1) * n + t + 1)
                    if t == 0:
                        pool.wait_ge(lnp_landed, 32 * (n + 1))
                    eng.tensor_tensor(h[:, t, :], h[:, t, :], lnp[:, 1, :], ALU.add).then_inc(h_ready, 1)

            norm(0, FFN[0])
            norm(1, OV)
            lower_upto(OQK + LEAD + 4)
            for hd in range(C_HEADS + 1):
                if hd < C_HEADS:
                    pool.wait_ge(sp_raw, hd + 1)
                    mask(sp, sp_masked)
                if hd:
                    pool.wait_ge(w_exp, hd)
                    mask(wt[:, (hd - 1) % 3], w_ready)
                lower_upto(min(OQK + LEAD + WS + hd, OOUT + TAIL))
            norm(2, FFN[1])
            norm(3, NBLK)

        @block.scalar
        def _(act):
            eng = nc.scalar
            rounded = [0]
            own = [0]

            def upper_upto(n):
                while rounded[0] <= min(n, NBLK - 1):
                    b = rounded[0]
                    act.wait_ge(w_landed[b % RAW], 16 * (b // RAW + 1))
                    if b >= WS:
                        act.wait_ge(w_used, b - WS + 1)
                    eng.copy(whi[:, b % WS, :], raw[:, b % RAW, :]).then_inc(w_hi, 1)
                    rounded[0] += 1

            def link(ins):
                own[0] += 1
                ins.then_inc(act_self, 1)
                act.wait_ge(act_self, own[0])

            def upper_x(n, t):
                act.wait_ge(turned, NT * n + t + 1)
                eng.copy(xhi[:, :, t * P:(t + 1) * P],
                         psf[:, 2 * t * S:2 * (t + 1) * S].rearrange("p (k n) -> p k n", k=KT)).then_inc(x_hi, 1)

            act.wait_ge(lam_landed, 48)
            eng.activation(dt2[:], dt2[:], ACT.Exp).then_inc(dt_ready, 1)
            for t in range(NT):
                upper_x(0, t)
            upper_upto(1)
            act.wait_ge(m_ready, 1)
            eng.activation(pl[:, 10, :], pl[:, 9, :], ACT.Exp).then_inc(mag_ready, 1)
            upper_upto(3)
            act.wait_ge(arg_ready, 1)
            eng.activation(pl[:, 6, :], pl[:, 12, :], ACT.Sin).then_inc(trig_ready, 1)
            eng.activation(pl[:, 5, :], pl[:, 13, :], ACT.Sin).then_inc(trig_ready, 1)

            def project_out(n, dst, scale=None):
                act.wait_ge(w_used, (n if n < AT else n + 4) + 1)
                src = ps[:, 4 + n % 2 if n < AT else 6 if n == AT + 1 else 4, :]
                if dst is None:
                    q = n
                    if q:
                        act.wait_ge(u_stored, 16 * q)
                    ins = eng.copy(uP[:].rearrange("p s c -> p c s"), src.rearrange("p (c s) -> p c s", s=L))
                elif scale:
                    ins = eng.mul(dst, src.rearrange("p (t n) -> p t n", n=P), scale)
                else:
                    ins = eng.copy(dst, src)
                ins.then_inc(proj_out, 1)

            for q in range(AT):
                upper_upto(q + 4)
                project_out(q, None)
            upper_upto(8)
            act.wait_ge(c_turned, 1)
            for b in range(4):
                upper_upto(8 + b)
            act.wait_ge(w_used, 2 * AT)
            for t in range(NT):
                eng.copy(v[:, t, :], ps[:, t, :]).then_inc(v_out, 1)

            def ssm_outs(steps):
                for q, s in steps:
                    k = STEPS * q + s
                    bank = ps[:, SSM_BANK[k % 2], :]
                    if s in (0, 1):
                        act.wait_ge(ssm_done, k + 1)
                        eng.copy((winr, wini)[s][:].rearrange("p a n -> p (a n)"), bank).then_inc(ssm_out[k % 2], 1)
                    if s in (5, 6):
                        act.wait_ge(ssm_done, k + 1)
                        if q:
                            act.wait_ge(y_stored, 16 * q)
                        eng.copy(y8[:].rearrange("p (a b) c -> p a b c", b=2)[:, :, s - 5, :],
                                 bank[:, 0:PQ * NC].rearrange("p (a c) -> p a c", c=NC)).then_inc(ssm_out[k % 2], 1)

            def qk_out(n):
                if n % 2 == 0:
                    project_out(AT + n, qT[:, n // 2, :].rearrange("p (t n) -> p t n", n=P)[:, :, ::-1], QSCALE)
                else:
                    project_out(AT + n, kT[:, n // 2, :])

            act.wait_ge(pl_turned, 1)
            act.wait_ge(rel_stored, 16)
            act.wait_ge(par_out, 1)
            for n in range(2):
                upper_upto(2 * AT + n + 4)
                qk_out(n)

            def softmax_exp(n):
                w = (ITEMS[n][1] + 1) * P
                act.wait_ge(s_negmax, n + 1)
                eng.activation(sc[:, n % 3, 0:w], sc[:, n % 3, 0:w], ACT.Exp, bias=sm[:, n % 3, 1:2],
                               accum_out=sm[:, n % 3, 2:3]).then_inc(s_exp, 1)

            def turned_out(n):
                hd, i = ITEMS[n]
                act.wait_ge(pt_done, n + 1)
                if hd and i == 0:
                    act.wait_ge(pv_done, hd)
                eng.copy(pt[:, 0:i + 1, i * P:(i + 1) * P],
                         ps[:, 2 + n % 2, 0:(i + 1) * P].rearrange("p (j n) -> p j n", n=P)[:, :, ::-1]).then_inc(
                             pt_out, 1)

            def pair_keep(j):
                act.wait_ge(pv_done, 2 * j + 2)
                eng.copy(kept[:, j, :], ps[:, 6, :]).then_inc(ao_kept, 1)

            def pair_upper(j):
                if j < 2:
                    act.wait_ge(ao_kept, j + 1)
                else:
                    act.wait_ge(pv_done, 2 * j + 2)
                act.wait_ge(w_used, GLU)
                eng.copy(xhi[:, j, :], kept[:, j, :] if j < 2 else ps[:, 6, :]).then_inc(ao_hi, 1)

            upper_upto(2 * AT + 6)
            for n in range(TICKS):
                if n < len(ITEMS):
                    softmax_exp(n)
                if 0 <= n - 2 < len(ITEMS):
                    turned_out(n - 2)
                ssm_outs(ssm_steps(n))
                if qk_of(n) is not None:
                    qk_out(qk_of(n))
                    upper_upto(2 * AT + qk_of(n) + 5)
                if n in (10, 18):
                    pair_keep((n - 10) // 8)
                if n in (X_USED, X_USED + 1):
                    pair_upper(n - X_USED)
                if n in (26, 34):
                    pair_upper((n - 10) // 8)

            for q in range(AT):
                act.wait_ge(y_landed[q], 16 * GQ)
                eng.activation(yT[:, q], yT[:, q], ACT.Gelu_apprx_tanh).then_inc(y_gelu, 1)
            for q in range(AT):
                act.wait_ge(y_gelu, q + 1)
                if q == 0:
                    act.wait_ge(pv_done, A_HEADS)
                eng.copy(yhi[:, q, :], yT[:, q].rearrange("p t c -> p (t c)")).then_inc(y_hi, 1)
            act.wait_ge(glub_landed, 16)
            for m in range(AT):
                if m % 2:
                    act.wait_ge(w_used, GLU + m // 2 + 1)
                else:
                    act.wait_ge(glu_done, m // 2 + 1)
                if m >= 2:
                    act.wait_ge(ob_ready, m - 1)
                eng.activation(sg[:, m % 2, :], ps[:, 4 + m % 2, :], ACT.Sigmoid,
                               bias=glub[:, m:m + 1]).then_inc(glu_sig, 1)
                act.wait_ge(ob_ready, m + 1)
                eng.copy(xhi[:, AT + m, :].rearrange("p (c t) -> p c t", t=L),
                         gt[:, m % 2, :].rearrange("p (t c) -> p c t", t=L)).then_inc(ob_hi, 1)

            def norm(n, f):
                def std(t):
                    act.wait_ge(var_ready, NT * n + t + 1)
                    eng.activation(lns[:, t, 1:2], lns[:, t, 0:1], ACT.Sqrt).then_inc(std_ready, 1)

                for t in range(NT - 1):
                    if n < 3 and t == 2:
                        upper_x(n + 1, 0)
                        upper_x(n + 1, 1)
                    std(t)
                    act.wait_ge(rstd_ready, (NT - 1) * n + t + 1)
                    eng.mul(h[:, t, :], h[:, t, :], lns[:, t, 2:3]).then_inc(scaled, 1)
                upper_upto(f + 3)
                std(NT - 1)
                if n < 3:
                    upper_upto(f + 4)
                    upper_x(n + 1, 2)
                    upper_x(n + 1, 3)

            def product(first, nk):
                for k in range(nk):
                    upper_upto(first + k)

            def ffn(layer):
                f = FFN[layer]
                for m in range(FT):
                    upper_upto(f + 2 * m + 4)
                    c = layer * FT + m
                    act.wait_ge(w_used, f + 2 * m + 1)
                    if m >= 2:
                        act.wait_ge(g_ready, c - 1)
                    eng.activation(sg[:, m % 2, :], ps[:, 2 * (m % 2), :], ACT.Silu).then_inc(silu_ready, 1)
                    upper_upto(f + 2 * m + 5)
                    act.wait_ge(g_ready, c + 1)
                    eng.copy(ghi[:, m, :], gt[:, m % 2, :]).then_inc(g_hi, 1)
                product(f + 2 * FT, FT)

            product(EOUT, KT)
            upper_upto(FFN[0])
            norm(0, FFN[0])
            ffn(0)
            upper_upto(OV)
            norm(1, OV)
            product(OV, KT)
            upper_upto(OQK + 3)
            act.wait_ge(w_used, OV + KT)
            for t in range(NT):
                eng.copy(ov[:, t, :], psf[:, 2 * t * S:2 * (t + 1) * S]).then_inc(ov_out, 1)

            def stick_logs(hd):
                act.wait_ge(z_done, hd + 1)
                if hd:
                    act.wait_ge(z_read, hd)
                link(eng.activation(lg[:], psf[:, 0:TRI_W], ACT.Abs))
                link(eng.activation(lg[:], lg[:], ACT.Exp, scale=-1.0))
                eng.activation(lg[:], lg[:], ACT.Ln, bias=1.0).then_inc(l_ready, 1)

            def stick_upper(hd):
                act.wait_ge(sp_masked, NT * (hd + 1))
                if hd:
                    act.wait_ge(r_done, hd)
                eng.copy(sphi[:], sp[:]).then_inc(sp_hi, 1)

            def stick_exp(hd):
                act.wait_ge(lw_ready, hd + 1)
                eng.activation(wt[:, hd % 3], wt[:, hd % 3], ACT.Exp).then_inc(w_exp, 1)

            def oqk_outs(n):
                act.wait_ge(w_used, OQK + n + 1)
                if n >= 4 and n % 2 == 0:
                    act.wait_ge(z_done, n - 2)
                hi = oqk_hi[:, n // 2 % 2, n % 2, :]
                if n % 2 == 0:
                    eng.mul(hi, ps[:, 6, :], QSCALE).then_inc(qk_hi, 1)
                else:
                    eng.copy(hi, ps[:, 6, :]).then_inc(qk_hi, 1)

            def pair_out(j):
                act.wait_ge(opv_done, 2 * j + 2)
                eng.copy(oatt[:, j, :], ps[:, 7, :]).then_inc(o_out, 1)

            def mix_upper(j):
                act.wait_ge(o_out, j + 1)
                eng.copy(xhi[:, j, :], oatt[:, j, :]).then_inc(omix_hi, 1)

            eng.preload_act_table_set("natural_log_exp_and_others")
            for n in range(LEAD):
                upper_upto(OQK + n + 4)
                oqk_outs(n)
            stick_logs(0)
            upper_upto(OQK + LEAD + 4)
            stick_upper(0)
            oqk_outs(LEAD)
            for hd in range(C_HEADS):
                if hd + 1 < C_HEADS:
                    stick_logs(hd + 1)
                stick_exp(hd)
                upper_upto(min(OQK + LEAD + hd + 5, OOUT + 3))
                if hd and hd % 2 == 0:
                    pair_out(hd // 2 - 1)
                if hd + 1 < C_HEADS:
                    stick_upper(hd + 1)
                if hd + 1 + LEAD < 2 * KT:
                    oqk_outs(hd + 1 + LEAD)
            for j in range(KT - 1):
                mix_upper(j)
            pair_out(KT - 1)
            mix_upper(KT - 1)
            upper_upto(OOUT + 2)
            product(OOUT, KT)
            upper_upto(FFN[1])
            norm(2, FFN[1])
            ffn(1)
            norm(3, NBLK)

        @block.vector
        def _(dve):
            eng = nc.vector
            own = [0]

            def count(ins):
                own[0] += 1
                ins.then_inc(dve_self, 1)

            def settle():
                dve.wait_ge(dve_self, own[0])

            def link(ins):
                count(ins)
                settle()

            def tt(o_, a, b, op):
                return eng.tensor_tensor(o_, a, b, op)

            def lower_x(n, t):
                dve.wait_ge(x_hi, NT * n + t + 1)
                cols = slice(t * P, (t + 1) * P)
                tt(xlo[:, :, cols], psf[:, 2 * t * S:2 * (t + 1) * S].rearrange("p (k n) -> p k n", k=KT),
                   xhi[:, :, cols].bitcast(F32), ALU.subtract).then_inc(x_ready, 1)

            def products4(a_r, a_i, b_r, b_i, n, shape):
                v4 = [t[:, 0:n] if len(shape) == 1 else
                      t[:, 0:n].rearrange("p (a b) -> p a b", b=shape[-1]) if len(shape) == 2 else
                      t[:, 0:n].rearrange("p (a b c) -> p a b c", b=shape[-2], c=shape[-1]) for t in t4]
                for o_, (a, b) in zip(v4, ((a_r, b_r), (a_i, b_i), (a_r, b_i), (a_i, b_r))):
                    count(tt(o_, a, b, ALU.mult))
                settle()
                return v4

            def cmul(o_r, o_i, a_r, a_i, b_r, b_i, n, shape):
                v4 = products4(a_r, a_i, b_r, b_i, n, shape)
                count(tt(o_r, v4[0], v4[1], ALU.subtract))
                count(tt(o_i, v4[2], v4[3], ALU.add))
                settle()

            AR, AI, FR, FI, M8, CS, SN, LR, LI, M, MAG, TH, RS, RC, A, B, C_, D_ = range(18)
            dve.wait_ge(lam_landed, 48)
            dve.wait_ge(dt_ready, 1)
            dtb = dt2[:].unsqueeze(2).broadcast_to((PAIRS, 2, PS))

            def q_(i):
                return pl[:, i, :]

            def q2(i):
                return pl[:, i, :].rearrange("a (b p) -> a b p", b=2)

            tt(q2(M), q2(LR), dtb, ALU.mult).then_inc(m_ready, 1)
            link(tt(q2(TH), q2(LI), dtb, ALU.mult))
            link(eng.tensor_scalar(q_(A), q_(TH), 1 / (2 * math.pi), ROUNDER, ALU.mult, ALU.add))
            link(eng.tensor_scalar(q_(A), q_(A), ROUNDER, None, ALU.subtract))
            for part in (TWO_PI_1, TWO_PI_2, TWO_PI_3):
                link(eng.scalar_tensor_tensor(out=q_(TH), in0=q_(A), scalar=-part, in1=q_(TH),
                                              op0=ALU.mult, op1=ALU.add))
            link(eng.tensor_scalar(q_(RS), q_(TH), PI_BELOW, -PI_BELOW, ALU.min, ALU.max))
            link(eng.tensor_scalar(q_(RC), q_(RS), -1.0, None, ALU.mult))
            link(tt(q_(RC), q_(RC), q_(RS), ALU.min))
            eng.tensor_scalar(q_(RC), q_(RC), math.pi / 2, None, ALU.add).then_inc(arg_ready, 1)
            for t in range(NT):
                lower_x(0, t)
            dve.wait_ge(mag_ready, 1)
            dve.wait_ge(trig_ready, 2)
            count(tt(q_(AR), q_(MAG), q_(CS), ALU.mult))
            count(tt(q_(AI), q_(MAG), q_(SN), ALU.mult))
            count(tt(q_(A), q_(LR), q_(LR), ALU.mult))
            count(tt(q_(B), q_(LI), q_(LI), ALU.mult))
            count(tt(q_(M8), q_(MAG), q_(MAG), ALU.mult))
            settle()
            count(tt(q_(A), q_(A), q_(B), ALU.add))
            count(eng.tensor_scalar(q_(C_), q_(AR), 1.0, None, ALU.subtract))
            count(tt(q_(D_), q_(M8), q_(M8), ALU.mult))
            settle()
            count(eng.reciprocal(q_(A), q_(A)))
            count(tt(q_(M8), q_(D_), q_(D_), ALU.mult))
            count(tt(q_(FR), q_(C_), q_(LR), ALU.mult))
            count(tt(q_(B), q_(AI), q_(LI), ALU.mult))
            count(tt(q_(FI), q_(AI), q_(LR), ALU.mult))
            count(tt(q_(TH), q_(C_), q_(LI), ALU.mult))
            settle()
            count(tt(q_(FR), q_(FR), q_(B), ALU.add))
            count(tt(q_(FI), q_(FI), q_(TH), ALU.subtract))
            settle()
            count(tt(q_(FR), q_(FR), q_(A), ALU.mult))
            count(tt(q_(FI), q_(FI), q_(A), ALU.mult))
            settle()
            eng.engine_nop().then_inc(pl_ready, 1)

            dve.wait_ge(rel_landed, 16)
            eng.tensor_copy(relext[:, 0:S - P], reltab[:, NREL - 1:NREL].broadcast_to((A_HEADS, S - P))).then_inc(
                relext_ready, 1)
            eng.tensor_copy(relext[:, S - P:5 * P], reltab[:, 2 * MAX_REL - 1::-1]
                            ).then_inc(relext_ready, 1)

            dve.wait_ge(d_landed, 16)
            dve.wait_ge(const_ready, 5)
            link(tt(dd[:], dd[:], ident[0:GI, 0:GI].unsqueeze(1).broadcast_to((GI, G, GI)), ALU.mult))

            dve.wait_ge(pl_turned, 1)
            eng.tensor_copy(par[:].rearrange("p a b -> p (a b)"), ps[:, 6, 0:7 * PAIRS]).then_inc(par_read, 1)
            dve.wait_ge(par_read, 1)
            dve.wait_ge(c_turned, 1)
            cre = ps[:, 7, :].rearrange("p (a b j) -> p a b j", b=2, j=GI)
            cim = ps[:, 0, :].rearrange("p (a b j) -> p a b j", b=2, j=GI)
            for b in range(2):
                rows = slice(b * PS, (b + 1) * PS)
                count(eng.tensor_copy(cr[rows], cre[rows, :, b, :]))
                count(eng.tensor_scalar(nci[rows], cim[rows, :, b, :], -1.0, None, ALU.mult))
            settle()
            eng.engine_nop().then_inc(par_out, 1)

            def wide(i, n):
                return par[:, i, :].unsqueeze(2).broadcast_to((P, PAIRS, n))

            dve.wait_ge(b_landed, 32)
            cmul(bbr[:], bbi[:], bnr[:], bni[:], wide(FR, GI), wide(FI, GI), PAIRS * GI, (PAIRS, GI))
            pr, pi, npi = pw[:, 0], pw[:, 1], pw[:, 2]
            count(eng.memset(pw[:, 0, :, 0:1], 1.0))
            count(eng.memset(pw[:, 1, :, 0:1], 0.0))
            count(eng.tensor_copy(pw[:, 0:2, :, 1], par[:, 0:2, :]))
            settle()
            n = 1
            while n < L:
                by_r = pw[:, 0, :, n:n + 1].broadcast_to((P, PAIRS, n))
                by_i = pw[:, 1, :, n:n + 1].broadcast_to((P, PAIRS, n))
                cmul(pw[:, 0, :, n + 1:2 * n + 1], pw[:, 1, :, n + 1:2 * n + 1], pw[:, 0, :, 1:n + 1],
                     pw[:, 1, :, 1:n + 1], by_r, by_i, PAIRS * n, (PAIRS, n))
                n *= 2
            link(eng.tensor_scalar(pw[:, 2], pw[:, 1], -1.0, None, ALU.mult))
            eng.engine_nop().then_inc(tables_ready, 1)
            a = (par[:, CS, :], par[:, SN, :])
            for k in range(int(math.log2(L))):
                b = (ph[:, k % 2, 0, :], ph[:, k % 2, 1, :])
                cmul(*b, *a, *a, PAIRS, (PAIRS,))
                a = b
            count(eng.memset(phr[:, :, 0:1], 1.0))
            count(eng.memset(phi[:, :, 0:1], 0.0))
            count(eng.tensor_copy(phr[:, :, 1], a[0]))
            count(eng.tensor_copy(phi[:, :, 1], a[1]))
            settle()
            n, k = 2, int(math.log2(L))
            while n < NC:
                b = (ph[:, k % 2, 0, :], ph[:, k % 2, 1, :])
                cmul(*b, *a, *a, PAIRS, (PAIRS,))
                a = b
                for lo in range(0, n, 16):
                    w = min(n, 16)
                    cmul(phr[:, :, n + lo:n + lo + w], phi[:, :, n + lo:n + lo + w], phr[:, :, lo:lo + w],
                         phi[:, :, lo:lo + w], a[0].unsqueeze(2).broadcast_to((P, PAIRS, w)),
                         a[1].unsqueeze(2).broadcast_to((P, PAIRS, w)), PAIRS * w, (PAIRS, w))
                n, k = 2 * n, k + 1
            link(eng.memset(decay[:], 0.0))

            def rotate(q, part):
                pq = slice(q * PQ, (q + 1) * PQ)
                fr_, fi_ = phr[:, pq], phi[:, pq]
                k = STEPS * q + 2

                def flat(t):
                    return t[:].rearrange("p a c -> p (a c)")

                if part == 0:
                    count(eng.tensor_copy(decay[:, :, 1:], par[:, M8, pq].unsqueeze(2).broadcast_to((P, PQ, NC - 1))))
                    bank = ps[:, SSM_BANK[k % 2], :]
                    sr = bank[:, 0:PQ * NC].rearrange("p (a c) -> p a c", c=NC)
                    si = bank[:, PQ * NC:2 * PQ * NC].rearrange("p (a c) -> p a c", c=NC)
                    dve.wait_ge(ssm_done, k + 1)
                    v4 = products4(sr, si, fr_, fi_, PQ * NC, (PQ, NC))
                    count(tt(zin_r[:], v4[0], v4[1], ALU.add))
                    tt(zin_i[:], v4[3], v4[2], ALU.subtract).then_inc(ssm_out[k % 2], 1)
                if part == 1:
                    dve.wait_ge(*ssm_read(q, 2))
                    settle()
                    count(eng.tensor_tensor_scan(flat(zr), flat(decay), flat(zin_r), 0.0, ALU.mult, ALU.add))
                    count(eng.tensor_tensor_scan(flat(zi), flat(decay), flat(zin_i), 0.0, ALU.mult, ALU.add))
                if part == 2:
                    settle()
                    v4 = products4(zr[:], zi[:], fr_, fi_, PQ * NC, (PQ, NC))
                    tt(xsr[:, :, 1:], v4[0], v4[1], ALU.subtract).then_inc(xs_ready, 1)
                    tt(xsi[:, :, 1:], v4[2], v4[3], ALU.add).then_inc(xs_ready, 1)

            def ssm_vector(n):
                for q, s in ssm_steps(n):
                    k = STEPS * q + s
                    if s in (3, 4):
                        dve.wait_ge(ssm_done, k + 1)
                        if q and s == 3:
                            dve.wait_ge(toep_landed, 16 * L * q)
                        eng.tensor_copy(gk[0:GI].rearrange("i (a b) t j -> i a b (t j)", b=2)[:, :, s - 3, :],
                                        ps[0:GI, SSM_BANK[k % 2], :].rearrange("i (a n) -> i a n", n=P)).then_inc(
                                            ssm_out[k % 2], 1)
                        dve.wait_ge(*ssm_read(q, s))
                    if s == 4:
                        tt(gk[0:GI, :, 0, :], gk[0:GI, :, 0, :], dd[:, q * GQ:(q + 1) * GQ, :],
                           ALU.add).then_inc(gk_ready, 1)
                    if s in (2, 3, 4):
                        rotate(q, s - 2)

            dve.wait_ge(const_ready, 5)

            def biased(n):
                hd, i = ITEMS[n]
                w = (i + 1) * P
                if i == 0:
                    dve.wait_ge(bias_landed[hd % 2], 16 * (hd // 2 + 1))
                    link(eng.memset(bias[P - CHUNK:P, hd % 2, S - CHUNK:S], MASKED))
                dve.wait_ge(s_done, n + 1)
                if n >= 3:
                    dve.wait_ge(pt_done, n - 2)
                eng.tensor_tensor_reduce(sc[:, n % 3, 0:w], ps[:, n % 2, 0:w], bias[:, hd % 2, S - w:S], 1.0, -3e38,
                                         ALU.add, ALU.max, sm[:, n % 3, 0:1]).then_inc(s_biased, 1)
                dve.wait_ge(s_biased, n + 1)
                eng.tensor_scalar(sm[:, n % 3, 1:2], sm[:, n % 3, 0:1], -1.0, None, ALU.mult).then_inc(s_negmax, 1)

            def normalised(n):
                w = (ITEMS[n][1] + 1) * P
                dve.wait_ge(s_exp, n + 1)
                link(eng.reciprocal(sm[:, n % 3, 3:4], sm[:, n % 3, 2:3]))
                eng.tensor_scalar(sc[:, n % 3, 0:w], sc[:, n % 3, 0:w], sm[:, n % 3, 3:4], None,
                                  ALU.mult).then_inc(p_ready, 1)

            def pair_lower(j):
                dve.wait_ge(ao_hi, j + 1)
                tt(xlo[:, j, :], kept[:, j, :] if j < 2 else ps[:, 6, :], xhi[:, j, :].bitcast(F32), ALU.subtract).then_inc(ao_out, 1)

            for n in range(TICKS):
                if n < len(ITEMS):
                    biased(n)
                if 0 <= n - 1 < len(ITEMS):
                    normalised(n - 1)
                ssm_vector(n)
                if X_USED < n <= X_USED + 3:
                    pair_lower(n - X_USED - 1)
            pair_lower(A_HEADS // 2 - 1)

            for q in range(AT):
                dve.wait_ge(y_hi, q + 1)
                tt(ylo[:, q, :], yT[:, q].rearrange("p t c -> p (t c)"), yhi[:, q, :].bitcast(F32),
                   ALU.subtract).then_inc(y_ready, 1)
            for m in range(AT):
                dve.wait_ge(glu_sig, m + 1)
                tt(gt[:, m % 2, :], yT[:, m].rearrange("p t c -> p (t c)"), sg[:, m % 2, :],
                   ALU.mult).then_inc(ob_ready, 1)
                dve.wait_ge(ob_hi, m + 1)
                tt(xlo[:, AT + m, :].rearrange("p (c t) -> p c t", t=L),
                   gt[:, m % 2, :].rearrange("p (t c) -> p c t", t=L),
                   xhi[:, AT + m, :].rearrange("p (c t) -> p c t", t=L).bitcast(F32), ALU.subtract).then_inc(mix_b, 1)

            def norm(n):
                dve.wait_ge(lnp_landed, 32 * (n + 1))

                def statistics(t):
                    if t < NT - 1:
                        dve.wait_ge(acc_done, (NT - 1) * n + t + 1)
                    else:
                        dve.wait_ge(w_used, (EOUT + KT, FFN[0] + 3 * FT, OOUT + KT, FFN[1] + 3 * FT)[n])
                    link(eng.scalar_tensor_tensor(out=h[:, t, :], in0=h[:, t, :], scalar=ALPHA,
                                                  in1=psf[:, 2 * t * S:2 * (t + 1) * S], op0=ALU.mult, op1=ALU.add))
                    for c in range(2):
                        count(eng.bn_stats(stats[:, t, c, :], h[:, t, c * S:(c + 1) * S]))
                    settle()
                    link(eng.bn_aggr(mv[:, t, :], stats[:, t].rearrange("p a b -> p (a b)")))
                    eng.tensor_scalar(lns[:, t, 0:1], mv[:, t, 1:2], EPS, None, ALU.add).then_inc(var_ready, 1)

                def centre(t):
                    link(eng.scalar_tensor_tensor(out=h[:, t, :], in0=h[:, t, :], scalar=mv[:, t, 0:1],
                                                  in1=lnp[:, 0, :], op0=ALU.subtract, op1=ALU.mult))
                    dve.wait_ge(std_ready, NT * n + t + 1)
                    if t < NT - 1:
                        eng.reciprocal(lns[:, t, 2:3], lns[:, t, 1:2]).then_inc(rstd_ready, 1)
                    else:
                        link(eng.reciprocal(lns[:, t, 2:3], lns[:, t, 1:2]))
                        eng.scalar_tensor_tensor(out=h[:, t, :], in0=h[:, t, :], scalar=lns[:, t, 2:3],
                                                 in1=lnp[:, 1, :], op0=ALU.mult, op1=ALU.add).then_inc(h_last, 1)

                for t in range(NT):
                    statistics(t)
                    centre(t)
                    if n < 3 and 1 <= t <= 2:
                        lower_x(n + 1, t - 1)
                if n < 3:
                    lower_x(n + 1, 2)
                    lower_x(n + 1, 3)

            def ffn(layer):
                for m in range(FT):
                    c = layer * FT + m
                    dve.wait_ge(silu_ready, c + 1)
                    dve.wait_ge(w_used, FFN[layer] + 2 * m + 2)
                    if m >= 2:
                        dve.wait_ge(g_lo, c - 1)
                    tt(gt[:, m % 2, :], ps[:, 2 * (m % 2) + 1, :], sg[:, m % 2, :], ALU.mult).then_inc(g_ready, 1)
                    dve.wait_ge(g_hi, c + 1)
                    tt(glo[:, m, :], gt[:, m % 2, :], ghi[:, m, :].bitcast(F32), ALU.subtract).then_inc(g_lo, 1)

            dve.wait_ge(h_landed, 16 * NT)
            norm(0)
            ffn(0)
            norm(1)

            def stick_plus(hd):
                dve.wait_ge(l_ready, hd + 1)
                if hd:
                    dve.wait_ge(sp_lo, hd)
                eng.scalar_tensor_tensor(out=sp[:], in0=psf[:, 0:TRI_W], scalar=0.0, in1=lg[:], op0=ALU.max,
                                         op1=ALU.add).then_inc(sp_raw, 1)
                if hd >= 3:
                    dve.wait_ge(opv_done, hd - 2)
                eng.scalar_tensor_tensor(out=wt[:, hd % 3], in0=psf[:, 0:TRI_W], scalar=0.0, in1=lg[:],
                                         op0=ALU.min, op1=ALU.subtract).then_inc(z_read, 1)

            def stick_lower(hd):
                dve.wait_ge(sp_hi, hd + 1)
                tt(splo[:], sp[:], sphi[:].bitcast(F32), ALU.subtract).then_inc(sp_lo, 1)

            def stick_weight(hd):
                dve.wait_ge(r_done, hd + 1)
                dve.wait_ge(z_read, hd + 1)
                tt(wt[:, hd % 3], wt[:, hd % 3], psf[:, 3 * S:3 * S + TRI_W], ALU.subtract).then_inc(lw_ready, 1)

            def qk_lower(n):
                dve.wait_ge(qk_hi, n + 1)
                hi = oqk_hi[:, n // 2 % 2, n % 2, :].bitcast(F32)
                lo = oqk_lo[:, n // 2 % 2, n % 2, :]
                eng.scalar_tensor_tensor(out=lo, in0=ps[:, 6, :], scalar=QSCALE if n % 2 == 0 else 1.0, in1=hi,
                                         op0=ALU.mult, op1=ALU.subtract).then_inc(qk_out, 1)

            for n in range(LEAD):
                qk_lower(n)
            stick_plus(0)
            stick_lower(0)
            qk_lower(LEAD)
            for hd in range(C_HEADS):
                stick_weight(hd)
                if hd + 1 < C_HEADS:
                    stick_plus(hd + 1)
                    stick_lower(hd + 1)
                if hd + 1 + LEAD < 2 * KT:
                    qk_lower(hd + 1 + LEAD)
            for j in range(KT):
                dve.wait_ge(omix_hi, j + 1)
                tt(xlo[:, j, :], oatt[:, j, :], xhi[:, j, :].bitcast(F32), ALU.subtract).then_inc(omix, 1)
            norm(2)
            ffn(1)
            norm(3)

        @block.tensor
        def _(pe):
            eng = nc.tensor

            def three(o_, w_hi_, w_lo_, x_hi_, x_lo_, start, stop):
                eng.matmul(o_, w_hi_, x_hi_, start=start, stop=False)
                eng.matmul(o_, w_hi_, x_lo_, start=False, stop=False)
                return eng.matmul(o_, w_lo_, x_hi_, start=False, stop=stop)

            def feature_major(b, o_, hi, lo, nk=KT, col=0, cols=P):
                pe.wait_ge(w_lo, b + 1)
                wh = whi[:, b % WS, :].rearrange("p (k n) -> p k n", k=nk)
                wl = wlo[:, b % WS, :].rearrange("p (k n) -> p k n", k=nk)
                c = slice(col, col + P)
                for k in range(nk):
                    mm = three(o_, wh[:, k, c], wl[:, k, c], hi[:, k, :], lo[:, k, :], k == 0, k == nk - 1)
                return mm

            def token_rows(b, k, r, width, hi, lo, t, bank, n_half, start, stop):
                c = slice(t * P, (t + 1) * P)
                for half in range(n_half):
                    w = slice(r * width + half * S, r * width + half * S + S)
                    o_ = ps[:, bank + half, :]
                    eng.matmul(o_, hi[:, k, c], whi[:, b % WS, w], start=start, stop=False)
                    eng.matmul(o_, hi[:, k, c], wlo[:, b % WS, w], start=False, stop=False)
                    mm = eng.matmul(o_, lo[:, k, c], whi[:, b % WS, w], start=False, stop=stop)
                return mm

            def turn(n, t):
                for k in range(KT):
                    mm = eng.transpose(psf[:, 2 * t * S + k * P:2 * t * S + (k + 1) * P],
                                       h[:, t, k * P:(k + 1) * P], ident[:])
                mm.then_inc(turned, 1)

            def turn_normed(n, t):
                if t < NT - 1:
                    pe.wait_ge(h_ready, (NT - 1) * (n - 1) + t + 1)
                else:
                    pe.wait_ge(h_last, n)
                turn(n, t)

            def token_major(first, nk, hi, lo, norm_n, ready=None, order=(0, 1, 2, 3), before=None):
                for k in range(nk - TAIL):
                    pe.wait_ge(w_lo, first + k + 1)
                    if ready:
                        ready(k)
                    for t in order:
                        if k == 0 and before:
                            before(t)
                        mm = token_rows(first + k, k, 0, D, hi, lo, t, 2 * t, 2, k == 0, False)
                    mm.then_inc(w_used, 1)
                for t in range(NT):
                    for k in range(nk - TAIL, nk):
                        if t == 0:
                            pe.wait_ge(w_lo, first + k + 1)
                            if ready:
                                ready(k)
                        mm = token_rows(first + k, k, 0, D, hi, lo, t, 2 * t, 2, False, k == nk - 1)
                        if t == NT - 1 and k < nk - 1:
                            mm.then_inc(w_used, 1)
                        if t >= 2 and k == nk - TAIL + 1 and norm_n < 3:
                            turn_normed(norm_n + 1, t - 2)
                    if t < NT - 1:
                        mm.then_inc(acc_done, 1)
                mm.then_inc(w_used, 1)
                return mm

            pe.wait_ge(const_ready, 5)
            for t in range(NT):
                pe.wait_ge(x_landed[t], 16)
                turn(0, t)
            pe.wait_ge(x_ready, NT)

            def project(n, b):
                if n >= 2:
                    pe.wait_ge(proj_out, n - 1)
                mm = feature_major(b, ps[:, 4 + n % 2, :], xhi, xlo)
                mm.then_inc(w_used, 1)

            project(0, 0)
            pe.wait_ge(pl_ready, 1)
            for i in range(7):
                mm = eng.transpose(ps[:, 6, i * PAIRS:(i + 1) * PAIRS], pl[:, i, :], ident[0:PAIRS, 0:PAIRS])
            mm.then_inc(pl_turned, 1)
            project(1, 1)
            pe.wait_ge(c_landed, 64)
            for src, bank in ((cdr, 7), (cdi, 0)):
                for t in range(AT):
                    mm = eng.transpose(ps[:, bank, t * P:(t + 1) * P], src[:, t].rearrange("p a b -> p (a b)"),
                                       ident[:])
            mm.then_inc(c_turned, 1)
            project(2, 2)
            project(3, 3)
            pe.wait_ge(par_out, 1)
            for b in range(4):
                pe.wait_ge(w_lo, AT + b + 1)
                for r in range(2):
                    k = 2 * b + r
                    for t in range(NT):
                        mm = token_rows(AT + b, k, r, WA, xhi, xlo, t, t, 1, k == 0, k == KT - 1)
                mm.then_inc(w_used, 1)

            def qk_part(n, part):
                b = 2 * AT + n
                if part == 0:
                    pe.wait_ge(proj_out, 3 if n == 0 else AT + n if n > 1 else 1)
                    pe.wait_ge(w_lo, b + 1)
                for k in (2 * part, 2 * part + 1):
                    c = slice(k * P, (k + 1) * P)
                    mm = three(ps[:, 6 if n == 1 else 4, :], whi[:, b % WS, c], wlo[:, b % WS, c], xhi[:, k, :],
                               xlo[:, k, :], k == 0, k == KT - 1)
                if part == 3:
                    mm.then_inc(w_used, 1)

            def ssm_products(steps):
                for q, s in steps:
                    step = STEPS * q + s
                    p7 = ps[:, SSM_BANK[step % 2], :]
                    if step >= 2:
                        pe.wait_ge(ssm_out[step % 2], step // 2)
                    if s in (0, 1):
                        pe.wait_ge(wn_ready, 2 * q + s + 1)
                        src = (wnr, wni)[s]
                        for a in range(PQ):
                            mm = eng.transpose(p7[:, a * P:(a + 1) * P], src[:, a].rearrange("p l i -> p (l i)"),
                                               ident[:])
                    if s in (3, 4):
                        pe.wait_ge(cx_ready, 4 * q + 4)
                        rows = slice((s - 3) * PS, (s - 2) * PS)
                        for a in range(PQ):
                            o_ = p7[0:GI, a * P:(a + 1) * P]
                            eng.matmul(o_, bbr[rows, q * PQ + a, :],
                                       cxr[rows, a, 0:L, :].rearrange("p l j -> p (l j)"), start=True, stop=False)
                            mm = eng.matmul(o_, bbi[rows, q * PQ + a, :],
                                            cxi[rows, a, 0:L, :].rearrange("p l j -> p (l j)"),
                                            start=False, stop=True)
                    if s == 2:
                        pe.wait_ge(u_landed[q], 16 * L)
                        pe.wait_ge(*ssm_read(q, 0))
                        pe.wait_ge(*ssm_read(q, 1))
                        for g in range(GQ):
                            a, b = g // 2, g % 2
                            rows = slice(b * PS, (b + 1) * PS)
                            for part, w in enumerate((winr, wini)):
                                o_ = p7[rows, part * PQ * NC + a * NC:part * PQ * NC + (a + 1) * NC]
                                mm = eng.matmul(o_, w[:, a, rows], u8[:, q, g, :], start=True, stop=True)
                    if s in (5, 6):
                        pe.wait_ge(xs_ready, 2 * q + 2)
                        pe.wait_ge(toep_landed, 16 * L * (q + 1))
                        rows = slice((s - 5) * PS, (s - 4) * PS)
                        for a in range(PQ):
                            g = 2 * a + s - 5
                            o_ = p7[:, a * NC:(a + 1) * NC]
                            eng.matmul(o_, toep[:, g, :], u8[:, q, g, :], start=True, stop=False)
                            eng.matmul(o_, cxr[rows, a, 1:, :].rearrange("p l j -> p (l j)"), xsr[rows, a, 0:NC],
                                       start=False, stop=False)
                            mm = eng.matmul(o_, cxi[rows, a, 1:, :].rearrange("p l j -> p (l j)"),
                                            xsi[rows, a, 0:NC], start=False, stop=True)
                    mm.then_inc(ssm_done, 1)

            for n in range(2):
                for part in range(4):
                    qk_part(n, part)

            pe.wait_ge(proj_out, AT + 1)
            pe.wait_ge(v_out, NT)

            def scores(n):
                hd, i = ITEMS[n]
                rows = slice((hd % 2) * HD, (hd % 2 + 1) * HD)
                if i == 0 and hd % 2 == 0:
                    pe.wait_ge(proj_out, AT + hd + 2)
                if n >= 2:
                    pe.wait_ge(s_biased, n - 1)
                eng.matmul(ps[:, n % 2, 0:(i + 1) * P], qT[rows, hd // 2, i * P:(i + 1) * P],
                           kT[rows, hd // 2, 0:(i + 1) * P], start=True, stop=True).then_inc(s_done, 1)

            def turn_probs(n):
                hd, i = ITEMS[n]
                pe.wait_ge(p_ready, n + 1)
                if n >= 2:
                    pe.wait_ge(pt_out, n - 1)
                for j in range(i + 1):
                    mm = eng.transpose(ps[:, 2 + n % 2, j * P:(j + 1) * P], sc[:, n % 3, j * P:(j + 1) * P], ident[:])
                mm.then_inc(pt_done, 1)

            def head_out(hd):
                rows = slice((hd % 2) * HD, (hd % 2 + 1) * HD)
                pe.wait_ge(pt_out, NT * (hd + 1))
                if hd in (2, 4):
                    pe.wait_ge(ao_kept, hd // 2)
                if hd == 6:
                    pe.wait_ge(ao_out, hd // 2)
                for j in range(NT):
                    mm = eng.matmul(ps[rows, 6, j * P:S], v[:, j, hd * HD:(hd + 1) * HD], pt[:, j, j * P:S],
                                    start=(j == 0), stop=(j == NT - 1))
                mm.then_inc(pv_done, 1)

            for n in range(TICKS):
                if n < len(ITEMS):
                    scores(n)
                if n >= 6 and n % NT == 2:
                    head_out((n - 6) // NT)
                if 0 <= n - 2 < len(ITEMS):
                    turn_probs(n - 2)
                ssm_products(ssm_steps(n))
                if n // 4 + 2 < 2 * AT:
                    qk_part(n // 4 + 2, n % 4)

            pe.wait_ge(y_ready, AT)
            for m in range(AT):
                b = GLU + m // 2
                if m >= 2:
                    pe.wait_ge(glu_sig, m - 1)
                mm = feature_major(b, ps[:, 4 + m % 2, :], yhi, ylo, nk=AT, col=(m % 2) * P)
                mm.then_inc(w_used if m % 2 else glu_done, 1)
            pe.wait_ge(ao_out, A_HEADS // 2)

            def mix_ready(k):
                if k >= AT:
                    pe.wait_ge(mix_b, k - AT + 1)

            def glu_banks_read(t):
                if t == 2:
                    pe.wait_ge(glu_sig, AT)

            token_major(EOUT, KT, xhi, xlo, 0, mix_ready, (0, 1, 3, 2), glu_banks_read)

            def overlapped(n, parts):
                pe.wait_ge(x_ready, NT * n + 2)
                for i, part in enumerate(parts):
                    part(0)
                    if i in (1, 2):
                        turn_normed(n, i + 1)
                pe.wait_ge(x_ready, NT * (n + 1))
                for part in parts:
                    part(1)

            def ffn(layer):
                f = FFN[layer]

                def half_unit(m, part):
                    b = f + 2 * m + part
                    wh = whi[:, b % WS, :].rearrange("p (k n) -> p k n", k=KT)
                    wl = wlo[:, b % WS, :].rearrange("p (k n) -> p k n", k=KT)

                    def run(half):
                        c = slice(half * 2 * P, (half + 1) * 2 * P)
                        if half == 0:
                            pe.wait_ge(w_lo, b + 1)
                        for k in range(KT):
                            mm = three(ps[:, 2 * m + part, c], wh[:, k], wl[:, k], xhi[:, k, c], xlo[:, k, c],
                                       k == 0, k == KT - 1)
                        if half:
                            mm.then_inc(w_used, 1)
                    return run

                overlapped(2 * layer + 1, [half_unit(m, part) for m in range(2) for part in range(2)])
                for m in range(2, FT):
                    c = layer * FT + m
                    for part in range(2):
                        b = f + 2 * m + part
                        if part == 0:
                            pe.wait_ge(g_ready, c - 1)
                        mm = feature_major(b, ps[:, 2 * (m % 2) + part, :], xhi, xlo)
                        mm.then_inc(w_used, 1)

                def ready(k):
                    pe.wait_ge(g_lo, layer * FT + k + 1)

                def before(t):
                    if t == 0:
                        pe.wait_ge(g_ready, (layer + 1) * FT)

                token_major(f + 2 * FT, FT, ghi, glo, 2 * layer + 1, ready, order=(2, 3, 0, 1), before=before)

            ffn(0)

            def v_part(k):
                def run(half):
                    if half == 0:
                        pe.wait_ge(w_lo, OV + k + 1)
                    for t in (2 * half, 2 * half + 1):
                        mm = token_rows(OV + k, k, 0, D, xhi, xlo, t, 2 * t, 2, k == 0, k == KT - 1)
                    if half:
                        mm.then_inc(w_used, 1)
                return run

            overlapped(2, [v_part(k) for k in range(KT // 2)])
            for k in range(KT // 2, KT):
                for half in range(2):
                    v_part(k)(half)
            pe.wait_ge(ov_out, NT)

            def oqk(n):
                if n:
                    pe.wait_ge(qk_out, n)
                b = OQK + n
                mm = feature_major(b, ps[:, 6, :], xhi, xlo)
                mm.then_inc(w_used, 1)

            def stick_scores(hd):
                rows = slice((hd % 2) * HD, (hd % 2 + 1) * HD)
                j_ = hd // 2
                pe.wait_ge(qk_out, 2 * j_ + 2)
                if hd:
                    pe.wait_ge(z_read, hd)
                for j in range(NT):
                    keys, queries = slice(j * P, (j + 1) * P), slice(j * P, S)
                    mm = three(psf[:, TRI[j]:TRI[j] + (NT - j) * P],
                               oqk_hi[rows, j_ % 2, 1, keys], oqk_lo[rows, j_ % 2, 1, keys],
                               oqk_hi[rows, j_ % 2, 0, queries], oqk_lo[rows, j_ % 2, 0, queries], True, True)
                mm.then_inc(z_done, 1)

            def stick_sums(hd):
                pe.wait_ge(sp_lo, hd + 1)
                if hd:
                    pe.wait_ge(lw_ready, hd)
                for j in range(NT):
                    for j2 in range(j, NT):
                        o_ = psf[:, 3 * S + TRI[j] + (j2 - j) * P:3 * S + TRI[j] + (NT - j) * P]
                        cols = slice(TRI[j2], TRI[j2] + (NT - j2) * P)
                        w = tri if j2 == j else ones
                        eng.matmul(o_, w[:], sphi[:, cols], start=(j2 == j), stop=False)
                        mm = eng.matmul(o_, w[:], splo[:, cols], start=False, stop=(j2 == NT - 1))
                mm.then_inc(r_done, 1)

            def stick_out(hd):
                rows = slice((hd % 2) * HD, (hd % 2 + 1) * HD)
                pe.wait_ge(w_ready, NT * (hd + 1))
                if hd >= 2 and hd % 2 == 0:
                    pe.wait_ge(o_out, hd // 2)
                for j in range(NT):
                    mm = eng.matmul(ps[rows, 7, j * P:S], ov[:, j, hd * HD:(hd + 1) * HD],
                                    wt[:, hd % 3, TRI[j]:TRI[j] + (NT - j) * P], start=(j == 0), stop=(j == NT - 1))
                mm.then_inc(opv_done, 1)

            for n in range(LEAD):
                oqk(n)
            pe.wait_ge(const_ready, 6)
            stick_scores(0)
            for hd in range(C_HEADS):
                if hd + LEAD < 2 * KT:
                    oqk(hd + LEAD)
                if hd + 1 < C_HEADS:
                    stick_scores(hd + 1)
                stick_sums(hd)
                if hd:
                    stick_out(hd - 1)
            stick_out(C_HEADS - 1)
            pe.wait_ge(omix, KT)
            token_major(OOUT, KT, xhi, xlo, 2)
            ffn(1)


_INS = ["x", "even_w_in", "even_rel_bias", "ssm_lambda_re", "ssm_lambda_im", "ssm_b_re", "ssm_b_im", "ssm_c_re",
        "ssm_c_im", "ssm_d", "ssm_log_dt", "ssm_glu_w", "ssm_glu_b", "even_w_out", "odd_w_in", "odd_w_out",
        "ffn_w1", "ffn_w3", "ffn_w2", "ln_mix_g", "ln_mix_b", "ln_ffn_g", "ln_ffn_b"]


def kernel(**inputs):
    import concourse.bacc as _bacc
    from concourse.bass_utils import run_bass_kernel_spmd as _run

    nc = _bacc.Bacc("TRN2", target_bir_lowering=False, num_devices=1)
    arrays, args = {}, []
    for name in _INS:
        a = np.ascontiguousarray(inputs[name])
        arrays[f"in_{name}"] = a
        args.append(nc.dram_tensor(f"in_{name}", a.shape, mybir.dt.from_np(a.dtype), kind="ExternalInput").ap())
    out = nc.dram_tensor("out", (1, S, D), F32, kind="ExternalOutput").ap()
    build(nc, *args, out)
    r = _run(nc, [arrays], core_ids=[0])
    return r.results[0]["out"]
```

```python
import math
from contextlib import ExitStack

import numpy as np
import concourse.bass as bass
from concourse import mybir

P = 128
D = 1024
S = 512
KT = D // P
NT = S // P
DFF = 2816
FT = DFF // P
WA = 512
AT = WA // P
HD = 64
A_HEADS = WA // HD
C_HEADS = D // HD
CHUNK = 64
MAX_REL = 2 * CHUNK
NREL = 2 * MAX_REL + 1
G, GI, PS = 32, 16, 64
PAIRS = G // 2
GQ = G // AT
PQ = PAIRS // AT
L = P // GI
NC = S // L
ALPHA = 4.0 ** 0.25
EPS = 1e-5
QSCALE = HD ** -0.5
MASKED = -1e30

WB = 1024
RAW = 3
WS = 5
TAIL = 4

ALU = mybir.AluOpType
ACT = mybir.ActivationFunctionType
F32 = mybir.dt.float32
F32R = mybir.dt.float32r

TWO_PI_1 = 6.28125
TWO_PI_2 = math.floor((2 * math.pi - TWO_PI_1) * 2 ** 20) / 2 ** 20
TWO_PI_3 = float(np.float32(2 * math.pi - TWO_PI_1 - TWO_PI_2))
ROUNDER = 1.5 * 2.0 ** 23
PI_BELOW = 3.1415925

TRI = {0: 0, 1: 512, 3: 896, 2: 1024}
TRI_W = 1280


def build(nc, x, even_w_in, rel, lam_re, lam_im, b_re, b_im, c_re, c_im, d_skip, log_dt, glu_w, glu_b,
          even_w_out, odd_w_in, odd_w_out, w1, w3, w2, ln_mix_g, ln_mix_b, ln_ffn_g, ln_ffn_b, out):
    blocks = []

    def feature_tile(w, c0):
        blocks.append(w[:, c0:c0 + P].rearrange("(k p) n -> p k n", p=P))

    def row_tiles(w, r0, c0, cols):
        n = WB // cols
        blocks.append(w[r0:r0 + n * P, c0:c0 + cols].rearrange("(k p) n -> p k n", p=P))

    ewi, ewo = even_w_in[0], even_w_out[0]
    owi, owo = odd_w_in[0], odd_w_out[0]
    for m in range(AT):
        feature_tile(ewi, 3 * WA + m * P)
    for b in range(4):
        row_tiles(ewi, b * 2 * P, 2 * WA, WA)
    for m in range(AT):
        feature_tile(ewi, m * P)
        feature_tile(ewi, WA + m * P)
    GLU = len(blocks)
    for b in range(2):
        blocks.append(glu_w[0][:, b * 256:(b + 1) * 256].rearrange("(k p) n -> p k n", p=P))
    EOUT = len(blocks)
    for k in range(KT):
        row_tiles(ewo, k * P, 0, D)
    FFN = [len(blocks), 0]

    def ffn_blocks(layer):
        FFN[layer] = len(blocks)
        for m in range(FT):
            feature_tile(w1[layer], m * P)
            feature_tile(w3[layer], m * P)
        for k in range(FT):
            row_tiles(w2[layer], k * P, 0, D)

    ffn_blocks(0)
    OV = len(blocks)
    for k in range(KT):
        row_tiles(owi, k * P, 2 * D, D)
    OQK = len(blocks)
    for m in range(KT):
        feature_tile(owi, m * P)
        feature_tile(owi, D + m * P)
    OOUT = len(blocks)
    for k in range(KT):
        row_tiles(owo, k * P, 0, D)
    ffn_blocks(1)
    NBLK = len(blocks)

    ctx = ExitStack()
    with ctx:
        base, top = 16512, 229344
        ctx.enter_context(nc.sbuf_tensor("whole_sbuf", [P, (top - base) // 4], F32))
        at = [base]

        def put(name, shape, dt=F32, off=None):
            o = at[0] if off is None else off
            t = nc.alloc_sbuf_tensor_at(name, shape, dt, offset=o)
            size = (4 * int(np.prod(shape[1:])) + 31) // 32 * 32
            if off is None:
                at[0] += size
            return t, o + size

        def fixed(name, shape, dt=F32):
            return put(name, shape, dt)[0]

        raw = fixed("raw", [P, RAW, WB])
        whi = fixed("whi", [P, WS, WB], F32R)
        wlo = fixed("wlo", [P, WS, WB], F32R)
        xhi = fixed("xhi", [P, KT, S], F32R)
        xlo = fixed("xlo", [P, KT, S], F32R)
        arena = at[0]
        h = fixed("h", [P, NT, D])
        g_region = at[0]
        ghi = fixed("ghi", [P, FT, S], F32R)
        glo = fixed("glo", [P, FT, S], F32R)
        lnp = fixed("lnp", [P, 2, D])
        arena_end = at[0]
        ident = fixed("ident", [P, P])
        tri = fixed("tri", [P, P], F32R)
        ones = fixed("ones", [P, P], F32R)
        sg = fixed("sg", [P, 2, S])
        gt = fixed("gt", [P, 2, S])
        stats = fixed("stats", [P, NT, 2, 6])
        mv = fixed("mv", [P, NT, 2])
        lns = fixed("lns", [P, NT, 4])
        glub = fixed("glub", [P, AT])
        sm = fixed("sm", [P, 3, 4])
        assert at[0] <= top

        e = [arena]

        def even(name, shape, dt=F32):
            t, e[0] = put(name, shape, dt, e[0])
            assert e[0] <= arena_end, (name, e[0] - arena_end)
            return t

        pt = even("pt", [P, NT, S])
        bias = even("bias", [P, 2, S])
        gk = even("gk", [2 * GI, PQ, L, GI])
        zin_r = even("zin_r", [P, PQ, NC])
        zin_i = even("zin_i", [P, PQ, NC])
        assert e[0] == g_region
        qT = even("qT", [P, AT, S])
        kT = even("kT", [P, AT, S])
        v = even("v", [P, NT, WA])
        sc = even("sc", [P, 3, S])
        yT = even("yT", [P, AT, L, NC])
        phr = even("phr", [P, PAIRS, NC])
        phi = even("phi", [P, PAIRS, NC])
        u8 = even("u8", [P, AT, GQ, NC])
        kept, _ = put("kept", [P, 2, S], F32, e[0])
        uP = even("uP", [P, L, NC])
        bnr = even("bnr", [P, PAIRS, GI])
        bni = even("bni", [P, PAIRS, GI])
        y8 = even("y8", [P, GQ, NC])
        winr = even("winr", [P, PQ, P])
        wini = even("wini", [P, PQ, P])
        cxr = even("cxr", [P, PQ, L + 1, GI])
        cxi = even("cxi", [P, PQ, L + 1, GI])
        toep = even("toep", [P, GQ, P])
        wnr = even("wnr", [P, PQ, L, GI])
        wni = even("wni", [P, PQ, L, GI])
        zr = even("zr", [P, PQ, NC])
        zi = even("zi", [P, PQ, NC])
        xsr = even("xsr", [P, PQ, 2, NC + 1])
        xsi = even("xsi", [P, PQ, 2, NC + 1])
        decay = even("decay", [P, PQ, NC])
        bbr = even("bbr", [P, PAIRS, GI])
        bbi = even("bbi", [P, PAIRS, GI])
        bdr = even("bdr", [P, PAIRS, 2, GI])
        bdi = even("bdi", [P, PAIRS, 2, GI])
        cr = even("cr", [P, PAIRS, GI])
        nci = even("nci", [P, PAIRS, GI])
        pw = even("pw", [P, 3, PAIRS, L + 1])
        par = even("par", [P, 7, PAIRS])
        ph = even("ph", [P, 2, 2, PAIRS])
        dd = even("dd", [2 * GI, PAIRS, GI])
        eye2 = even("eye2", [2 * GI, GI])
        t4 = [sg[:, i // 2, (i % 2) * 256:(i % 2 + 1) * 256] for i in range(4)]
        pl, o = put("pl", [PAIRS, 24, P], F32, g_region)
        reltab, o = put("reltab", [A_HEADS, NREL], F32, o)
        relext, o = put("relext", [A_HEADS, 5 * P], F32, o)
        dt2, o = put("dt2", [PAIRS, 2], F32, o)
        assert o <= g_region + 2 * 4 * AT * S
        cdr, o = put("cdr", [P, AT, 2, PS], F32, g_region + 2 * 4 * AT * S)
        cdi, o = put("cdi", [P, AT, 2, PS], F32, o)
        yhi, o = put("yhi", [P, AT, S], F32R, g_region)
        ylo, o = put("ylo", [P, AT, S], F32R, o)

        oatt, o = put("oatt", [P, KT, S], F32, g_region)
        oqk_hi, o = put("oqk_hi", [P, 2, 2, S], F32R, o)
        oqk_lo, o = put("oqk_lo", [P, 2, 2, S], F32R, o)
        ov, o = put("ov", [P, NT, D], F32, o)
        lg, o = put("lg", [P, TRI_W], F32, o)
        sp, o = put("sp", [P, TRI_W], F32, o)
        sphi, o = put("sphi", [P, TRI_W], F32R, o)
        splo, o = put("splo", [P, TRI_W], F32R, o)
        wt, o = put("wt", [P, 3, TRI_W], F32, o)
        assert o <= g_region + 2 * 4 * FT * S, o - g_region

        ps = ctx.enter_context(nc.psum_tensor("ps", [P, 8, S], F32))
        psf = ps[:].rearrange("p b n -> p (b n)")

        u_dram = nc.dram_tensor("u_scratch", (AT, P, S), F32, kind="Internal").ap()
        y_dram = nc.dram_tensor("y_scratch", (AT, P, S), F32, kind="Internal").ap()
        rel_dram = nc.dram_tensor("rel_scratch", (A_HEADS, 5 * P), F32, kind="Internal").ap()

        def sem(name):
            return ctx.enter_context(nc.semaphore(name))

        w_landed = [sem(f"w_landed{i}") for i in range(RAW)]
        w_hi, w_lo, w_used = sem("w_hi"), sem("w_lo"), sem("w_used")
        x_landed = [sem(f"x_landed{i}") for i in range(NT)]
        lam_landed, b_landed, c_landed, rel_landed, glub_landed, d_landed = (
            sem(n) for n in ("lam_landed", "b_landed", "c_landed", "rel_landed", "glub_landed", "d_landed"))
        const_ready, const_zero = sem("const_ready"), sem("const_zero")
        turned, x_hi, x_ready = sem("turned"), sem("x_hi"), sem("x_ready")
        proj_out, v_out = sem("proj_out"), sem("v_out")
        dt_ready, m_ready, mag_ready, arg_ready, trig_ready = (
            sem(n) for n in ("dt_ready", "m_ready", "mag_ready", "arg_ready", "trig_ready"))
        pl_ready, pl_turned, par_read, c_turned, par_out = (
            sem(n) for n in ("pl_ready", "pl_turned", "par_read", "c_turned", "par_out"))
        u_stored, y_stored = sem("u_stored"), sem("y_stored")
        u_landed = [sem(f"u_landed{i}") for i in range(AT)]
        y_landed = [sem(f"y_landed{i}") for i in range(AT)]
        toep_landed = sem("toep_landed")
        wn_ready, cx_ready, gk_ready, xs_ready = (
            sem(n) for n in ("wn_ready", "cx_ready", "gk_ready", "xs_ready"))
        ssm_done = sem("ssm_done")
        ssm_out = [sem(f"ssm_out{i}") for i in range(2)]
        tables_ready, pool_self = sem("tables_ready"), sem("pool_self")
        bd_ready = sem("bd_ready")
        relext_ready, rel_stored = sem("relext_ready"), sem("rel_stored")
        bias_landed = [sem(f"bias_landed{i}") for i in range(2)]
        s_done, s_biased, s_negmax, s_exp, p_ready, pt_done, pt_out, pv_done, ao_hi, ao_out = (
            sem(n) for n in ("s_done", "s_biased", "s_negmax", "s_exp", "p_ready", "pt_done", "pt_out",
                             "pv_done", "ao_hi", "ao_out"))
        ao_kept = sem("ao_kept")
        y_gelu, y_hi, y_ready, glu_done, glu_sig, ob_ready, ob_hi, mix_b = (
            sem(n) for n in ("y_gelu", "y_hi", "y_ready", "glu_done", "glu_sig", "ob_ready", "ob_hi", "mix_b"))
        acc_done, var_ready, std_ready, rstd_ready, scaled, h_ready, h_last, lnp_landed, h_landed = (
            sem(n) for n in ("acc_done", "var_ready", "std_ready", "rstd_ready", "scaled", "h_ready", "h_last",
                             "lnp_landed", "h_landed"))
        silu_ready, g_ready, g_hi, g_lo = (sem(n) for n in ("silu_ready", "g_ready", "g_hi", "g_lo"))
        ov_out, qk_hi, qk_out = sem("ov_out"), sem("qk_hi"), sem("qk_out")
        z_done, l_ready, z_read, sp_raw, sp_masked, sp_hi, sp_lo = (
            sem(n) for n in ("z_done", "l_ready", "z_read", "sp_raw", "sp_masked", "sp_hi", "sp_lo"))
        r_done, lw_ready, w_exp, w_ready, opv_done, o_out = (
            sem(n) for n in ("r_done", "lw_ready", "w_exp", "w_ready", "opv_done", "o_out"))
        omix_hi, omix = sem("omix_hi"), sem("omix")
        early_done, early_added = sem("early_done"), sem("early_added")
        dve_self, act_self = sem("dve_self"), sem("act_self")
        out_stored = sem("out_stored")

        ITEMS = [(hd, i) for hd in range(A_HEADS) for i in range(NT)]
        TICKS = len(ITEMS) + NT - 1
        STEPS = 5
        TOEP = 16 * L * 2
        PERIOD = 7
        SSM_BANK = (7, 5)

        def ssm_steps(n):
            after = [(n // PERIOD - 1, 4)] if n % PERIOD == 0 else []
            now = [(n // PERIOD, n % PERIOD)] if n % PERIOD < 4 else []
            return [(q, st) for q, st in after + now if 0 <= q < AT]

        def ssm_read(q, st):
            k = STEPS * q + st
            return ssm_out[k % 2], k // 2 + 1

        X_USED = 24

        def qk_of(n):
            return n // 4 + 2 if n % 4 == 3 and n // 4 + 2 < 2 * AT else None

        EARLY_K = KT // 2

        def mixed_behind(hd):
            return {C_HEADS - 4: range(EARLY_K), C_HEADS - 3: (4, 5), C_HEADS - 1: (6,)}.get(hd, ())

        EARLY = [(t, half) for t in range(NT) for half in range(2)]
        LEAD = 3

        def qk_bank(n):
            return 7 if n == 1 else 6

        block = ctx.enter_context(nc.Block())

        @block.sync
        def _(sp_):
            eng = nc.sync
            issued = [0]

            def weights_upto(n):
                while issued[0] < min(n, NBLK):
                    b = issued[0]
                    if b >= RAW:
                        sp_.wait_ge(w_lo, b - RAW + 1)
                    src = blocks[b]
                    dst = raw[:, b % RAW, :].rearrange("p (k n) -> p k n", k=src.shape[1])
                    eng.dma_start(dst, src).then_inc(w_landed[b % RAW], 16)
                    issued[0] += 1

            xt = x[0].rearrange("(t p) d -> t p d", p=P)
            eng.dma_start(pl[:, 7, :], lam_re[0].rearrange("(a b) p -> a (b p)", b=2)).then_inc(lam_landed, 16)
            eng.dma_start(pl[:, 8, :], lam_im[0].rearrange("(a b) p -> a (b p)", b=2)).then_inc(lam_landed, 16)
            eng.dma_start(dt2[:], log_dt[0].rearrange("(a b) -> a b", b=2)).then_inc(lam_landed, 16)
            eng.dma_start(h[:, 0, :], xt[0]).then_inc(x_landed[0], 16)
            weights_upto(1)
            for t in range(1, NT):
                eng.dma_start(h[:, t, :], xt[t]).then_inc(x_landed[t], 16)
            weights_upto(2)
            eng.dma_start(bnr[:], b_re[0].rearrange("(a b) p i -> (b p) a i", b=2)).then_inc(b_landed, 16)
            eng.dma_start(bni[:], b_im[0].rearrange("(a b) p i -> (b p) a i", b=2)).then_inc(b_landed, 16)
            for dst, src in ((cdr, c_re), (cdi, c_im)):
                for dup in range(2):
                    eng.dma_start(dst[:, :, dup, :], src[0].rearrange("(t g) j p -> (g j) t p", g=GQ)).then_inc(
                        c_landed, 16)
            eng.dma_start(reltab[:], rel[0]).then_inc(rel_landed, 16)
            for b in range(2):
                eng.dma_start(dd[b * GI:(b + 1) * GI], d_skip[0].rearrange("(a b) j -> b a j", b=2)[b]
                              .partition_broadcast(GI)).then_inc(d_landed, 16)
            eng.dma_start(glub[:], glu_b[0].rearrange("(t p) -> p t", p=P),
                          allow_slow_non_contiguous=True).then_inc(glub_landed, 16)
            weights_upto(5)

            for q in range(AT):
                weights_upto(q + 7)
                sp_.wait_ge(proj_out, q + 1)
                eng.dma_start(u_dram[q], uP[:].rearrange("p s c -> p (s c)")).then_inc(u_stored, 16)
                sp_.wait_ge(u_stored, 16 * (q + 1))
                src = u_dram[q].rearrange("(g i) (s c) -> s i g c", g=GQ, s=L)
                for s in range(L):
                    r = L - 1 - s
                    eng.dma_start(u8[GI * r:GI * (r + 1), q], src[s]).then_inc(u_landed[q], 16)

            def load_bias(hd):
                if hd >= 2:
                    sp_.wait_ge(s_biased, NT * (hd - 1))
                src = bass.AP(rel_dram.tensor, hd * 5 * P, [[1, P], [1, S]])
                eng.dma_start(bias[:, hd % 2, :], src).then_inc(bias_landed[hd % 2], 16)

            def ssm_moves(steps):
                for q, s in steps:
                    if s == 3:
                        sp_.wait_ge(gk_ready, q + 1)
                        if q:
                            sp_.wait_ge(ssm_done, STEPS * q)
                        else:
                            sp_.wait_ge(const_ready, 8)
                        for r in range(L):
                            for b in range(2):
                                eng.dma_start(toep[GI * r:GI * (r + 1), b::2, GI * (L - 1 - r):],
                                              gk[GI * b:GI * (b + 1), :, 0:r + 1, :].rearrange(
                                                  "i a t j -> i a (t j)")).then_inc(toep_landed, 16)
                    if s == 4:
                        sp_.wait_ge(*ssm_read(q, 4))
                        eng.dma_start(y_dram[q], y8[:].rearrange("p g c -> p (g c)")).then_inc(y_stored, 16)
                        sp_.wait_ge(y_stored, 16 * (q + 1))
                        src = y_dram[q].rearrange("(t j) (g c) -> g j t c", t=L, g=GQ)
                        for g in range(GQ):
                            eng.dma_start(yT[GI * g:GI * (g + 1), q], src[g]).then_inc(y_landed[q], 16)

            weights_upto(2 * AT + 4)
            sp_.wait_ge(relext_ready, 2)
            eng.dma_start(rel_dram, relext[:]).then_inc(rel_stored, 16)
            sp_.wait_ge(rel_stored, 16)
            sp_.wait_ge(x_ready, NT)
            load_bias(0)
            load_bias(1)
            weights_upto(2 * AT + 8)
            for n in range(TICKS):
                if qk_of(n) is not None:
                    weights_upto(2 * AT + qk_of(n) + 7)
                if n % NT == 1 and 0 < n // NT < A_HEADS - 1:
                    load_bias(n // NT + 1)
                ssm_moves(ssm_steps(n))

            def load_norm(n):
                for i, p in enumerate([(ln_mix_g, ln_mix_b), (ln_ffn_g, ln_ffn_b)][n % 2]):
                    eng.dma_start(lnp[:, i, :], p[n // 2].partition_broadcast(P)).then_inc(lnp_landed, 16)

            weights_upto(GLU + WS + RAW)
            sp_.wait_ge(pv_done, A_HEADS)
            sp_.wait_ge(s_biased, A_HEADS * NT)
            sp_.wait_ge(ssm_done, STEPS * AT)
            sp_.wait_ge(xs_ready, 4 * AT)
            sp_.wait_ge(toep_landed, TOEP * AT)
            for t in range(NT):
                eng.dma_start(h[:, t, :], xt[t]).then_inc(h_landed, 16)
            load_norm(0)
            weights_upto(FFN[0] + WS)
            for n, upto in ((1, OV + WS), (2, FFN[1] + WS), (3, NBLK)):
                sp_.wait_ge(h_ready, (NT - 1) * n)
                sp_.wait_ge(h_last, n)
                load_norm(n)
                weights_upto(upto)
            ot = out[0].rearrange("(t p) d -> t p d", p=P)
            for t in range(NT):
                if t < NT - 1:
                    sp_.wait_ge(h_ready, 3 * (NT - 1) + t + 1)
                else:
                    sp_.wait_ge(h_last, 4)
                eng.dma_start(ot[t], h[:, t, :]).then_inc(out_stored, 16)
            sp_.wait_ge(out_stored, 16 * NT)

        @block.gpsimd
        def _(pool):
            eng = nc.gpsimd
            eng.memset(ident[:], 0.0).then_inc(const_zero, 1)
            eng.memset(ones[:].bitcast(F32), 1.0).then_inc(const_ready, 1)
            eng.memset(toep[:], 0.0).then_inc(const_ready, 1)
            eng.memset(xsr[:], 0.0).then_inc(const_ready, 1)
            eng.memset(xsi[:], 0.0).then_inc(const_ready, 1)
            eng.memset(bdr[:], 0.0).then_inc(const_ready, 1)
            eng.memset(bdi[:], 0.0).then_inc(const_ready, 1)
            pool.wait_ge(const_zero, 1)
            eng.affine_select(out=ident[:], in_=ident[:], compare_op=ALU.not_equal, fill=1.0, base=0,
                              pattern=[[-1, P]], channel_multiplier=1).then_inc(const_ready, 1)
            pool.wait_ge(const_ready, 7)
            eng.affine_select(out=tri[:], in_=ones[:].bitcast(F32), compare_op=ALU.is_gt, fill=0.0, base=0,
                              pattern=[[-1, P]], channel_multiplier=1).then_inc(const_ready, 1)
            split = [0]

            def lower_upto(n):
                while split[0] < min(n, NBLK):
                    b = split[0]
                    pool.wait_ge(w_hi, b + 1)
                    eng.tensor_tensor(wlo[:, b % WS, :], raw[:, b % RAW, :], whi[:, b % WS, :].bitcast(F32),
                                      ALU.subtract).then_inc(w_lo, 1)
                    split[0] += 1

            def mask(t, signal):
                for j in range(NT):
                    o = TRI[j]
                    eng.affine_select(out=t[:, o:o + P], in_=t[:, o:o + P], compare_op=ALU.is_gt, fill=0.0,
                                      base=0, pattern=[[1, P]], channel_multiplier=-1).then_inc(signal, 1)

            own = [0]

            def link(ins):
                own[0] += 1
                ins.then_inc(pool_self, 1)
                pool.wait_ge(pool_self, own[0])

            def sum_of_products(o_, a, b, c, d, op, signal, value):
                n = int(np.prod(o_.shape[1:]))
                t0, t1 = (gt[:, k, 0:n].rearrange("p (a b c) -> p a b c", b=o_.shape[2], c=GI) for k in range(2))
                eng.tensor_tensor(t0, a, b, ALU.mult).then_inc(pool_self, 1)
                own[0] += 1
                link(eng.tensor_tensor(t1, c, d, ALU.mult))
                eng.tensor_tensor(o_, t0, t1, op).then_inc(signal, 1)
                pool.wait_ge(signal, value)

            def build_in(q):
                if q:
                    pool.wait_ge(ssm_done, STEPS * (q - 1) + 2)
                pq = slice(q * PQ, (q + 1) * PQ)
                sh = (P, PQ, L, GI)
                b_r = bbr[:, pq].unsqueeze(2).broadcast_to(sh)
                b_i = bbi[:, pq].unsqueeze(2).broadcast_to(sh)
                a_r, a_i = (pw[:, k, pq, 0:L].unsqueeze(3).broadcast_to(sh) for k in range(2))
                sum_of_products(wnr[:], b_r, a_r, b_i, a_i, ALU.subtract, wn_ready, 2 * q + 1)
                sum_of_products(wni[:], b_r, a_i, b_i, a_r, ALU.add, wn_ready, 2 * q + 2)

            def build_out(q):
                if q:
                    pool.wait_ge(ssm_done, STEPS * q)
                pq = slice(q * PQ, (q + 1) * PQ)
                for half in range(2):
                    lo = half * (L // 2)
                    n = L // 2 + half
                    sh = (P, PQ, n, GI)
                    c_r = cr[:, pq].unsqueeze(2).broadcast_to(sh)
                    c_i = nci[:, pq].unsqueeze(2).broadcast_to(sh)
                    a_r, a_i, a_n = (pw[:, k, pq, lo:lo + n].unsqueeze(3).broadcast_to(sh) for k in range(3))
                    sum_of_products(cxr[:, :, lo:lo + n], c_r, a_r, c_i, a_i, ALU.add, cx_ready,
                                    4 * q + 2 * half + 1)
                    sum_of_products(cxi[:, :, lo:lo + n], c_r, a_n, c_i, a_r, ALU.add, cx_ready,
                                    4 * q + 2 * half + 2)

            lower_upto(2 * AT + 2)
            pool.wait_ge(tables_ready, 1)
            build_in(0)
            lower_upto(2 * AT + 3)
            build_out(0)
            lower_upto(2 * AT + 6)
            for n in range(TICKS):
                if n % PERIOD == 2 and n // PERIOD + 1 < AT:
                    build_in(n // PERIOD + 1)
                if n and n % PERIOD == 0 and n // PERIOD < AT:
                    build_out(n // PERIOD)
                if qk_of(n) is not None:
                    lower_upto(2 * AT + qk_of(n) + 5)

            def norm(n, f):
                lower_upto(f + 1)
                for t in range(NT - 1):
                    if t == NT - 2:
                        lower_upto(f + 2)
                    pool.wait_ge(scaled, (NT - 1) * n + t + 1)
                    if t == 0:
                        pool.wait_ge(lnp_landed, 32 * (n + 1))
                    eng.tensor_tensor(h[:, t, :], h[:, t, :], lnp[:, 1, :], ALU.add).then_inc(h_ready, 1)

            norm(0, FFN[0])
            norm(1, OV)
            lower_upto(OQK + LEAD + 4)
            for hd in range(C_HEADS + 1):
                if hd < C_HEADS:
                    pool.wait_ge(sp_raw, hd + 1)
                    mask(sp, sp_masked)
                if hd:
                    pool.wait_ge(w_exp, hd)
                    mask(wt[:, (hd - 1) % 3], w_ready)
                lower_upto(min(OQK + LEAD + WS + hd, OOUT + WS))
            norm(2, FFN[1])
            norm(3, NBLK)

        @block.scalar
        def _(act):
            eng = nc.scalar
            rounded = [0]
            own = [0]

            def upper_upto(n):
                while rounded[0] <= min(n, NBLK - 1):
                    b = rounded[0]
                    act.wait_ge(w_landed[b % RAW], 16 * (b // RAW + 1))
                    if b >= WS:
                        act.wait_ge(w_used, b - WS + 1)
                    eng.copy(whi[:, b % WS, :], raw[:, b % RAW, :]).then_inc(w_hi, 1)
                    rounded[0] += 1

            def link(ins):
                own[0] += 1
                ins.then_inc(act_self, 1)
                act.wait_ge(act_self, own[0])

            def upper_x(n, t):
                act.wait_ge(turned, NT * n + t + 1)
                eng.copy(xhi[:, :, t * P:(t + 1) * P],
                         psf[:, 2 * t * S:2 * (t + 1) * S].rearrange("p (k n) -> p k n", k=KT)).then_inc(x_hi, 1)

            act.wait_ge(lam_landed, 48)
            eng.activation(dt2[:], dt2[:], ACT.Exp).then_inc(dt_ready, 1)
            for t in range(NT):
                upper_x(0, t)
            upper_upto(1)
            act.wait_ge(m_ready, 1)
            eng.activation(pl[:, 10, :], pl[:, 9, :], ACT.Exp).then_inc(mag_ready, 1)
            upper_upto(3)
            act.wait_ge(arg_ready, 1)
            eng.activation(pl[:, 6, :], pl[:, 12, :], ACT.Sin).then_inc(trig_ready, 1)
            eng.activation(pl[:, 5, :], pl[:, 13, :], ACT.Sin).then_inc(trig_ready, 1)

            def project_out(n, dst, scale=None):
                act.wait_ge(w_used, (n if n < AT else n + 4) + 1)
                src = ps[:, 4 + n % 2 if n < AT else 6 if n == AT + 1 else 4, :]
                if dst is None:
                    q = n
                    if q:
                        act.wait_ge(u_stored, 16 * q)
                    ins = eng.copy(uP[:].rearrange("p s c -> p c s"), src.rearrange("p (c s) -> p c s", s=L))
                elif scale:
                    ins = eng.mul(dst, src.rearrange("p (t n) -> p t n", n=P), scale)
                else:
                    ins = eng.copy(dst, src)
                ins.then_inc(proj_out, 1)

            for q in range(AT):
                upper_upto(q + 4)
                project_out(q, None)
            upper_upto(8)
            act.wait_ge(c_turned, 1)
            for b in range(4):
                upper_upto(8 + b)
            act.wait_ge(w_used, 2 * AT)
            for t in range(NT):
                eng.copy(v[:, t, :], ps[:, t, :]).then_inc(v_out, 1)

            def ssm_outs(steps):
                for q, s in steps:
                    k = STEPS * q + s
                    bank = ps[:, SSM_BANK[k % 2], :]
                    if s in (0, 1):
                        act.wait_ge(ssm_done, k + 1)
                        eng.copy((winr, wini)[s][:].rearrange("p a n -> p (a n)"), bank).then_inc(ssm_out[k % 2], 1)
                    if s == 4:
                        act.wait_ge(ssm_done, k + 1)
                        if q:
                            act.wait_ge(y_stored, 16 * q)
                        eng.copy(y8[:].rearrange("p g c -> p (g c)"), bank).then_inc(ssm_out[k % 2], 1)

            def qk_out(n):
                if n % 2 == 0:
                    project_out(AT + n, qT[:, n // 2, :].rearrange("p (t n) -> p t n", n=P)[:, :, ::-1], QSCALE)
                else:
                    project_out(AT + n, kT[:, n // 2, :])

            act.wait_ge(pl_turned, 1)
            act.wait_ge(rel_stored, 16)
            act.wait_ge(par_out, 1)
            for n in range(2):
                upper_upto(2 * AT + n + 4)
                qk_out(n)

            def softmax_exp(n):
                w = (ITEMS[n][1] + 1) * P
                act.wait_ge(s_negmax, n + 1)
                eng.activation(sc[:, n % 3, 0:w], sc[:, n % 3, 0:w], ACT.Exp, bias=sm[:, n % 3, 1:2],
                               accum_out=sm[:, n % 3, 2:3]).then_inc(s_exp, 1)

            def turned_out(n):
                hd, i = ITEMS[n]
                act.wait_ge(pt_done, n + 1)
                if hd and i == 0:
                    act.wait_ge(pv_done, hd)
                eng.copy(pt[:, 0:i + 1, i * P:(i + 1) * P],
                         ps[:, 2 + n % 2, 0:(i + 1) * P].rearrange("p (j n) -> p j n", n=P)[:, :, ::-1]).then_inc(
                             pt_out, 1)

            def pair_keep(j):
                act.wait_ge(pv_done, 2 * j + 2)
                if j == 0:
                    act.wait_ge(u_stored, 16 * AT)
                    act.wait_ge(bd_ready, 4)
                eng.copy(kept[:, j, :], ps[:, 6, :]).then_inc(ao_kept, 1)

            def pair_upper(j):
                if j < 2:
                    act.wait_ge(ao_kept, j + 1)
                else:
                    act.wait_ge(pv_done, 2 * j + 2)
                act.wait_ge(w_used, GLU)
                eng.copy(xhi[:, j, :], kept[:, j, :] if j < 2 else ps[:, 6, :]).then_inc(ao_hi, 1)

            act.wait_ge(tables_ready, 1)
            act.wait_ge(const_ready, 7)
            for b in range(2):
                rows = slice(b * PS, (b + 1) * PS)
                eng.copy(bdr[rows, :, b, :], bbr[rows]).then_inc(bd_ready, 1)
                eng.copy(bdi[rows, :, b, :], bbi[rows]).then_inc(bd_ready, 1)
            upper_upto(2 * AT + 6)
            for n in range(TICKS):
                if n < len(ITEMS):
                    softmax_exp(n)
                if 0 <= n - 2 < len(ITEMS):
                    turned_out(n - 2)
                ssm_outs(ssm_steps(n))
                if qk_of(n) is not None:
                    qk_out(qk_of(n))
                    upper_upto(2 * AT + qk_of(n) + 5)
                if n in (10, 18):
                    pair_keep((n - 10) // 8)
                if n in (X_USED, X_USED + 1):
                    pair_upper(n - X_USED)
                if n == len(ITEMS):
                    for q in range(AT):
                        act.wait_ge(y_landed[q], 16 * GQ)
                        eng.activation(yT[:, q], yT[:, q], ACT.Gelu_apprx_tanh).then_inc(y_gelu, 1)
                if n == len(ITEMS) + 1:
                    act.wait_ge(s_done, len(ITEMS))
                    for q in range(AT):
                        act.wait_ge(y_gelu, q + 1)
                        eng.copy(yhi[:, q, :], yT[:, q].rearrange("p t c -> p (t c)")).then_inc(y_hi, 1)
                if n in (26, 34):
                    pair_upper((n - 10) // 8)

            act.wait_ge(glub_landed, 16)
            for m in range(AT):
                if m % 2:
                    act.wait_ge(w_used, GLU + m // 2 + 1)
                else:
                    act.wait_ge(glu_done, m // 2 + 1)
                if m >= 2:
                    act.wait_ge(ob_ready, m - 1)
                eng.activation(sg[:, m % 2, :], ps[:, 4 + m % 2, :], ACT.Sigmoid,
                               bias=glub[:, m:m + 1]).then_inc(glu_sig, 1)
                act.wait_ge(ob_ready, m + 1)
                eng.copy(xhi[:, AT + m, :].rearrange("p (c t) -> p c t", t=L),
                         gt[:, m % 2, :].rearrange("p (t c) -> p c t", t=L)).then_inc(ob_hi, 1)

            def norm(n, f):
                def std(t):
                    act.wait_ge(var_ready, NT * n + t + 1)
                    eng.activation(lns[:, t, 1:2], lns[:, t, 0:1], ACT.Sqrt).then_inc(std_ready, 1)

                for t in range(NT - 1):
                    if n < 3 and t == 2:
                        upper_x(n + 1, 0)
                        upper_x(n + 1, 1)
                    std(t)
                    act.wait_ge(rstd_ready, (NT - 1) * n + t + 1)
                    eng.mul(h[:, t, :], h[:, t, :], lns[:, t, 2:3]).then_inc(scaled, 1)
                upper_upto(f + 3)
                std(NT - 1)
                if n < 3:
                    upper_upto(f + 4)
                    upper_x(n + 1, 2)
                    upper_x(n + 1, 3)

            def product(first, nk):
                for k in range(nk):
                    upper_upto(first + k)

            def ffn(layer):
                f = FFN[layer]
                for m in range(FT):
                    upper_upto(f + 2 * m + 4)
                    c = layer * FT + m
                    act.wait_ge(w_used, f + 2 * m + 1)
                    if m >= 2:
                        act.wait_ge(g_ready, c - 1)
                    eng.activation(sg[:, m % 2, :], ps[:, 2 * (m % 2), :], ACT.Silu).then_inc(silu_ready, 1)
                    upper_upto(f + 2 * m + 5)
                    act.wait_ge(g_ready, c + 1)
                    eng.copy(ghi[:, m, :], gt[:, m % 2, :]).then_inc(g_hi, 1)
                product(f + 2 * FT, FT)

            product(EOUT, KT)
            upper_upto(FFN[0])
            norm(0, FFN[0])
            ffn(0)
            upper_upto(OV)
            norm(1, OV)
            product(OV, KT)
            upper_upto(OQK + 3)
            act.wait_ge(w_used, OV + KT)
            for t in (3, 0, 1, 2):
                eng.copy(ov[:, t, :], psf[:, 2 * t * S:2 * (t + 1) * S]).then_inc(ov_out, 1)

            def stick_logs(hd):
                act.wait_ge(z_done, hd + 1)
                if hd:
                    act.wait_ge(z_read, hd)
                link(eng.activation(lg[:], psf[:, 0:TRI_W], ACT.Abs))
                link(eng.activation(lg[:], lg[:], ACT.Exp, scale=-1.0))
                eng.activation(lg[:], lg[:], ACT.Ln, bias=1.0).then_inc(l_ready, 1)

            def stick_upper(hd):
                act.wait_ge(sp_masked, NT * (hd + 1))
                if hd:
                    act.wait_ge(r_done, hd)
                eng.copy(sphi[:], sp[:]).then_inc(sp_hi, 1)

            def stick_exp(hd):
                act.wait_ge(lw_ready, hd + 1)
                eng.activation(wt[:, hd % 3], wt[:, hd % 3], ACT.Exp).then_inc(w_exp, 1)

            def oqk_outs(n):
                act.wait_ge(w_used, OQK + n + 1)
                if n >= 4 and n % 2 == 0:
                    act.wait_ge(z_done, n - 2)
                hi = oqk_hi[:, n // 2 % 2, n % 2, :]
                if n % 2 == 0:
                    eng.mul(hi, ps[:, qk_bank(n), :], QSCALE).then_inc(qk_hi, 1)
                else:
                    eng.copy(hi, ps[:, qk_bank(n), :]).then_inc(qk_hi, 1)

            def pair_out(j):
                act.wait_ge(opv_done, 2 * j + 2)
                eng.copy(oatt[:, j, :], ps[:, 7, :]).then_inc(o_out, 1)

            def mix_upper(j):
                act.wait_ge(o_out, j + 1)
                act.wait_ge(w_used, OOUT)
                eng.copy(xhi[:, j, :], oatt[:, j, :]).then_inc(omix_hi, 1)

            eng.preload_act_table_set("natural_log_exp_and_others")
            for n in range(LEAD):
                upper_upto(OQK + n + 4)
                oqk_outs(n)
            stick_logs(0)
            upper_upto(OQK + LEAD + 4)
            stick_upper(0)
            oqk_outs(LEAD)
            for hd in range(C_HEADS):
                if hd + 1 < C_HEADS:
                    stick_logs(hd + 1)
                stick_exp(hd)
                upper_upto(min(OQK + LEAD + hd + 5, OOUT + 4))
                if hd and hd % 2 == 0:
                    pair_out(hd // 2 - 1)
                if hd + 1 < C_HEADS:
                    stick_upper(hd + 1)
                if hd + 1 + LEAD < 2 * KT:
                    oqk_outs(hd + 1 + LEAD)
                for j in mixed_behind(hd):
                    mix_upper(j)
            upper_upto(OOUT + 6)
            pair_out(KT - 1)
            mix_upper(KT - 1)
            upper_upto(OOUT + 7)
            upper_upto(FFN[1])
            norm(2, FFN[1])
            ffn(1)
            norm(3, NBLK)

        @block.vector
        def _(dve):
            eng = nc.vector
            own = [0]

            def count(ins):
                own[0] += 1
                ins.then_inc(dve_self, 1)

            def settle():
                dve.wait_ge(dve_self, own[0])

            def link(ins):
                count(ins)
                settle()

            def tt(o_, a, b, op):
                return eng.tensor_tensor(o_, a, b, op)

            def lower_x(n, t):
                dve.wait_ge(x_hi, NT * n + t + 1)
                cols = slice(t * P, (t + 1) * P)
                tt(xlo[:, :, cols], psf[:, 2 * t * S:2 * (t + 1) * S].rearrange("p (k n) -> p k n", k=KT),
                   xhi[:, :, cols].bitcast(F32), ALU.subtract).then_inc(x_ready, 1)

            def products4(a_r, a_i, b_r, b_i, n, shape):
                v4 = [t[:, 0:n] if len(shape) == 1 else
                      t[:, 0:n].rearrange("p (a b) -> p a b", b=shape[-1]) if len(shape) == 2 else
                      t[:, 0:n].rearrange("p (a b c) -> p a b c", b=shape[-2], c=shape[-1]) for t in t4]
                for o_, (a, b) in zip(v4, ((a_r, b_r), (a_i, b_i), (a_r, b_i), (a_i, b_r))):
                    count(tt(o_, a, b, ALU.mult))
                settle()
                return v4

            def cmul(o_r, o_i, a_r, a_i, b_r, b_i, n, shape):
                v4 = products4(a_r, a_i, b_r, b_i, n, shape)
                count(tt(o_r, v4[0], v4[1], ALU.subtract))
                count(tt(o_i, v4[2], v4[3], ALU.add))
                settle()

            AR, AI, FR, FI, M8, CS, SN, LR, LI, M, MAG, TH, RS, RC, A, B, C_, D_ = range(18)
            dve.wait_ge(lam_landed, 48)
            dve.wait_ge(dt_ready, 1)
            dtb = dt2[:].unsqueeze(2).broadcast_to((PAIRS, 2, PS))

            def q_(i):
                return pl[:, i, :]

            def q2(i):
                return pl[:, i, :].rearrange("a (b p) -> a b p", b=2)

            tt(q2(M), q2(LR), dtb, ALU.mult).then_inc(m_ready, 1)
            link(tt(q2(TH), q2(LI), dtb, ALU.mult))
            link(eng.tensor_scalar(q_(A), q_(TH), 1 / (2 * math.pi), ROUNDER, ALU.mult, ALU.add))
            link(eng.tensor_scalar(q_(A), q_(A), ROUNDER, None, ALU.subtract))
            for part in (TWO_PI_1, TWO_PI_2, TWO_PI_3):
                link(eng.scalar_tensor_tensor(out=q_(TH), in0=q_(A), scalar=-part, in1=q_(TH),
                                              op0=ALU.mult, op1=ALU.add))
            link(eng.tensor_scalar(q_(RS), q_(TH), PI_BELOW, -PI_BELOW, ALU.min, ALU.max))
            link(eng.tensor_scalar(q_(RC), q_(RS), -1.0, None, ALU.mult))
            link(tt(q_(RC), q_(RC), q_(RS), ALU.min))
            eng.tensor_scalar(q_(RC), q_(RC), math.pi / 2, None, ALU.add).then_inc(arg_ready, 1)
            for t in range(NT):
                lower_x(0, t)
            dve.wait_ge(mag_ready, 1)
            dve.wait_ge(trig_ready, 2)
            count(tt(q_(AR), q_(MAG), q_(CS), ALU.mult))
            count(tt(q_(AI), q_(MAG), q_(SN), ALU.mult))
            count(tt(q_(A), q_(LR), q_(LR), ALU.mult))
            count(tt(q_(B), q_(LI), q_(LI), ALU.mult))
            count(tt(q_(M8), q_(MAG), q_(MAG), ALU.mult))
            settle()
            count(tt(q_(A), q_(A), q_(B), ALU.add))
            count(eng.tensor_scalar(q_(C_), q_(AR), 1.0, None, ALU.subtract))
            count(tt(q_(D_), q_(M8), q_(M8), ALU.mult))
            settle()
            count(eng.reciprocal(q_(A), q_(A)))
            count(tt(q_(M8), q_(D_), q_(D_), ALU.mult))
            count(tt(q_(FR), q_(C_), q_(LR), ALU.mult))
            count(tt(q_(B), q_(AI), q_(LI), ALU.mult))
            count(tt(q_(FI), q_(AI), q_(LR), ALU.mult))
            count(tt(q_(TH), q_(C_), q_(LI), ALU.mult))
            settle()
            count(tt(q_(FR), q_(FR), q_(B), ALU.add))
            count(tt(q_(FI), q_(FI), q_(TH), ALU.subtract))
            settle()
            count(tt(q_(FR), q_(FR), q_(A), ALU.mult))
            count(tt(q_(FI), q_(FI), q_(A), ALU.mult))
            settle()
            eng.engine_nop().then_inc(pl_ready, 1)

            dve.wait_ge(rel_landed, 16)
            eng.tensor_copy(relext[:, 0:S - P], reltab[:, NREL - 1:NREL].broadcast_to((A_HEADS, S - P))).then_inc(
                relext_ready, 1)
            eng.tensor_copy(relext[:, S - P:5 * P], reltab[:, 2 * MAX_REL - 1::-1]
                            ).then_inc(relext_ready, 1)

            dve.wait_ge(d_landed, 32)
            dve.wait_ge(const_ready, 7)
            link(tt(eye2[:], ident[0:2 * GI, 0:GI], ident[0:2 * GI, GI:2 * GI], ALU.add))
            link(tt(dd[:], dd[:], eye2[:].unsqueeze(1).broadcast_to((2 * GI, PAIRS, GI)), ALU.mult))

            dve.wait_ge(pl_turned, 1)
            eng.tensor_copy(par[:].rearrange("p a b -> p (a b)"), ps[:, 6, 0:7 * PAIRS]).then_inc(par_read, 1)
            dve.wait_ge(par_read, 1)
            dve.wait_ge(c_turned, 1)
            cre = ps[:, 7, :].rearrange("p (a b j) -> p a b j", b=2, j=GI)
            cim = ps[:, 0, :].rearrange("p (a b j) -> p a b j", b=2, j=GI)
            for b in range(2):
                rows = slice(b * PS, (b + 1) * PS)
                count(eng.tensor_copy(cr[rows], cre[rows, :, b, :]))
                count(eng.tensor_scalar(nci[rows], cim[rows, :, b, :], -1.0, None, ALU.mult))
            settle()
            eng.engine_nop().then_inc(par_out, 1)

            def wide(i, n):
                return par[:, i, :].unsqueeze(2).broadcast_to((P, PAIRS, n))

            dve.wait_ge(b_landed, 32)
            cmul(bbr[:], bbi[:], bnr[:], bni[:], wide(FR, GI), wide(FI, GI), PAIRS * GI, (PAIRS, GI))
            count(eng.memset(pw[:, 0, :, 0:1], 1.0))
            count(eng.memset(pw[:, 1, :, 0:1], 0.0))
            count(eng.tensor_copy(pw[:, 0:2, :, 1], par[:, 0:2, :]))
            settle()
            n = 1
            while n < L:
                by_r = pw[:, 0, :, n:n + 1].broadcast_to((P, PAIRS, n))
                by_i = pw[:, 1, :, n:n + 1].broadcast_to((P, PAIRS, n))
                cmul(pw[:, 0, :, n + 1:2 * n + 1], pw[:, 1, :, n + 1:2 * n + 1], pw[:, 0, :, 1:n + 1],
                     pw[:, 1, :, 1:n + 1], by_r, by_i, PAIRS * n, (PAIRS, n))
                n *= 2
            link(eng.tensor_scalar(pw[:, 2], pw[:, 1], -1.0, None, ALU.mult))
            eng.engine_nop().then_inc(tables_ready, 1)
            a = (par[:, CS, :], par[:, SN, :])
            for k in range(int(math.log2(L))):
                b = (ph[:, k % 2, 0, :], ph[:, k % 2, 1, :])
                cmul(*b, *a, *a, PAIRS, (PAIRS,))
                a = b
            count(eng.memset(phr[:, :, 0:1], 1.0))
            count(eng.memset(phi[:, :, 0:1], 0.0))
            count(eng.tensor_copy(phr[:, :, 1], a[0]))
            count(eng.tensor_copy(phi[:, :, 1], a[1]))
            settle()
            n, k = 2, int(math.log2(L))
            while n < NC:
                b = (ph[:, k % 2, 0, :], ph[:, k % 2, 1, :])
                cmul(*b, *a, *a, PAIRS, (PAIRS,))
                a = b
                for lo in range(0, n, 16):
                    w = min(n, 16)
                    cmul(phr[:, :, n + lo:n + lo + w], phi[:, :, n + lo:n + lo + w], phr[:, :, lo:lo + w],
                         phi[:, :, lo:lo + w], a[0].unsqueeze(2).broadcast_to((P, PAIRS, w)),
                         a[1].unsqueeze(2).broadcast_to((P, PAIRS, w)), PAIRS * w, (PAIRS, w))
                n, k = 2 * n, k + 1
            link(eng.memset(decay[:], 0.0))

            def rotate(q, part):
                pq = slice(q * PQ, (q + 1) * PQ)
                fr_, fi_ = phr[:, pq], phi[:, pq]
                k = STEPS * q + 2

                def flat(t):
                    return t[:].rearrange("p a c -> p (a c)")

                if part == 0:
                    count(eng.tensor_copy(decay[:, :, 1:], par[:, M8, pq].unsqueeze(2).broadcast_to((P, PQ, NC - 1))))
                    bank = ps[:, SSM_BANK[k % 2], :]
                    sr = bank[:, 0:PQ * NC].rearrange("p (a c) -> p a c", c=NC)
                    si = bank[:, PQ * NC:2 * PQ * NC].rearrange("p (a c) -> p a c", c=NC)
                    dve.wait_ge(ssm_done, k + 1)
                    v4 = products4(sr, si, fr_, fi_, PQ * NC, (PQ, NC))
                    count(tt(zin_r[:], v4[0], v4[1], ALU.add))
                    tt(zin_i[:], v4[3], v4[2], ALU.subtract).then_inc(ssm_out[k % 2], 1)
                if part == 1:
                    dve.wait_ge(*ssm_read(q, 2))
                    settle()
                    count(eng.tensor_tensor_scan(flat(zr), flat(decay), flat(zin_r), 0.0, ALU.mult, ALU.add))
                    count(eng.tensor_tensor_scan(flat(zi), flat(decay), flat(zin_i), 0.0, ALU.mult, ALU.add))
                if part == 2:
                    settle()
                    v4 = products4(zr[:], zi[:], fr_, fi_, PQ * NC, (PQ, NC))
                    for b in range(2):
                        rows = slice(b * PS, (b + 1) * PS)
                        tt(xsr[rows, :, b, 1:], v4[0][rows], v4[1][rows], ALU.subtract).then_inc(xs_ready, 1)
                        tt(xsi[rows, :, b, 1:], v4[2][rows], v4[3][rows], ALU.add).then_inc(xs_ready, 1)

            def ssm_vector(n):
                for q, s in ssm_steps(n):
                    k = STEPS * q + s
                    if s == 3:
                        dve.wait_ge(ssm_done, k + 1)
                        if q:
                            dve.wait_ge(toep_landed, TOEP * q)
                        eng.tensor_copy(gk[:].rearrange("i a t j -> i (a t j)"),
                                        ps[0:2 * GI, SSM_BANK[k % 2], :]).then_inc(ssm_out[k % 2], 1)
                        dve.wait_ge(*ssm_read(q, s))
                        tt(gk[:, :, 0, :], gk[:, :, 0, :], dd[:, q * PQ:(q + 1) * PQ, :],
                           ALU.add).then_inc(gk_ready, 1)
                if n // PERIOD < AT and 2 <= n % PERIOD <= 4:
                    rotate(n // PERIOD, n % PERIOD - 2)

            dve.wait_ge(const_ready, 7)

            def biased(n):
                hd, i = ITEMS[n]
                w = (i + 1) * P
                if i == 0:
                    dve.wait_ge(bias_landed[hd % 2], 16 * (hd // 2 + 1))
                    link(eng.memset(bias[P - CHUNK:P, hd % 2, S - CHUNK:S], MASKED))
                dve.wait_ge(s_done, n + 1)
                if n >= 3:
                    dve.wait_ge(pt_done, n - 2)
                eng.tensor_tensor_reduce(sc[:, n % 3, 0:w], ps[:, n % 2, 0:w], bias[:, hd % 2, S - w:S], 1.0, -3e38,
                                         ALU.add, ALU.max, sm[:, n % 3, 0:1]).then_inc(s_biased, 1)
                dve.wait_ge(s_biased, n + 1)
                eng.tensor_scalar(sm[:, n % 3, 1:2], sm[:, n % 3, 0:1], -1.0, None, ALU.mult).then_inc(s_negmax, 1)

            def normalised(n):
                w = (ITEMS[n][1] + 1) * P
                dve.wait_ge(s_exp, n + 1)
                link(eng.reciprocal(sm[:, n % 3, 3:4], sm[:, n % 3, 2:3]))
                eng.tensor_scalar(sc[:, n % 3, 0:w], sc[:, n % 3, 0:w], sm[:, n % 3, 3:4], None,
                                  ALU.mult).then_inc(p_ready, 1)

            def pair_lower(j):
                dve.wait_ge(ao_hi, j + 1)
                tt(xlo[:, j, :], kept[:, j, :] if j < 2 else ps[:, 6, :], xhi[:, j, :].bitcast(F32),
                   ALU.subtract).then_inc(ao_out, 1)

            for n in range(TICKS):
                if n < len(ITEMS):
                    biased(n)
                if 0 <= n - 1 < len(ITEMS):
                    normalised(n - 1)
                ssm_vector(n)
                if X_USED < n <= X_USED + 3:
                    pair_lower(n - X_USED - 1)

            for q in range(AT):
                dve.wait_ge(y_hi, q + 1)
                tt(ylo[:, q, :], yT[:, q].rearrange("p t c -> p (t c)"), yhi[:, q, :].bitcast(F32),
                   ALU.subtract).then_inc(y_ready, 1)
            pair_lower(A_HEADS // 2 - 1)
            for m in range(AT):
                dve.wait_ge(glu_sig, m + 1)
                tt(gt[:, m % 2, :], yT[:, m].rearrange("p t c -> p (t c)"), sg[:, m % 2, :],
                   ALU.mult).then_inc(ob_ready, 1)
                dve.wait_ge(ob_hi, m + 1)
                tt(xlo[:, AT + m, :].rearrange("p (c t) -> p c t", t=L),
                   gt[:, m % 2, :].rearrange("p (t c) -> p c t", t=L),
                   xhi[:, AT + m, :].rearrange("p (c t) -> p c t", t=L).bitcast(F32), ALU.subtract).then_inc(mix_b, 1)

            def norm(n):
                dve.wait_ge(lnp_landed, 32 * (n + 1))

                def statistics(t):
                    if t < NT - 1:
                        dve.wait_ge(acc_done, (NT - 1) * n + t + 1)
                    else:
                        dve.wait_ge(w_used, (EOUT + KT, FFN[0] + 3 * FT, OOUT + KT, FFN[1] + 3 * FT)[n])
                    link(eng.scalar_tensor_tensor(out=h[:, t, :], in0=h[:, t, :], scalar=1.0 if n == 2 else ALPHA,
                                                  in1=psf[:, 2 * t * S:2 * (t + 1) * S], op0=ALU.mult, op1=ALU.add))
                    for c in range(2):
                        count(eng.bn_stats(stats[:, t, c, :], h[:, t, c * S:(c + 1) * S]))
                    settle()
                    link(eng.bn_aggr(mv[:, t, :], stats[:, t].rearrange("p a b -> p (a b)")))
                    eng.tensor_scalar(lns[:, t, 0:1], mv[:, t, 1:2], EPS, None, ALU.add).then_inc(var_ready, 1)

                def centre(t):
                    link(eng.scalar_tensor_tensor(out=h[:, t, :], in0=h[:, t, :], scalar=mv[:, t, 0:1],
                                                  in1=lnp[:, 0, :], op0=ALU.subtract, op1=ALU.mult))
                    dve.wait_ge(std_ready, NT * n + t + 1)
                    if t < NT - 1:
                        eng.reciprocal(lns[:, t, 2:3], lns[:, t, 1:2]).then_inc(rstd_ready, 1)
                    else:
                        link(eng.reciprocal(lns[:, t, 2:3], lns[:, t, 1:2]))
                        eng.scalar_tensor_tensor(out=h[:, t, :], in0=h[:, t, :], scalar=lns[:, t, 2:3],
                                                 in1=lnp[:, 1, :], op0=ALU.mult, op1=ALU.add).then_inc(h_last, 1)

                for t in range(NT):
                    statistics(t)
                    centre(t)
                    if n < 3 and 1 <= t <= 2:
                        lower_x(n + 1, t - 1)
                if n < 3:
                    lower_x(n + 1, 2)
                    lower_x(n + 1, 3)

            def ffn(layer):
                for m in range(FT):
                    c = layer * FT + m
                    dve.wait_ge(silu_ready, c + 1)
                    dve.wait_ge(w_used, FFN[layer] + 2 * m + 2)
                    if m >= 2:
                        dve.wait_ge(g_lo, c - 1)
                    tt(gt[:, m % 2, :], ps[:, 2 * (m % 2) + 1, :], sg[:, m % 2, :], ALU.mult).then_inc(g_ready, 1)
                    dve.wait_ge(g_hi, c + 1)
                    tt(glo[:, m, :], gt[:, m % 2, :], ghi[:, m, :].bitcast(F32), ALU.subtract).then_inc(g_lo, 1)

            dve.wait_ge(h_landed, 16 * NT)
            norm(0)
            ffn(0)
            norm(1)

            def stick_plus(hd):
                dve.wait_ge(l_ready, hd + 1)
                if hd:
                    dve.wait_ge(sp_lo, hd)
                eng.scalar_tensor_tensor(out=sp[:], in0=psf[:, 0:TRI_W], scalar=0.0, in1=lg[:], op0=ALU.max,
                                         op1=ALU.add).then_inc(sp_raw, 1)
                if hd >= 3:
                    dve.wait_ge(opv_done, hd - 2)
                eng.scalar_tensor_tensor(out=wt[:, hd % 3], in0=psf[:, 0:TRI_W], scalar=0.0, in1=lg[:],
                                         op0=ALU.min, op1=ALU.subtract).then_inc(z_read, 1)

            def stick_lower(hd):
                dve.wait_ge(sp_hi, hd + 1)
                tt(splo[:], sp[:], sphi[:].bitcast(F32), ALU.subtract).then_inc(sp_lo, 1)

            def stick_weight(hd):
                dve.wait_ge(r_done, hd + 1)
                dve.wait_ge(z_read, hd + 1)
                tt(wt[:, hd % 3], wt[:, hd % 3], psf[:, 3 * S:3 * S + TRI_W], ALU.subtract).then_inc(lw_ready, 1)

            def qk_lower(n):
                dve.wait_ge(qk_hi, n + 1)
                hi = oqk_hi[:, n // 2 % 2, n % 2, :].bitcast(F32)
                lo = oqk_lo[:, n // 2 % 2, n % 2, :]
                eng.scalar_tensor_tensor(out=lo, in0=ps[:, qk_bank(n), :], scalar=QSCALE if n % 2 == 0 else 1.0, in1=hi,
                                         op0=ALU.mult, op1=ALU.subtract).then_inc(qk_out, 1)

            for n in range(LEAD):
                qk_lower(n)
            stick_plus(0)
            stick_lower(0)
            qk_lower(LEAD)
            def mix_lower(j):
                dve.wait_ge(omix_hi, j + 1)
                tt(xlo[:, j, :], oatt[:, j, :], xhi[:, j, :].bitcast(F32), ALU.subtract).then_inc(omix, 1)

            def early_add(i):
                t, half = EARLY[i]
                c = slice(half * S, (half + 1) * S)
                if i < len(EARLY) - 1:
                    dve.wait_ge(early_done, i + 1)
                else:
                    dve.wait_ge(w_used, OOUT + EARLY_K)
                eng.scalar_tensor_tensor(out=h[:, t, c], in0=h[:, t, c], scalar=ALPHA, in1=ps[:, 6, :], op0=ALU.mult,
                                         op1=ALU.add).then_inc(early_added, 1)

            for hd in range(C_HEADS):
                stick_weight(hd)
                if hd + 1 < C_HEADS:
                    stick_plus(hd + 1)
                    if hd == C_HEADS - 3:
                        early_add(0)
                    if hd == C_HEADS - 2:
                        early_add(1)
                    stick_lower(hd + 1)
                if hd + 1 + LEAD < 2 * KT:
                    qk_lower(hd + 1 + LEAD)
                if hd == C_HEADS - 2:
                    early_add(2)
                for j in mixed_behind(hd):
                    mix_lower(j)
            for i in range(3, len(EARLY)):
                early_add(i)
            mix_lower(KT - 1)
            dve.wait_ge(early_added, len(EARLY))
            norm(2)
            ffn(1)
            norm(3)

        @block.tensor
        def _(pe):
            eng = nc.tensor

            def three(o_, w_hi_, w_lo_, x_hi_, x_lo_, start, stop):
                eng.matmul(o_, w_hi_, x_hi_, start=start, stop=False)
                eng.matmul(o_, w_hi_, x_lo_, start=False, stop=False)
                return eng.matmul(o_, w_lo_, x_hi_, start=False, stop=stop)

            def feature_major(b, o_, hi, lo, nk=KT, col=0, ready=None):
                pe.wait_ge(w_lo, b + 1)
                wh = whi[:, b % WS, :].rearrange("p (k n) -> p k n", k=nk)
                wl = wlo[:, b % WS, :].rearrange("p (k n) -> p k n", k=nk)
                c = slice(col, col + P)
                for k in range(nk):
                    if ready:
                        ready(k)
                    mm = three(o_, wh[:, k, c], wl[:, k, c], hi[:, k, :], lo[:, k, :], k == 0, k == nk - 1)
                return mm

            def token_rows(b, k, r, width, hi, lo, t, bank, n_half, start, stop):
                c = slice(t * P, (t + 1) * P)
                for half in range(n_half):
                    w = slice(r * width + half * S, r * width + half * S + S)
                    o_ = ps[:, bank + half, :]
                    eng.matmul(o_, hi[:, k, c], whi[:, b % WS, w], start=start, stop=False)
                    eng.matmul(o_, hi[:, k, c], wlo[:, b % WS, w], start=False, stop=False)
                    mm = eng.matmul(o_, lo[:, k, c], whi[:, b % WS, w], start=False, stop=stop)
                return mm

            def turn(n, t):
                for k in range(KT):
                    mm = eng.transpose(psf[:, 2 * t * S + k * P:2 * t * S + (k + 1) * P],
                                       h[:, t, k * P:(k + 1) * P], ident[:])
                mm.then_inc(turned, 1)

            def turn_normed(n, t):
                if t < NT - 1:
                    pe.wait_ge(h_ready, (NT - 1) * (n - 1) + t + 1)
                else:
                    pe.wait_ge(h_last, n)
                turn(n, t)

            def token_major(first, nk, hi, lo, norm_n, ready=None, order=(0, 1, 2, 3), before=None, k0=0):
                for k in range(k0, nk - TAIL):
                    pe.wait_ge(w_lo, first + k + 1)
                    if ready:
                        ready(k)
                    for t in order:
                        if k == 0 and before:
                            before(t)
                        mm = token_rows(first + k, k, 0, D, hi, lo, t, 2 * t, 2, k == k0, False)
                    mm.then_inc(w_used, 1)
                for t in range(NT):
                    for k in range(nk - TAIL, nk):
                        if t == 0:
                            pe.wait_ge(w_lo, first + k + 1)
                            if ready:
                                ready(k)
                        if k == k0 and before:
                            before(t)
                        mm = token_rows(first + k, k, 0, D, hi, lo, t, 2 * t, 2, k == k0, k == nk - 1)
                        if t == NT - 1 and k < nk - 1:
                            mm.then_inc(w_used, 1)
                        if t >= 2 and k == nk - TAIL + 1 and norm_n < 3:
                            turn_normed(norm_n + 1, t - 2)
                    if t < NT - 1:
                        mm.then_inc(acc_done, 1)
                mm.then_inc(w_used, 1)
                return mm

            pe.wait_ge(const_ready, 7)
            for t in range(NT):
                pe.wait_ge(x_landed[t], 16)
                turn(0, t)
            pe.wait_ge(x_ready, NT)

            def project(n, b):
                if n >= 2:
                    pe.wait_ge(proj_out, n - 1)
                mm = feature_major(b, ps[:, 4 + n % 2, :], xhi, xlo)
                mm.then_inc(w_used, 1)

            project(0, 0)
            pe.wait_ge(pl_ready, 1)
            for i in range(7):
                mm = eng.transpose(ps[:, 6, i * PAIRS:(i + 1) * PAIRS], pl[:, i, :], ident[0:PAIRS, 0:PAIRS])
            mm.then_inc(pl_turned, 1)
            project(1, 1)
            pe.wait_ge(c_landed, 64)
            for src, bank in ((cdr, 7), (cdi, 0)):
                for t in range(AT):
                    mm = eng.transpose(ps[:, bank, t * P:(t + 1) * P], src[:, t].rearrange("p a b -> p (a b)"),
                                       ident[:])
            mm.then_inc(c_turned, 1)
            project(2, 2)
            project(3, 3)
            pe.wait_ge(par_out, 1)
            for b in range(4):
                pe.wait_ge(w_lo, AT + b + 1)
                for r in range(2):
                    k = 2 * b + r
                    for t in range(NT):
                        mm = token_rows(AT + b, k, r, WA, xhi, xlo, t, t, 1, k == 0, k == KT - 1)
                mm.then_inc(w_used, 1)

            def qk_part(n, part):
                b = 2 * AT + n
                if part == 0:
                    pe.wait_ge(proj_out, 3 if n == 0 else AT + n if n > 1 else 1)
                    pe.wait_ge(w_lo, b + 1)
                for k in (2 * part, 2 * part + 1):
                    c = slice(k * P, (k + 1) * P)
                    mm = three(ps[:, 6 if n == 1 else 4, :], whi[:, b % WS, c], wlo[:, b % WS, c], xhi[:, k, :],
                               xlo[:, k, :], k == 0, k == KT - 1)
                if part == 3:
                    mm.then_inc(w_used, 1)

            def ssm_products(steps):
                for q, s in steps:
                    step = STEPS * q + s
                    p7 = ps[:, SSM_BANK[step % 2], :]
                    if step >= 2:
                        pe.wait_ge(ssm_out[step % 2], step // 2)
                    if s in (0, 1):
                        pe.wait_ge(wn_ready, 2 * q + s + 1)
                        src = (wnr, wni)[s]
                        for a in range(PQ):
                            mm = eng.transpose(p7[:, a * P:(a + 1) * P], src[:, a].rearrange("p l i -> p (l i)"),
                                               ident[:])
                    if s == 3:
                        pe.wait_ge(cx_ready, 4 * q + 4)
                        if q == 0:
                            pe.wait_ge(bd_ready, 4)
                        for a in range(PQ):
                            o_ = p7[0:2 * GI, a * P:(a + 1) * P]
                            eng.matmul(o_, bdr[:, q * PQ + a].rearrange("p b i -> p (b i)"),
                                       cxr[:, a, 0:L, :].rearrange("p l j -> p (l j)"), start=True, stop=False)
                            mm = eng.matmul(o_, bdi[:, q * PQ + a].rearrange("p b i -> p (b i)"),
                                            cxi[:, a, 0:L, :].rearrange("p l j -> p (l j)"),
                                            start=False, stop=True)
                    if s == 2:
                        pe.wait_ge(u_landed[q], 16 * L)
                        pe.wait_ge(*ssm_read(q, 0))
                        pe.wait_ge(*ssm_read(q, 1))
                        for g in range(GQ):
                            a, b = g // 2, g % 2
                            rows = slice(b * PS, (b + 1) * PS)
                            for part, w in enumerate((winr, wini)):
                                o_ = p7[rows, part * PQ * NC + a * NC:part * PQ * NC + (a + 1) * NC]
                                mm = eng.matmul(o_, w[:, a, rows], u8[:, q, g, :], start=True, stop=True)
                    if s == 4:
                        pe.wait_ge(xs_ready, 4 * q + 4)
                        pe.wait_ge(toep_landed, TOEP * (q + 1))
                        for a in range(PQ):
                            o_ = p7[:, 2 * a * NC:2 * (a + 1) * NC]
                            eng.matmul(o_, cxr[:, a, 1:, :].rearrange("p l j -> p (l j)"), xsr[:, a, :, 0:NC],
                                       start=True, stop=False)
                            for g in (2 * a, 2 * a + 1):
                                eng.matmul(p7[:, g * NC:(g + 1) * NC], toep[:, g, :], u8[:, q, g, :], start=False,
                                           stop=False)
                            mm = eng.matmul(o_, cxi[:, a, 1:, :].rearrange("p l j -> p (l j)"),
                                            xsi[:, a, :, 0:NC], start=False, stop=True)
                    mm.then_inc(ssm_done, 1)

            for n in range(2):
                for part in range(4):
                    qk_part(n, part)

            pe.wait_ge(proj_out, AT + 1)
            pe.wait_ge(v_out, NT)

            def scores(n):
                hd, i = ITEMS[n]
                rows = slice((hd % 2) * HD, (hd % 2 + 1) * HD)
                if i == 0 and hd % 2 == 0:
                    pe.wait_ge(proj_out, AT + hd + 2)
                if n >= 2:
                    pe.wait_ge(s_biased, n - 1)
                eng.matmul(ps[:, n % 2, 0:(i + 1) * P], qT[rows, hd // 2, i * P:(i + 1) * P],
                           kT[rows, hd // 2, 0:(i + 1) * P], start=True, stop=True).then_inc(s_done, 1)

            def turn_probs(n):
                hd, i = ITEMS[n]
                pe.wait_ge(p_ready, n + 1)
                if n >= 2:
                    pe.wait_ge(pt_out, n - 1)
                for j in range(i + 1):
                    mm = eng.transpose(ps[:, 2 + n % 2, j * P:(j + 1) * P], sc[:, n % 3, j * P:(j + 1) * P], ident[:])
                mm.then_inc(pt_done, 1)

            def head_out(hd):
                rows = slice((hd % 2) * HD, (hd % 2 + 1) * HD)
                pe.wait_ge(pt_out, NT * (hd + 1))
                if hd in (2, 4):
                    pe.wait_ge(ao_kept, hd // 2)
                if hd == 6:
                    pe.wait_ge(ao_out, hd // 2)
                for j in range(NT):
                    mm = eng.matmul(ps[rows, 6, j * P:S], v[:, j, hd * HD:(hd + 1) * HD], pt[:, j, j * P:S],
                                    start=(j == 0), stop=(j == NT - 1))
                mm.then_inc(pv_done, 1)

            for n in range(TICKS):
                if n < len(ITEMS):
                    scores(n)
                if n >= 6 and n % NT == 2:
                    head_out((n - 6) // NT)
                if 0 <= n - 2 < len(ITEMS):
                    turn_probs(n - 2)
                ssm_products(ssm_steps(n))
                if n // 4 + 2 < 2 * AT:
                    qk_part(n // 4 + 2, n % 4)

            def y_is_ready(k):
                pe.wait_ge(y_ready, k + 1)

            for m in range(AT):
                b = GLU + m // 2
                if m >= 2:
                    pe.wait_ge(glu_sig, m - 1)
                mm = feature_major(b, ps[:, 4 + m % 2, :], yhi, ylo, nk=AT, col=(m % 2) * P,
                                   ready=None if m else y_is_ready)
                mm.then_inc(w_used if m % 2 else glu_done, 1)
            pe.wait_ge(ao_out, A_HEADS // 2)

            def mix_ready(k):
                if k >= AT:
                    pe.wait_ge(mix_b, k - AT + 1)

            def glu_banks_read(t):
                if t == 2:
                    pe.wait_ge(glu_sig, AT)

            token_major(EOUT, KT, xhi, xlo, 0, mix_ready, (0, 1, 3, 2), glu_banks_read)

            def overlapped(n, parts):
                pe.wait_ge(x_ready, NT * n + 2)
                for i, part in enumerate(parts):
                    part(0)
                    if i in (1, 2):
                        turn_normed(n, i + 1)
                pe.wait_ge(x_ready, NT * (n + 1))
                for part in parts:
                    part(1)

            def ffn(layer):
                f = FFN[layer]

                def half_unit(m, part):
                    b = f + 2 * m + part
                    wh = whi[:, b % WS, :].rearrange("p (k n) -> p k n", k=KT)
                    wl = wlo[:, b % WS, :].rearrange("p (k n) -> p k n", k=KT)

                    def run(half):
                        c = slice(half * 2 * P, (half + 1) * 2 * P)
                        if half == 0:
                            pe.wait_ge(w_lo, b + 1)
                        for k in range(KT):
                            mm = three(ps[:, 2 * m + part, c], wh[:, k], wl[:, k], xhi[:, k, c], xlo[:, k, c],
                                       k == 0, k == KT - 1)
                        if half:
                            mm.then_inc(w_used, 1)
                    return run

                overlapped(2 * layer + 1, [half_unit(m, part) for m in range(2) for part in range(2)])
                for m in range(2, FT):
                    c = layer * FT + m
                    for part in range(2):
                        b = f + 2 * m + part
                        if part == 0:
                            pe.wait_ge(g_ready, c - 1)
                        mm = feature_major(b, ps[:, 2 * (m % 2) + part, :], xhi, xlo)
                        mm.then_inc(w_used, 1)

                def ready(k):
                    pe.wait_ge(g_lo, layer * FT + k + 1)

                def before(t):
                    if t == 0:
                        pe.wait_ge(g_ready, (layer + 1) * FT)

                token_major(f + 2 * FT, FT, ghi, glo, 2 * layer + 1, ready, order=(2, 3, 0, 1), before=before)

            ffn(0)

            def v_part(k):
                def run(half):
                    if half == 0:
                        pe.wait_ge(w_lo, OV + k + 1)
                    for t in (2 * half, 2 * half + 1):
                        mm = token_rows(OV + k, k, 0, D, xhi, xlo, t, 2 * t, 2, k == 0, k == KT - 1)
                    if half:
                        mm.then_inc(w_used, 1)
                return run

            overlapped(2, [v_part(k) for k in range(KT // 2)])
            for k in range(KT // 2, KT):
                for half in range(2):
                    v_part(k)(half)

            def oqk(n):
                if n > 1:
                    pe.wait_ge(qk_out, n if n > 2 else 1)
                else:
                    pe.wait_ge(ov_out, 1)
                b = OQK + n
                mm = feature_major(b, ps[:, qk_bank(n), :], xhi, xlo)
                mm.then_inc(w_used, 1)

            def stick_scores(hd):
                rows = slice((hd % 2) * HD, (hd % 2 + 1) * HD)
                j_ = hd // 2
                pe.wait_ge(qk_out, 2 * j_ + 2)
                if hd:
                    pe.wait_ge(z_read, hd)
                for j in range(NT):
                    keys, queries = slice(j * P, (j + 1) * P), slice(j * P, S)
                    mm = three(psf[:, TRI[j]:TRI[j] + (NT - j) * P],
                               oqk_hi[rows, j_ % 2, 1, keys], oqk_lo[rows, j_ % 2, 1, keys],
                               oqk_hi[rows, j_ % 2, 0, queries], oqk_lo[rows, j_ % 2, 0, queries], True, True)
                mm.then_inc(z_done, 1)

            def stick_sums(hd):
                pe.wait_ge(sp_lo, hd + 1)
                if hd:
                    pe.wait_ge(lw_ready, hd)
                for j in range(NT):
                    for j2 in range(j, NT):
                        o_ = psf[:, 3 * S + TRI[j] + (j2 - j) * P:3 * S + TRI[j] + (NT - j) * P]
                        cols = slice(TRI[j2], TRI[j2] + (NT - j2) * P)
                        w = tri if j2 == j else ones
                        eng.matmul(o_, w[:], sphi[:, cols], start=(j2 == j), stop=False)
                        mm = eng.matmul(o_, w[:], splo[:, cols], start=False, stop=(j2 == NT - 1))
                mm.then_inc(r_done, 1)

            def stick_out(hd):
                rows = slice((hd % 2) * HD, (hd % 2 + 1) * HD)
                pe.wait_ge(w_ready, NT * (hd + 1))
                if hd >= 2 and hd % 2 == 0:
                    pe.wait_ge(o_out, hd // 2)
                for j in range(NT):
                    mm = eng.matmul(ps[rows, 7, j * P:S], ov[:, j, hd * HD:(hd + 1) * HD],
                                    wt[:, hd % 3, TRI[j]:TRI[j] + (NT - j) * P], start=(j == 0), stop=(j == NT - 1))
                mm.then_inc(opv_done, 1)

            def early_part(i):
                t, half = EARLY[i]
                if i:
                    pe.wait_ge(early_added, i)
                else:
                    pe.wait_ge(omix, EARLY_K)
                    pe.wait_ge(qk_out, 2 * KT)
                for k in range(EARLY_K):
                    b = OOUT + k
                    if i == 0:
                        pe.wait_ge(w_lo, b + 1)
                    c, w = slice(t * P, (t + 1) * P), slice(half * S, (half + 1) * S)
                    eng.matmul(ps[:, 6, :], xhi[:, k, c], whi[:, b % WS, w], start=k == 0, stop=False)
                    eng.matmul(ps[:, 6, :], xhi[:, k, c], wlo[:, b % WS, w], start=False, stop=False)
                    mm = eng.matmul(ps[:, 6, :], xlo[:, k, c], whi[:, b % WS, w], start=False,
                                    stop=k == EARLY_K - 1)
                    if i == len(EARLY) - 1 and k < EARLY_K - 1:
                        mm.then_inc(w_used, 1)
                mm.then_inc(w_used if i == len(EARLY) - 1 else early_done, 1)

            for n in range(LEAD):
                oqk(n)
            pe.wait_ge(const_ready, 8)
            pe.wait_ge(ov_out, NT)
            stick_scores(0)
            for hd in range(C_HEADS):
                if hd + LEAD < 2 * KT:
                    oqk(hd + LEAD)
                if hd + 1 < C_HEADS:
                    stick_scores(hd + 1)
                stick_sums(hd)
                if hd == C_HEADS - 3:
                    early_part(0)
                if hd == C_HEADS - 2:
                    early_part(1)
                if hd == C_HEADS - 1:
                    early_part(3)
                if hd:
                    stick_out(hd - 1)
                if hd == C_HEADS - 2:
                    early_part(2)
            for i in range(4, len(EARLY)):
                early_part(i)
            stick_out(C_HEADS - 1)

            def omix_ready(k):
                pe.wait_ge(omix, k + 1)

            def banks_read(t):
                if t == 0:
                    pe.wait_ge(lw_ready, C_HEADS)
                if t == NT - 1:
                    pe.wait_ge(early_added, len(EARLY))

            token_major(OOUT, KT, xhi, xlo, 2, omix_ready, before=banks_read, k0=EARLY_K)
            ffn(1)


_INS = ["x", "even_w_in", "even_rel_bias", "ssm_lambda_re", "ssm_lambda_im", "ssm_b_re", "ssm_b_im", "ssm_c_re",
        "ssm_c_im", "ssm_d", "ssm_log_dt", "ssm_glu_w", "ssm_glu_b", "even_w_out", "odd_w_in", "odd_w_out",
        "ffn_w1", "ffn_w3", "ffn_w2", "ln_mix_g", "ln_mix_b", "ln_ffn_g", "ln_ffn_b"]


def kernel(**inputs):
    import concourse.bacc as _bacc
    from concourse.bass_utils import run_bass_kernel_spmd as _run

    nc = _bacc.Bacc("TRN2", target_bir_lowering=False, num_devices=1)
    arrays, args = {}, []
    for name in _INS:
        a = np.ascontiguousarray(inputs[name])
        arrays[f"in_{name}"] = a
        args.append(nc.dram_tensor(f"in_{name}", a.shape, mybir.dt.from_np(a.dtype), kind="ExternalInput").ap())
    out = nc.dram_tensor("out", (1, S, D), F32, kind="ExternalOutput").ap()
    build(nc, *args, out)
    r = _run(nc, [arrays], core_ids=[0])
    return r.results[0]["out"]
```
